# Optimizing a Trainium2 kernel written in Bass

```python
import math
import jax, jax.numpy as jnp
from jax import lax
import numpy as np

D_MODEL = 1024
BATCH = 1
SEQ = 512
DEPTH = 1

N_MIXERS = 2
RMS_EPS = 1e-6

MLA_HEADS = 8
QK_NOPE_DIM = 128
QK_ROPE_DIM = 64
V_HEAD_DIM = 128
Q_LORA_RANK = 384
KV_LORA_RANK = 256
ROPE_THETA = 10000.0
Q_BLOCK = 128
MLA_WIDTH = MLA_HEADS * V_HEAD_DIM
MLA_QK_DIM = QK_NOPE_DIM + QK_ROPE_DIM
MLA_IN_WIDTH = Q_LORA_RANK + KV_LORA_RANK + QK_ROPE_DIM + MLA_WIDTH

HYENA_WIDTH = D_MODEL
HYENA_ORDER = 2
SHORT_CONV = 3
POS_EMB_DIM = 33
POS_BANDS = (POS_EMB_DIM - 1) // 2
FILTER_HIDDEN = 64
N_DIRS = 2
DECAY_TARGET = 1e-2
FAST_DECAY_PCT = 0.3
SLOW_DECAY_PCT = 1.5
MIN_DECAY = math.log(DECAY_TARGET) / SLOW_DECAY_PCT
MAX_DECAY = math.log(DECAY_TARGET) / FAST_DECAY_PCT
FILTER_OUT_GAIN = 0.05
HYENA_IN_WIDTH = (HYENA_ORDER + 1) * HYENA_WIDTH + HYENA_WIDTH


def rms_norm(x, g):
    xf = x.astype(jnp.float32)
    y = xf * lax.rsqrt(jnp.mean(xf * xf, axis=-1, keepdims=True) + RMS_EPS)
    return (y * g.astype(jnp.float32)).astype(x.dtype)

def rope_tables(L):
    inv = 1.0 / (ROPE_THETA ** (jnp.arange(0, QK_ROPE_DIM, 2, dtype=jnp.float32) / QK_ROPE_DIM))
    ang = jnp.arange(L, dtype=jnp.float32)[:, None] * inv[None, :]
    return jnp.cos(ang), jnp.sin(ang)

def apply_rope(x, cos, sin):
    xf = x.astype(jnp.float32)
    x1, x2 = xf[..., :QK_ROPE_DIM // 2], xf[..., QK_ROPE_DIM // 2:]
    out = jnp.concatenate([x1 * cos - x2 * sin, x1 * sin + x2 * cos], axis=-1)
    return out.astype(x.dtype)

def mla_mixer(h, w_in, q_norm, w_uq, kv_norm, w_ukv, w_out):
    B, L, _ = h.shape
    proj = h @ w_in
    s1 = Q_LORA_RANK
    s2 = s1 + KV_LORA_RANK
    s3 = s2 + QK_ROPE_DIM
    c_q, c_kv, k_pe, gate = proj[..., :s1], proj[..., s1:s2], proj[..., s2:s3], proj[..., s3:]
    q = (rms_norm(c_q, q_norm) @ w_uq).reshape(B, L, MLA_HEADS, MLA_QK_DIM)
    q_nope, q_pe = q[..., :QK_NOPE_DIM], q[..., QK_NOPE_DIM:]
    kv = (rms_norm(c_kv, kv_norm) @ w_ukv).reshape(B, L, MLA_HEADS, QK_NOPE_DIM + V_HEAD_DIM)
    k_nope, v = kv[..., :QK_NOPE_DIM], kv[..., QK_NOPE_DIM:]
    cos, sin = rope_tables(L)
    q_pe = apply_rope(q_pe, cos[:, None, :], sin[:, None, :])
    k_pe = apply_rope(k_pe, cos, sin)
    scale = MLA_QK_DIM ** -0.5
    n_blk = L // Q_BLOCK

    def to_blocks(t):
        return jnp.moveaxis(t.reshape(B, n_blk, Q_BLOCK, *t.shape[2:]), 1, 0)

    def attend(blk):
        qn, qp = blk
        s = (jnp.einsum('bqhd,bkhd->bhqk', qn, k_nope)
             + jnp.einsum('bqhr,bkr->bhqk', qp, k_pe))
        p = jax.nn.softmax(s.astype(jnp.float32) * scale, axis=-1).astype(v.dtype)
        return jnp.einsum('bhqk,bkhd->bqhd', p, v)

    o = lax.map(attend, (to_blocks(q_nope), to_blocks(q_pe)))
    o = jnp.moveaxis(o, 0, 1).reshape(B, L, MLA_WIDTH)
    return (o * jax.nn.silu(gate)) @ w_out

def hyena_filters(L, w1, b1, w2, b2, w3, b3, w4, freq):
    f32 = jnp.float32
    t = jnp.linspace(0.0, 1.0, L, dtype=f32)[:, None]
    w = 2.0 * math.pi * jnp.arange(L, dtype=f32) / L
    bands = jnp.linspace(1e-4, POS_BANDS - 1, POS_BANDS, dtype=f32)
    fw = w[:, None] * bands[None, :]
    z = jnp.concatenate([t, jnp.cos(fw), -jnp.sin(fw)], axis=-1)
    fr = freq.astype(f32)
    a = jnp.sin(fr * (z @ w1.astype(f32) + b1.astype(f32)))
    a = jnp.sin(fr * (a @ w2.astype(f32) + b2.astype(f32)))
    a = jnp.sin(fr * (a @ w3.astype(f32) + b3.astype(f32)))
    hf = (a @ w4.astype(f32)).reshape(L, HYENA_ORDER, N_DIRS, HYENA_WIDTH)
    deltas = jnp.abs(jnp.linspace(MIN_DECAY, MAX_DECAY, HYENA_WIDTH, dtype=f32))
    decay = jnp.exp(-t * deltas[None, :])
    return hf * decay[:, None, None, :]

def two_sided_kernel(h_fwd, h_bwd):
    return jnp.concatenate([h_fwd, jnp.zeros_like(h_fwd[:1]), h_bwd[:0:-1]], axis=0)

def bidir_long_conv(u, k, bias):
    L = u.shape[1]
    uf = u.astype(jnp.float32)
    spec = jnp.fft.rfft(uf, n=2 * L, axis=1) * jnp.fft.rfft(k, n=2 * L, axis=0)[None]
    y = jnp.fft.irfft(spec, n=2 * L, axis=1)[:, :L]
    return (y + uf * bias.astype(jnp.float32)).astype(u.dtype)

def hyena_mixer(h, w_in, conv_w, conv_b, filt_w1, filt_b1, filt_w2, filt_b2,
                filt_w3, filt_b3, filt_w4, filt_freq, filt_bias, w_out):
    B, L, _ = h.shape
    proj = h @ w_in
    u, gate = proj[..., :(HYENA_ORDER + 1) * HYENA_WIDTH], proj[..., (HYENA_ORDER + 1) * HYENA_WIDTH:]
    pad = SHORT_CONV // 2
    up = jnp.pad(u, ((0, 0), (pad, pad), (0, 0)))
    u = conv_b + sum(up[:, j:j + L] * conv_w[j] for j in range(SHORT_CONV))
    x1 = u[..., :HYENA_WIDTH]
    x2 = u[..., HYENA_WIDTH:2 * HYENA_WIDTH]
    v = u[..., 2 * HYENA_WIDTH:]
    filt = hyena_filters(L, filt_w1, filt_b1, filt_w2, filt_b2, filt_w3, filt_b3, filt_w4, filt_freq)
    z = v
    for n, g_n in enumerate((x1, x2)):
        k = two_sided_kernel(filt[:, n, 0], filt[:, n, 1])
        z = g_n * bidir_long_conv(z, k, filt_bias[n])
    return (z * jax.nn.silu(gate)) @ w_out

def first_inputs(seed: int = 0) -> dict:
    key = jax.random.key(seed)
    ks = iter(jax.random.split(key, 32))
    f32 = jnp.float32

    def nrm(shape, scale):
        return jax.random.normal(next(ks), shape, f32) * scale

    def gain(n):
        return jnp.ones((n,), f32) + nrm((n,), 0.01)

    d = D_MODEL
    return {
        "x": nrm((BATCH, SEQ, d), 1.0),
        "l0_norm": gain(d),
        "l0_w_in": nrm((d, MLA_IN_WIDTH), d ** -0.5),
        "l0_q_norm": gain(Q_LORA_RANK),
        "l0_w_uq": nrm((Q_LORA_RANK, MLA_HEADS * MLA_QK_DIM), Q_LORA_RANK ** -0.5),
        "l0_kv_norm": gain(KV_LORA_RANK),
        "l0_w_ukv": nrm((KV_LORA_RANK, MLA_HEADS * (QK_NOPE_DIM + V_HEAD_DIM)), KV_LORA_RANK ** -0.5),
        "l0_w_out": nrm((MLA_WIDTH, d), MLA_WIDTH ** -0.5),
        "l1_norm": gain(d),
        "l1_w_in": nrm((d, HYENA_IN_WIDTH), d ** -0.5),
        "l1_conv_w": nrm((SHORT_CONV, (HYENA_ORDER + 1) * HYENA_WIDTH), SHORT_CONV ** -0.5),
        "l1_conv_b": nrm(((HYENA_ORDER + 1) * HYENA_WIDTH,), 0.02),
        "l1_filt_w1": nrm((POS_EMB_DIM, FILTER_HIDDEN), POS_EMB_DIM ** -0.5),
        "l1_filt_b1": nrm((FILTER_HIDDEN,), 0.1),
        "l1_filt_w2": nrm((FILTER_HIDDEN, FILTER_HIDDEN), FILTER_HIDDEN ** -0.5),
        "l1_filt_b2": nrm((FILTER_HIDDEN,), 0.1),
        "l1_filt_w3": nrm((FILTER_HIDDEN, FILTER_HIDDEN), FILTER_HIDDEN ** -0.5),
        "l1_filt_b3": nrm((FILTER_HIDDEN,), 0.1),
        "l1_filt_w4": nrm((FILTER_HIDDEN, HYENA_ORDER * N_DIRS * HYENA_WIDTH), FILTER_OUT_GAIN * FILTER_HIDDEN ** -0.5),
        "l1_filt_freq": jnp.ones((FILTER_HIDDEN,), f32) + nrm((FILTER_HIDDEN,), 0.1),
        "l1_filt_bias": nrm((HYENA_ORDER, HYENA_WIDTH), 0.2),
        "l1_w_out": nrm((HYENA_WIDTH, d), HYENA_WIDTH ** -0.5),
        "final_norm": gain(d),
    }

def first_block(x, l0_norm, l0_w_in, l0_q_norm, l0_w_uq, l0_kv_norm, l0_w_ukv, l0_w_out,
              l1_norm, l1_w_in, l1_conv_w, l1_conv_b, l1_filt_w1, l1_filt_b1, l1_filt_w2,
              l1_filt_b2, l1_filt_w3, l1_filt_b3, l1_filt_w4, l1_filt_freq, l1_filt_bias,
              l1_w_out, final_norm):
    mixers = (mla_mixer, hyena_mixer)
    layers = (
        (l0_norm, (l0_w_in, l0_q_norm, l0_w_uq, l0_kv_norm, l0_w_ukv, l0_w_out)),
        (l1_norm, (l1_w_in, l1_conv_w, l1_conv_b, l1_filt_w1, l1_filt_b1, l1_filt_w2, l1_filt_b2,
                   l1_filt_w3, l1_filt_b3, l1_filt_w4, l1_filt_freq, l1_filt_bias, l1_w_out)),
    )
    h = x
    for i in range(DEPTH):
        g, params = layers[i]
        h = h + mixers[i % N_MIXERS](rms_norm(h, g), *params)
    return rms_norm(h, final_norm)


GLA_HEADS = 4
GLA_DK = D_MODEL // 2
GLA_DV = D_MODEL
GLA_GATE_RANK = 16
GLA_TAU = 16.0
GLA_CHUNK = 64
DSA_HEADS = 8
DSA_HEAD_DIM = 128
DSA_LATENT = 256
IDX_HEADS = 8
IDX_DIM = 64
DSA_TOPK = 256
PEER_HEADS = 8
PEER_NKEYS = 128
PEER_NEXPERTS = PEER_NKEYS * PEER_NKEYS
PEER_DKEY = 256
PEER_TOPK = 16
PEER_TOKEN_BLOCK = 128
NORM_EPS = 1e-6

IN_SIZES = (GLA_DK, GLA_DK, GLA_DV, GLA_DV, GLA_GATE_RANK,
            DSA_HEADS * DSA_HEAD_DIM, DSA_LATENT, IDX_HEADS * IDX_DIM, IDX_DIM, IDX_HEADS,
            D_MODEL, D_MODEL)
IN_TOTAL = sum(IN_SIZES)


def _rmsnorm(x, g):
    x32 = x.astype(jnp.float32)
    y = x32 * lax.rsqrt(jnp.mean(x32 * x32, axis=-1, keepdims=True) + NORM_EPS)
    return (y * g.astype(jnp.float32)).astype(x.dtype)

def _alibi_slopes(n_heads):
    return jnp.exp2(-8.0 * jnp.arange(1, n_heads + 1, dtype=jnp.float32) / n_heads)

def _gla_chunked(q, k, v, log_alpha):
    B, H, S, dk = q.shape
    dv = v.shape[-1]
    C = GLA_CHUNK
    n = S // C
    q, k, v, la = [t.astype(jnp.float32).reshape(B, H, n, C, t.shape[-1]) for t in (q, k, v, log_alpha)]
    b = jnp.cumsum(la, axis=3)
    b_last = b[:, :, :, -1:, :]
    q_dec = q * jnp.exp(b)
    k_inv = k * jnp.exp(-b)
    k_end = k * jnp.exp(b_last - b)
    causal = jnp.tril(jnp.ones((C, C), dtype=bool))
    attn = jnp.where(causal, jnp.einsum('bhnid,bhnjd->bhnij', q_dec, k_inv), 0.0)
    o_intra = jnp.einsum('bhnij,bhnjv->bhniv', attn, v)

    def step(state, inp):
        q_c, k_c, v_c, decay_c = inp
        o_c = jnp.einsum('bhid,bhdv->bhiv', q_c, state)
        state = decay_c[..., None] * state + jnp.einsum('bhjd,bhjv->bhdv', k_c, v_c)
        return state, o_c

    xs = (jnp.moveaxis(q_dec, 2, 0), jnp.moveaxis(k_end, 2, 0), jnp.moveaxis(v, 2, 0),
          jnp.moveaxis(jnp.exp(b_last[:, :, :, 0, :]), 2, 0))
    state0 = jnp.zeros((B, H, dk, dv), jnp.float32)
    _, o_inter = lax.scan(step, state0, xs)
    o = o_intra + jnp.moveaxis(o_inter, 0, 2)
    return o.reshape(B, H, S, dv)

def _gla_branch(q, k, v, r, g_low, w_gate_up, b_gate, norm_g):
    B, S, _ = q.shape
    dkh = GLA_DK // GLA_HEADS
    dvh = GLA_DV // GLA_HEADS
    gate_logit = (g_low @ w_gate_up + b_gate).astype(jnp.float32)
    log_alpha = jax.nn.log_sigmoid(gate_logit) / GLA_TAU

    def heads(t, d):
        return t.reshape(B, S, GLA_HEADS, d).transpose(0, 2, 1, 3)

    o = _gla_chunked(heads(q, dkh) * (dkh ** -0.5), heads(k, dkh), heads(v, dvh), heads(log_alpha, dkh))
    o = o.transpose(0, 2, 1, 3)
    o = _rmsnorm(o, norm_g.reshape(GLA_HEADS, dvh)).reshape(B, S, GLA_DV)
    return o.astype(r.dtype) * jax.nn.silu(r)

def _dsa_branch(q, kv_raw, iq, ik, iw, kv_norm_g, w_uk, w_uv):
    B, S, _ = q.shape
    n_blocks = S // Q_BLOCK
    k_sel = min(DSA_TOPK, S // 4)
    c_kv = _rmsnorm(kv_raw, kv_norm_g)
    slopes = _alibi_slopes(DSA_HEADS)
    key_pos = jnp.arange(S, dtype=jnp.int32)

    def to_blocks(t):
        return t.reshape((B, n_blocks, Q_BLOCK) + t.shape[2:]).swapaxes(0, 1)

    q_b = to_blocks(q.reshape(B, S, DSA_HEADS, DSA_HEAD_DIM))
    iq_b = to_blocks(iq.reshape(B, S, IDX_HEADS, IDX_DIM))
    iw_b = to_blocks(iw)

    def block(inp):
        qb, iqb, iwb, blk = inp
        t = blk * Q_BLOCK + jnp.arange(Q_BLOCK, dtype=jnp.int32)
        rel = jax.nn.relu(jnp.einsum('bqhd,bsd->bqhs', iqb, ik).astype(jnp.float32) * (IDX_DIM ** -0.5))
        score = jnp.einsum('bqh,bqhs->bqs', iwb.astype(jnp.float32) * (IDX_HEADS ** -0.5), rel)
        score = jnp.where(key_pos[None, None, :] <= t[None, :, None], score, -jnp.inf)
        _, idx = lax.top_k(score, k_sel)
        kv_sel = jax.vmap(lambda cb, ib: cb[ib])(c_kv, idx)
        q_lat = jnp.einsum('bqhd,hdc->bqhc', qb, w_uk)
        logits = jnp.einsum('bqhc,bqkc->bqhk', q_lat, kv_sel).astype(jnp.float32) * (DSA_HEAD_DIM ** -0.5)
        dist = t[None, :, None] - idx
        logits = logits - slopes[None, None, :, None] * dist[:, :, None, :].astype(jnp.float32)
        logits = jnp.where((dist >= 0)[:, :, None, :], logits, -jnp.inf)
        p = jax.nn.softmax(logits, axis=-1).astype(kv_sel.dtype)
        o_lat = jnp.einsum('bqhk,bqkc->bqhc', p, kv_sel)
        o = jnp.einsum('bqhc,hcd->bqhd', o_lat, w_uv)
        return o.reshape(B, Q_BLOCK, DSA_HEADS * DSA_HEAD_DIM)

    out = lax.map(block, (q_b, iq_b, iw_b, jnp.arange(n_blocks, dtype=jnp.int32)))
    return out.swapaxes(0, 1).reshape(B, S, DSA_HEADS * DSA_HEAD_DIM)

def _peer(h, w_q, sub_keys_1, sub_keys_2, expert_u, expert_v):
    B, S, D = h.shape
    half = PEER_DKEY // 2
    q = (h @ w_q).reshape(B, S, PEER_HEADS, PEER_DKEY)
    s1 = jnp.einsum('bshd,nd->bshn', q[..., :half], sub_keys_1).astype(jnp.float32)
    s2 = jnp.einsum('bshd,nd->bshn', q[..., half:], sub_keys_2).astype(jnp.float32)
    v1, i1 = lax.top_k(s1, PEER_TOPK)
    v2, i2 = lax.top_k(s2, PEER_TOPK)
    cand = (v1[..., :, None] + v2[..., None, :]).reshape(B, S, PEER_HEADS, PEER_TOPK * PEER_TOPK)
    best, ci = lax.top_k(cand, PEER_TOPK)
    ia = jnp.take_along_axis(i1, ci // PEER_TOPK, axis=-1)
    ib = jnp.take_along_axis(i2, ci % PEER_TOPK, axis=-1)
    expert_idx = ia * PEER_NKEYS + ib
    gates = jax.nn.softmax(best, axis=-1)
    n_blocks = (B * S) // PEER_TOKEN_BLOCK
    h_b = h.reshape(n_blocks, PEER_TOKEN_BLOCK, D)
    i_b = expert_idx.reshape(n_blocks, PEER_TOKEN_BLOCK, PEER_HEADS, PEER_TOPK)
    g_b = gates.reshape(n_blocks, PEER_TOKEN_BLOCK, PEER_HEADS, PEER_TOPK)

    def block(inp):
        hx, ix, gx = inp
        u = expert_u[ix]
        v = expert_v[ix]
        a = jax.nn.gelu(jnp.einsum('td,thkd->thk', hx, u).astype(jnp.float32), approximate=False) * gx
        return jnp.einsum('thk,thkd->td', a.astype(hx.dtype), v)

    return lax.map(block, (h_b, i_b, g_b)).reshape(B, S, D)

def second_inputs(seed: int = 0) -> dict:
    key = jax.random.key(seed)
    ks = jax.random.split(key, 24)
    D = D_MODEL

    def nrm(k, shape, scale):
        return jax.random.normal(k, shape, jnp.float32) * scale

    def gain(k, shape):
        return 1.0 + 0.1 * jax.random.normal(k, shape, jnp.float32)

    return {
        "x": nrm(ks[0], (BATCH, SEQ, D), 1.0),
        "c": nrm(ks[1], (BATCH, D), 1.0),
        "w_ada": nrm(ks[2], (DEPTH, D, 6 * D), 0.5 * D ** -0.5),
        "b_ada": nrm(ks[3], (DEPTH, 6 * D), 0.02),
        "norm1_g": gain(ks[4], (DEPTH, D)),
        "w_in": nrm(ks[5], (DEPTH, D, IN_TOTAL), D ** -0.5),
        "gla_w_gate_up": nrm(ks[6], (DEPTH, GLA_GATE_RANK, GLA_DK), GLA_GATE_RANK ** -0.5),
        "gla_b_gate": nrm(ks[7], (DEPTH, GLA_DK), 0.1),
        "gla_norm_g": gain(ks[8], (DEPTH, GLA_DV)),
        "dsa_kv_norm_g": gain(ks[9], (DEPTH, DSA_LATENT)),
        "dsa_w_uk": nrm(ks[10], (DEPTH, DSA_HEADS, DSA_HEAD_DIM, DSA_LATENT), DSA_HEAD_DIM ** -0.5),
        "dsa_w_uv": nrm(ks[11], (DEPTH, DSA_HEADS, DSA_LATENT, DSA_HEAD_DIM), DSA_LATENT ** -0.5),
        "w_branch_a": nrm(ks[12], (DEPTH, GLA_DV, D), GLA_DV ** -0.5),
        "w_branch_b": nrm(ks[13], (DEPTH, DSA_HEADS * DSA_HEAD_DIM, D), (DSA_HEADS * DSA_HEAD_DIM) ** -0.5),
        "w_out": nrm(ks[14], (DEPTH, D, D), D ** -0.5),
        "norm2_g": gain(ks[15], (DEPTH, D)),
        "peer_w_q": nrm(ks[16], (DEPTH, D, PEER_HEADS * PEER_DKEY), D ** -0.5),
        "peer_sub_keys_1": nrm(ks[17], (DEPTH, PEER_NKEYS, PEER_DKEY // 2), (PEER_DKEY // 2) ** -0.5),
        "peer_sub_keys_2": nrm(ks[18], (DEPTH, PEER_NKEYS, PEER_DKEY // 2), (PEER_DKEY // 2) ** -0.5),
        "peer_u": nrm(ks[19], (DEPTH, PEER_NEXPERTS, D), D ** -0.5),
        "peer_v": nrm(ks[20], (DEPTH, PEER_NEXPERTS, D), PEER_HEADS ** -0.5),
        "final_norm_g": gain(ks[21], (D,)),
    }

def second_block(x, c, w_ada, b_ada, norm1_g, w_in, gla_w_gate_up, gla_b_gate, gla_norm_g,
              dsa_kv_norm_g, dsa_w_uk, dsa_w_uv, w_branch_a, w_branch_b, w_out, norm2_g,
              peer_w_q, peer_sub_keys_1, peer_sub_keys_2, peer_u, peer_v, final_norm_g):
    split_points = np.cumsum(IN_SIZES)[:-1].tolist()
    for l in range(DEPTH):
        ada = jax.nn.silu(c) @ w_ada[l] + b_ada[l]
        shift1, scale1, gate1, shift2, scale2, gate2 = jnp.split(ada[:, None, :], 6, axis=-1)

        h = _rmsnorm(x, norm1_g[l]) * (1.0 + scale1) + shift1
        proj = h @ w_in[l]
        (gq, gk, gv, gr, glow, dq, dkv, iq, ik, iw, za, zb) = jnp.split(proj, split_points, axis=-1)
        ya = _gla_branch(gq, gk, gv, gr, glow, gla_w_gate_up[l], gla_b_gate[l], gla_norm_g[l]) @ w_branch_a[l]
        yb = _dsa_branch(dq, dkv, iq, ik, iw, dsa_kv_norm_g[l], dsa_w_uk[l], dsa_w_uv[l]) @ w_branch_b[l]
        y = (jax.nn.sigmoid(za) * ya + jax.nn.sigmoid(zb) * yb) @ w_out[l]
        x = x + gate1 * y

        h2 = _rmsnorm(x, norm2_g[l]) * (1.0 + scale2) + shift2
        x = x + gate2 * _peer(h2, peer_w_q[l], peer_sub_keys_1[l], peer_sub_keys_2[l], peer_u[l], peer_v[l])
    return _rmsnorm(x, final_norm_g)


def setup_inputs(seed=0):
    out = dict(first_inputs(seed))
    for name, value in second_inputs(seed + 1).items():
        if name != "x":
            out[name + "_2"] = value
    return out


def reference(
    x, l0_norm, l0_w_in, l0_q_norm, l0_w_uq, l0_kv_norm, l0_w_ukv, l0_w_out, l1_norm, l1_w_in,
    l1_conv_w, l1_conv_b, l1_filt_w1, l1_filt_b1, l1_filt_w2, l1_filt_b2, l1_filt_w3,
    l1_filt_b3, l1_filt_w4, l1_filt_freq, l1_filt_bias, l1_w_out, final_norm, c_2, w_ada_2,
    b_ada_2, norm1_g_2, w_in_2, gla_w_gate_up_2, gla_b_gate_2, gla_norm_g_2, dsa_kv_norm_g_2,
    dsa_w_uk_2, dsa_w_uv_2, w_branch_a_2, w_branch_b_2, w_out_2, norm2_g_2, peer_w_q_2,
    peer_sub_keys_1_2, peer_sub_keys_2_2, peer_u_2, peer_v_2, final_norm_g_2,
):
    x = first_block(
        x, l0_norm, l0_w_in, l0_q_norm, l0_w_uq, l0_kv_norm, l0_w_ukv, l0_w_out, l1_norm,
        l1_w_in, l1_conv_w, l1_conv_b, l1_filt_w1, l1_filt_b1, l1_filt_w2, l1_filt_b2,
        l1_filt_w3, l1_filt_b3, l1_filt_w4, l1_filt_freq, l1_filt_bias, l1_w_out, final_norm,
    )
    return second_block(
        x, c_2, w_ada_2, b_ada_2, norm1_g_2, w_in_2, gla_w_gate_up_2, gla_b_gate_2,
        gla_norm_g_2, dsa_kv_norm_g_2, dsa_w_uk_2, dsa_w_uv_2, w_branch_a_2, w_branch_b_2,
        w_out_2, norm2_g_2, peer_w_q_2, peer_sub_keys_1_2, peer_sub_keys_2_2, peer_u_2,
        peer_v_2, final_norm_g_2,
    )


_drawn_inputs = setup_inputs


def setup_inputs(seed=0):
    import zlib

    import numpy as np

    out = dict(_drawn_inputs(seed))
    spreads = {}
    factors = {'l0_norm': 8.0,
     'l0_q_norm': 8.0,
     'l0_kv_norm': 8.0,
     'final_norm': 10.643,
     'gla_w_gate_up_2': 3.104,
     'gla_b_gate_2': 8.0,
     'gla_norm_g_2': 19.182,
     'dsa_kv_norm_g_2': 4.52,
     'norm2_g_2': 8.96}
    for name, (base, spread) in spreads.items():
        noise = np.random.default_rng([zlib.crc32(name.encode()), seed]).standard_normal(out[name].shape)
        drawn = base * np.exp(spread * noise) if base else spread * noise
        out[name] = __import__('jax').numpy.asarray(drawn.astype(out[name].dtype))
    for name, factor in factors.items():
        out[name] = (out[name] * factor).astype(out[name].dtype)
    return out
```

```python
from contextlib import ExitStack

import numpy as np

import concourse.bass as bass
from concourse import mybir

F32 = mybir.dt.float32
F32R = mybir.dt.float32r
U32 = mybir.dt.uint32
ALU = mybir.AluOpType
ACT = mybir.ActivationFunctionType
AXX = mybir.AxisListType.X

P = 128
T = 512
NT = 4
EPS = 1e-6
ITEM = 2048
GLA_H = 4
H = 8
NEG = -1e30
FILL = -1e38
TAKEN = -3e38
AHEAD = 3
CT = 16

VEC = {}
_at = 0
for _name, _n in (("l0_norm", 8), ("l0_q_norm", 3), ("l0_kv_norm", 2), ("final_norm", 8), ("c_2", 8),
                  ("b_ada_2", 48), ("norm1_g_2", 8), ("gla_b_gate_2", 4), ("gla_norm_g_2", 8),
                  ("dsa_kv_norm_g_2", 2), ("norm2_g_2", 8), ("final_norm_g_2", 8)):
    VEC[_name] = (_at, _n)
    _at += _n
NVEC = _at
CONST = {"ident": (0, 128), "ones": (128, 128), "iota": (256, 128), "rel": (384, 512), "reset": (896, 512)}
NCONST = 1408


class Calls:

    def __init__(self, **methods):
        self.methods = methods

    def hold(self, name, args, kwargs):
        method = self.methods[name]
        return lambda: method(*args, **kwargs)

    def activation(self, *args, **kwargs):
        return self.hold("activation", args, kwargs)

    def tensor_copy(self, *args, **kwargs):
        return self.hold("tensor_copy", args, kwargs)

    def tensor_tensor(self, *args, **kwargs):
        return self.hold("tensor_tensor", args, kwargs)

    def tensor_scalar(self, *args, **kwargs):
        return self.hold("tensor_scalar", args, kwargs)

    def scalar_tensor_tensor(self, *args, **kwargs):
        return self.hold("scalar_tensor_tensor", args, kwargs)

    def tensor_tensor_scan(self, *args, **kwargs):
        return self.hold("tensor_tensor_scan", args, kwargs)

    def tensor_reduce(self, *args, **kwargs):
        return self.hold("tensor_reduce", args, kwargs)

    def reciprocal(self, *args, **kwargs):
        return self.hold("reciprocal", args, kwargs)

    def max(self, *args, **kwargs):
        return self.hold("max", args, kwargs)

    def max_index(self, *args, **kwargs):
        return self.hold("max_index", args, kwargs)

    def match_replace(self, *args, **kwargs):
        return self.hold("match_replace", args, kwargs)

    def memset(self, *args, **kwargs):
        return self.hold("memset", args, kwargs)

    def affine_select(self, *args, **kwargs):
        return self.hold("affine_select", args, kwargs)

    def matmul(self, *args, **kwargs):
        return self.hold("matmul", args, kwargs)

    def transpose(self, *args, **kwargs):
        return self.hold("transpose", args, kwargs)

    def dma_start(self, *args, **kwargs):
        return self.hold("dma_start", args, kwargs)

    def wait_ge(self, *args, **kwargs):
        return self.hold("wait_ge", args, kwargs)


class Engine:

    def __init__(self, sem, **methods):
        self.sem, self.n, self.seen, self.ops, self.open = sem, 0, {}, [], False
        self.calls = Calls(**methods)

    def wait(self, *tokens):
        for tok in tokens:
            if tok is None:
                continue
            sem, value = tok
            if self.seen.get(sem.name, 0) < value:
                self.seen[sem.name] = value
                self.ops.append((self.calls.wait_ge(sem, value), None, 0))

    def do(self, fn, *tokens, sig=True):
        self.wait(*tokens)
        if sig:
            self.n += 1
        self.ops.append((fn(self.calls), self.sem if sig else None, 1))
        self.open = not sig
        return (self.sem, self.n)

    def dma(self, dst, src, sem):
        self.ops.append((self.calls.dma_start(dst, src), sem, 16))

    def now(self):
        assert not self.open
        return (self.sem, self.n) if self.n else None

    def run(self):
        for call, sem, by in self.ops:
            instruction = call()
            if sem is not None:
                instruction.then_inc(sem, by)


class Slots:

    def __init__(self, aps):
        self.free = [(ap, ()) for ap in aps]

    def take(self):
        return self.free.pop(0)

    def give(self, ap, *tokens):
        self.free.append((ap, tokens))


def build(nc, ins, out):
    ctx = ExitStack()
    with ctx:
        def sb(name, n, dt=F32):
            return ctx.enter_context(nc.sbuf_tensor(name, [P, n], dt))

        def sem(name):
            return ctx.enter_context(nc.semaphore(name))

        PE = Engine(sem("s_pe"), matmul=nc.tensor.matmul, transpose=nc.tensor.transpose, wait_ge=nc.tensor.wait_ge)
        SC = Engine(sem("s_act"), activation=nc.scalar.activation, dma_start=nc.scalar.dma_start,
                    wait_ge=nc.scalar.wait_ge)
        v = nc.vector
        VE = Engine(sem("s_dve"), tensor_copy=v.tensor_copy, tensor_tensor=v.tensor_tensor,
                    tensor_scalar=v.tensor_scalar, scalar_tensor_tensor=v.scalar_tensor_tensor,
                    tensor_tensor_scan=v.tensor_tensor_scan, tensor_reduce=v.tensor_reduce,
                    reciprocal=v.reciprocal, max=v.max, max_index=v.max_index, match_replace=v.match_replace,
                    wait_ge=v.wait_ge)
        GP = Engine(sem("s_pool"), memset=nc.gpsimd.memset, affine_select=nc.gpsimd.affine_select,
                    wait_ge=nc.gpsimd.wait_ge)
        SP = Engine(sem("s_sp"), dma_start=nc.sync.dma_start, wait_ge=nc.sync.wait_ge)

        raw = sb("raw", 4 * ITEM)
        whl = sb("whl", 4 * ITEM, F32R)
        xhl = sb("xhl", 8192, F32R)
        yhl = sb("yhl", 8192, F32R)
        XT = sb("XT", 4096)
        cst = sb("cst", NCONST)
        vec = sb("vec", NVEC)
        ada = sb("ada", 48)
        mod = sb("mod", 16)
        sc8 = sb("sc8", 8)
        skT = sb("skT", 256)
        LN = 14400
        L = sb("L", LN)
        banks = Slots([ctx.enter_context(nc.psum_tensor(f"bank{i}", [P, 512], F32))[:, :] for i in range(8)])

        def C(name):
            o, n = CONST[name]
            return cst[:, o:o + n]

        def V(name, j):
            o, _ = VEC[name]
            return vec[:, o + j:o + j + 1]

        def F(ap):
            return ap.bitcast(F32)

        ident, ones, iota = C("ident"), C("ones"), C("iota")

        class Local:
            def __init__(self):
                self.at = 0

            def __call__(self, n):
                ap = L[:, self.at:self.at + n]
                self.at += n
                assert self.at <= LN, self.at
                return ap

        def phase():
            toks = [e.now() for e in (PE, SC, VE, GP)]
            for e in (PE, SC, VE, GP):
                e.wait(*toks)
            return Local()

        s_in = [sem(f"s_in{i}") for i in range(6)]

        def load(i, dst, src, *tokens):
            SP.wait(*tokens)
            SP.dma(dst, src, s_in[i])

        load(0, XT[:, :].rearrange("p (k t) -> p k t", k=8), ins["xT"].rearrange("(k p) t -> p k t", p=P))
        load(1, cst[:, 0:384], ins["consts"][:, 0:384])
        load(2, vec[:, :], ins["vecs"])
        tk_x, tk_c, tk_v = (s_in[0], 16), (s_in[1], 16), (s_in[2], 16)

        items = []
        for i in range(8):
            items.append(("l0_in", ins["l0_in"][i], ITEM, True))
        for i in range(4):
            items.append(("uq", ins["l0_uq"][i], 1536, True))
            items.append(("ukv", ins["l0_ukv"][i], 1024, True))
            for j in range(6):
                items.append(("ada", ins["w_ada"][6 * i + j], ITEM, False))
        for i in range(4):
            items.append(("l0_out", ins["l0_out"][i], ITEM, True))
        items.append(("small", ins["w_small"], ITEM, True))
        for h in range(GLA_H):
            for j in range(3):
                items.append(("gla", ins["w_gla"][3 * h + j], ITEM, True))
        for i in range(4):
            items.append(("za", ins["w_za"][i], ITEM, True))
            items.append(("ba", ins["w_ba"][i], ITEM, True))
        items.append(("dkv", ins["w_dkv"][0], ITEM, True))
        for i in range(2):
            items.append(("iq", ins["w_iq"][i], ITEM, True))
        for i in range(4):
            if i % 2 == 0:
                items.append(("ukuv", ins["w_ukuv"][i // 2], ITEM, False))
            items.append(("dq", ins["w_dq"][i], ITEM, True))
        for i in range(4):
            items.append(("zb", ins["w_zb"][i], ITEM, True))
            items.append(("bb", ins["w_bb"][i], ITEM, True))
        for i in range(4):
            items.append(("w_out", ins["w_out"][i], ITEM, True))
        for i in range(8):
            items.append(("pq", ins["w_pq"][i], ITEM, True))
        NG = 32
        for g in range(AHEAD):
            items += [("U", ins["U"][2 * g + j], ITEM, True) for j in range(2)]
        for g in range(NG):
            items += [("V", ins["V"][2 * g + j], ITEM, True) for j in range(2)]
            if g + AHEAD < NG:
                items += [("U", ins["U"][2 * (g + AHEAD) + j], ITEM, True) for j in range(2)]

        s_raw = [sem(f"s_raw{i}") for i in range(4)]
        raw_free = [()] * 4
        landed = {}
        state = {"dma": 0, "conv": 0, "use": 0}

        def pump():
            while state["dma"] < len(items) and raw_free[state["dma"] % 4] is not None:
                i = state["dma"]
                r = i % 4
                name, src, n, _ = items[i]
                SP.wait(*raw_free[r])
                raw_free[r] = None
                SP.dma(raw[:, r * ITEM:r * ITEM + n], src, s_raw[r])
                landed[i] = (s_raw[r], 16 * (i // 4 + 1))
                state["dma"] += 1

        whl_free = [(), ()]
        ready = {}
        nconv = [0]

        def convert():
            i = state["conv"]
            if i >= len(items):
                return
            name, src, n, conv = items[i]
            assert i in landed
            r = i % 4
            src_ap = raw[:, r * ITEM:r * ITEM + n]
            if conv:
                w = nconv[0] % 2
                if whl_free[w] is None:
                    return
                nconv[0] += 1
                hi = whl[:, 2 * w * ITEM:2 * w * ITEM + n]
                lo = whl[:, (2 * w + 1) * ITEM:(2 * w + 1) * ITEM + n]
                h = n // 2
                th = None
                for a, b in ((0, h), (h, n)):
                    th = SC.do(lambda e: e.activation(hi[:, a:b], src_ap[:, a:b], ACT.Copy),
                               landed[i], *whl_free[w])
                    tl = VE.do(lambda e: e.tensor_tensor(lo[:, a:b], src_ap[:, a:b], F(hi[:, a:b]),
                                                                   ALU.subtract),
                               landed[i], th, *whl_free[w])
                whl_free[w] = None
                raw_free[r] = (th, tl)
                ready[i] = (hi, lo, (th, tl), w)
            else:
                ready[i] = (src_ap, None, (landed[i],), r)
            state["conv"] += 1
            pump()

        def take(name):
            i = state["use"]
            assert items[i][0] == name, (items[i][0], name)
            while state["conv"] <= min(i + 1, len(items) - 1):
                before = state["conv"]
                convert()
                if state["conv"] == before:
                    break
            assert i in ready
            state["use"] += 1
            return (i,) + ready.pop(i)

        def done(item, *tokens):
            i, _, _, _, where = item
            if items[i][3]:
                whl_free[where] = tokens
            else:
                raw_free[where] = tokens
                pump()

        pump()

        def mm(bank, lhsT, rhs, start, stop, *tokens, sig=False):
            return PE.do(lambda e: e.matmul(bank, lhsT, rhs, start=start, stop=stop, skip_group_check=True),
                         *tokens, sig=sig)

        def mm3(o, a, b, nk, *tokens):
            PE.wait(*tokens)
            for k in range(nk):
                (ah, al), (bh, bl) = a(k), b(k)
                mm(o, ah, bh, k == 0, False)
                mm(o, ah, bl, False, False)
                tok = mm(o, al, bh, False, k == nk - 1, sig=k == nk - 1)
            return tok

        def split(hi, lo, src, tok, *waits):
            th = SC.do(lambda e: e.activation(hi, src, ACT.Copy), tok, *waits)
            tl = VE.do(lambda e: e.tensor_tensor(lo, src, F(hi), ALU.subtract), tok, th, *waits)
            return th, tl

        def hl(base, n):
            def at(k, a=0, b=T):
                return base[:, k * T + a:k * T + b], base[:, n + k * T + a:n + k * T + b]
            return at

        X = hl(xhl, 4096)
        Y = hl(yhl, 4096)

        def wchunk(item, nk, width, c):
            _, hi, lo, _, _ = item
            def at(k):
                o = k * width + c * P
                return hi[:, o:o + P], lo[:, o:o + P]
            return at

        def bank():
            return banks.take()

        def projT(item, c, src, nk=8, width=256, *tokens):
            b, free = bank()
            tok = mm3(b, wchunk(item, nk, width, c), lambda k: src(k), nk, *item[3], *free, *tokens)
            return b, tok

        def rstd(sq_src, nk, width, r, sq, *tokens):
            b, free = bank()
            PE.wait(*free)
            sqs = Slots([sq[:, 0:T], sq[:, T:2 * T]])
            for k in range(nk):
                s, fr = sqs.take()
                src = sq_src(k)
                t = SC.do(lambda e, s=s, src=src: e.activation(s, src, ACT.Square), *tokens, *fr)
                tp = mm(b, ones, s, k == 0, k == nk - 1, t, tk_c, sig=True)
                sqs.give(s, tp)
            t0 = VE.do(lambda e: e.tensor_scalar(r, b, 1.0 / width, EPS, ALU.mult, ALU.add), tp, *tokens)
            banks.give(b, t0)
            t = SC.do(lambda e: e.activation(r, r, ACT.Sqrt), t0)
            return VE.do(lambda e: e.reciprocal(r, r), t)

        loc = Local()
        cq, ckv, kpe, gate = loc(1536), loc(1024), loc(512), loc(4096)
        rt, tmp = loc(T), loc(1024)
        rope = cst[:, 384:1408]
        load(3, rope, ins["rope"])
        tk_r = (s_in[3], 16)
        cosT, sinT = rope[:, 0:T], rope[:, T:2 * T]

        def x_at(k):
            return XT[:, k * T:(k + 1) * T]

        def norm_into(dst, src, nk, r, tr, gain, tmps, *tokens):
            toks = []
            tm = Slots([tmps[:, 0:T], tmps[:, T:2 * T]])
            for k in range(nk):
                t_, fr = tm.take()
                hi, lo = dst(k)
                a = VE.do(lambda e: e.scalar_tensor_tensor(t_, src(k), gain(k), r, ALU.mult, ALU.mult),
                          tr, tk_v, *fr, *tokens)
                th, tl = split(hi, lo, t_, a)
                tm.give(t_, th, tl)
                toks = [th, tl]
            return toks

        tr = rstd(x_at, 8, 1024, rt, tmp, tk_x)
        tX = norm_into(X, x_at, 8, rt, tr, lambda k: V("l0_norm", k), tmp, tr)

        it = None
        t_l = None
        for ch in range(15):
            if ch % 2 == 0:
                it = take("l0_in")
            b, tok = projT(it, ch % 2, X, 8, 256, *tX)
            if ch % 2 == 1 or ch == 14:
                done(it, tok)
            if ch < 5:
                dst = cq[:, ch * T:(ch + 1) * T] if ch < 3 else ckv[:, (ch - 3) * T:(ch - 2) * T]
                t = SC.do(lambda e, d=dst, b=b: e.activation(d, b, ACT.Copy), tok)
                banks.give(b, t)
                t_l = t
            elif ch == 5:
                t_k = VE.do(lambda e: e.tensor_tensor(kpe, b, cosT, ALU.mult), tok, tk_r)
                banks.give(b, t_k)
            elif ch == 6:
                t2 = VE.do(lambda e: e.tensor_tensor(tmp[:, 0:T], b, sinT, ALU.mult), tok, tk_r, *tX)
                banks.give(b, t2)
                t_k = VE.do(lambda e: e.tensor_tensor(kpe, kpe, tmp[:, 0:T], ALU.add), t2, t_k)
            else:
                g = gate[:, (ch - 7) * T:(ch - 6) * T]
                t = SC.do(lambda e: e.activation(g, b, ACT.Silu), tok)
                banks.give(b, t)
        last_pe = tok
        CQ = hl(xhl, 2560)
        CK = lambda k, a=0, b_=T: CQ(k + 3, a, b_)
        tr = rstd(lambda k: cq[:, k * T:(k + 1) * T], 3, 384, rt, tmp, t_l, t_k)
        t1 = norm_into(CQ, lambda k: cq[:, k * T:(k + 1) * T], 3, rt, tr, lambda k: V("l0_q_norm", k), tmp, tr, last_pe)
        tr = rstd(lambda k: ckv[:, k * T:(k + 1) * T], 2, 256, rt, tmp, *t1)
        t2 = norm_into(CK, lambda k: ckv[:, k * T:(k + 1) * T], 2, rt, tr, lambda k: V("l0_kv_norm", k), tmp, tr)

        silc = sc8[:, 0:8]
        o_, n_ = VEC["c_2"]
        t_c = SC.do(lambda e: e.activation(silc, vec[:, o_:o_ + 8], ACT.Silu), tk_v)
        adab, free = bank()
        PE.wait(*free)

        class Attn:

            def __init__(self, loc, causal, scale):
                self.causal, self.scale = causal, scale
                self.P = [Slots([loc((qt + 1) * P if causal else T)]) for qt in range(NT)]
                self.PT = Slots([loc(4 * T)])
                self.st = Slots([loc(4) for _ in range(8)])

            def scores(self, parts, bias=None, *tokens):
                rows = []
                for qt in range(NT):
                    n = (qt + 1) * P if self.causal else T
                    b, free = bank()
                    PE.wait(*free, *tokens)
                    for j, (q, k) in enumerate(parts):
                        ts = mm(b[:, 0:n], q(qt * P, (qt + 1) * P), k(n), j == 0, j == len(parts) - 1,
                                sig=j == len(parts) - 1)
                    p, pf = self.P[qt].take()
                    st, sf = self.st.take()
                    pn = p[:, 0:n]
                    if bias is None:
                        tm = VE.do(lambda e: e.tensor_reduce(st[:, 0:1], b, AXX, ALU.max, negate=True),
                                   ts, *sf)
                        tm = VE.do(lambda e: e.tensor_scalar(st[:, 1:2], st[:, 0:1], self.scale, None,
                                                                    ALU.mult), tm)
                        te = SC.do(lambda e: e.activation(
                            pn, b, ACT.Exp, bias=st[:, 1:2], scale=self.scale, accum_out=st[:, 2:3]), tm, *pf)
                        banks.give(b, te)
                    else:
                        bb, tb, bfree = bias(qt)
                        t0 = VE.do(lambda e: e.scalar_tensor_tensor(
                            pn, b[:, 0:n], self.scale, bb, ALU.mult, ALU.add), ts, tb, *pf)
                        banks.give(b, t0)
                        bfree(t0)
                        tm = VE.do(lambda e: e.tensor_reduce(st[:, 1:2], pn, AXX, ALU.max,
                                                                           negate=True), t0, *sf)
                        te = SC.do(lambda e: e.activation(
                            pn, pn, ACT.Exp, bias=st[:, 1:2], scale=1.0, accum_out=st[:, 2:3]), tm)
                    ti = VE.do(lambda e: e.reciprocal(st[:, 3:4], st[:, 2:3]), te)
                    tn = VE.do(lambda e: e.tensor_scalar(pn, pn, st[:, 3:4], None, ALU.mult), ti)
                    self.st.give(st, tn)
                    rows.append((p, tn))
                return rows

            def values(self, rows, v, *tokens):
                pt, ptf = self.PT.take()
                ptv = pt.rearrange("p (c q) -> p c q", c=4)
                toks = []
                for qt in range(NT):
                    p, tn = rows[qt]
                    nc_ = qt + 1 if self.causal else NT
                    b, free = bank()
                    PE.wait(*free)
                    for c in range(nc_):
                        tt = PE.do(lambda e: e.transpose(b[:, c * P:(c + 1) * P],
                                                                        p[:, c * P:(c + 1) * P], ident),
                                   tn, tk_c, sig=c == nc_ - 1)
                    self.P[qt].give(p, tt)
                    cp = lambda e: e.tensor_copy(
                        ptv[:, 0:nc_, qt * P:(qt + 1) * P], b[:, 0:nc_ * P].rearrange("p (c q) -> p c q", c=nc_))
                    ca = lambda e: e.activation(
                        ptv[:, 0:nc_, qt * P:(qt + 1) * P], b[:, 0:nc_ * P].rearrange("p (c q) -> p c q", c=nc_),
                        ACT.Copy)
                    tc = VE.do(cp, tt, *ptf) if qt % 2 else SC.do(ca, tt, *ptf)
                    banks.give(b, tc)
                    toks.append(tc)
                o, free = bank()
                PE.wait(*free, *toks, *tokens)
                for c in range(4):
                    a = c * P if self.causal else 0
                    to = mm(o[:, a:T], v(c), ptv[:, c, a:T], c == 0, c == 3, sig=c == 3)
                self.PT.give(pt, to)
                return o, to

        loc = phase()
        loc(2560)
        kpe_keep = loc(512)
        gate_keep = loc(4096)
        qn = Slots([L[:, 0:1024]])
        kn = Slots([L[:, 1024:2048]])
        qp = Slots([L[:, 2048:2560]])
        loc.at += 1536
        vv = Slots([loc(1024)])
        attn = Attn(loc, False, (128 + 64) ** -0.5)
        rtmp = L[:, 7168:7680]

        def evac(dst, b, tok, *waits, eng=None):
            if eng is VE:
                t = VE.do(lambda e: e.tensor_copy(dst, b), tok, *waits)
            else:
                t = SC.do(lambda e: e.activation(dst, b, ACT.Copy), tok, *waits)
            banks.give(b if b.shape[1] == 512 else b, t)
            return t

        pend = []

        def finish_l0(job):
            rows, vh, hd, tv, rel = job
            o, to = attn.values(rows, vh, tv)
            og = tmpo[:, (hd % 2) * T:(hd % 2 + 1) * T]
            t = VE.do(lambda e: e.tensor_tensor(og, o, gate_keep[:, hd * T:(hd + 1) * T], ALU.mult), to,
                      *ogfree[hd % 2])
            banks.give(o, t)
            hi, lo = Y(hd)
            th, tl = split(hi, lo, og, t)
            ogfree[hd % 2] = (th, tl)
            if rel:
                rel(to)
            return th, tl

        tmpo = L[:, 7680:8704]
        ogfree = [(), ()]
        for pr in range(4):
            it = take("uq")
            hs = []
            qb, qf = qn.take()
            for c in range(2):
                b, tok = projT(it, c, CQ, 3, 512, *t1)
                tq = evac(qb[:, c * T:(c + 1) * T], b, tok, *qf)
            b, tok = projT(it, 2, CQ, 3, 512)
            pb, pf = qp.take()
            ta = VE.do(lambda e: e.tensor_tensor(pb, b, cosT, ALU.mult), tok, *pf)
            banks.give(b, ta)
            b, tok = projT(it, 3, CQ, 3, 512)
            done(it, tok)
            tb = VE.do(lambda e: e.tensor_tensor(rtmp, b, sinT, ALU.mult), tok)
            banks.give(b, tb)
            tp = VE.do(lambda e: e.tensor_tensor(pb, pb, rtmp, ALU.add), ta, tb)
            it = take("ukv")
            kb, kf = kn.take()
            for c in range(2):
                b, tok = projT(it, c, CK, 2, 512, *t2)
                tkk = evac(kb[:, c * T:(c + 1) * T], b, tok, *kf)
            vb, vf = vv.take()
            for tt2 in range(2):
                b, free = bank()
                PE.wait(*free)
                _, hi, lo, _, _ = it
                for half in range(2):
                    qt = 2 * tt2 + half
                    first = half == 0
                    for k in range(2):
                        a = CK(k, qt * P, (qt + 1) * P)
                        w = (hi[:, k * 512 + 256:k * 512 + 512], lo[:, k * 512 + 256:k * 512 + 512])
                        o = b[:, half * 256:(half + 1) * 256]
                        mm(o, a[0], w[0], first and k == 0, False)
                        mm(o, a[0], w[1], False, False)
                        tok = mm(o, a[1], w[0], False, k == 1 and half == 1, sig=k == 1 and half == 1)
                tv = evac(vb[:, tt2 * 512:(tt2 + 1) * 512], b, tok, *vf, eng=VE)
            done(it, tok)
            for j in range(2):
                hd = 2 * pr + j
                o64 = 64 * j
                rows = attn.scores(
                    [(lambda a, b, j=j: qb[:, j * T + a:j * T + b], lambda n, j=j: kb[:, j * T:j * T + n]),
                     (lambda a, b, o=o64: pb[o:o + 64, a:b], lambda n, o=o64: kpe_keep[o:o + 64, 0:n])],
                    None, tq, tp, tkk)
                for q_ in range(3):
                    ia = take("ada")
                    i0 = 6 * pr + 3 * j + q_
                    src = ia[1]
                    for c in range(2):
                        for k in range(8):
                            ta_ = mm(adab[:, 2 * i0 + c:2 * i0 + c + 1], src[:, k * 256 + c * P:k * 256 + (c + 1) * P],
                                     silc[:, k:k + 1], i0 == 0 and c == 0 and k == 0, False, *ia[3], t_c,
                                     sig=k == 7)
                    done(ia, ta_)
                rel = None
                tO = finish_l0((rows, lambda c, j=j, vb=vb: vb[:, c * 256 + j * P:c * 256 + (j + 1) * P], hd, tv, rel))
            e_pe = PE.now()
            qn.give(qb, e_pe)
            kn.give(kb, e_pe)
            qp.give(pb, e_pe)
            vv.give(vb, e_pe)
        o_, n_ = VEC["b_ada_2"]
        t_ada = VE.do(lambda e: e.tensor_tensor(ada[:, :], adab[:, 0:48], vec[:, o_:o_ + 48], ALU.add), ta_, tk_v)
        banks.give(adab, t_ada)

        def AD(part, k):
            return ada[:, part * 8 + k:part * 8 + k + 1]

        for i in range(4):
            it = take("l0_out")
            for c in range(2):
                b, tok = projT(it, c, Y, 8, 256, *tO)
                m = 2 * i + c
                t_x = VE.do(lambda e: e.tensor_tensor(x_at(m), x_at(m), b, ALU.add), tok)
                banks.give(b, t_x)
            done(it, tok)

        load(1, cst[:, 384:NCONST], ins["consts"][:, 384:NCONST], VE.now())
        tk_c2 = (s_in[1], 32)
        loc = phase()
        rt, tmp = loc(T), loc(1024)
        tr = rstd(x_at, 8, 1024, rt, tmp, t_x)
        tk = None
        for k in range(8):
            tk = VE.do(lambda e: e.scalar_tensor_tensor(x_at(k), x_at(k), V("final_norm", k), rt,
                                                             ALU.mult, ALU.mult), tr)

        def modulated(scale_part, shift_part, gname, tk, tmp, rt):
            g0, _ = VEC[gname]
            t_m = VE.do(lambda e: e.scalar_tensor_tensor(mod[:, 0:8], ada[:, scale_part * 8:scale_part * 8 + 8], 1.0,
                                                         vec[:, g0:g0 + 8], ALU.add, ALU.mult), t_ada, SC.now())
            tr = rstd(x_at, 8, 1024, rt, tmp, tk)
            tm = Slots([tmp[:, 0:T], tmp[:, T:2 * T]])
            for k in range(8):
                t_, fr = tm.take()
                hi, lo = X(k)
                a = VE.do(lambda e: e.tensor_tensor(t_, x_at(k), rt, ALU.mult), tr, *fr)
                a = SC.do(lambda e: e.activation(t_, t_, ACT.Identity, bias=AD(shift_part, k),
                                                             scale=mod[:, k:k + 1]), a, t_m)
                th, tl = split(hi, lo, t_, a)
                tm.give(t_, th, tl)
            return th, tl

        tX = modulated(1, 0, "norm1_g_2", tk, tmp, rt)

        loc = Local()
        YM = loc(4096)
        glow = loc(T)
        iw = loc(32)
        ik = loc(T)
        keep = loc.at
        it = take("small")
        b, tok = projT(it, 0, X, 8, 256, *tX)
        t_ik = evac(ik, b, tok)
        b, free = bank()
        tok = mm3(b, lambda k: (it[1][:, k * 256 + 128:k * 256 + 256], it[2][:, k * 256 + 128:k * 256 + 256]),
                  X, 8, *free)
        t_gl = evac(glow, b, tok)
        b, free = bank()
        PE.wait(*free)
        for qt in range(NT):
            for k in range(8):
                a = X(k, qt * P, (qt + 1) * P)
                w = (it[1][:, k * 256 + 144:k * 256 + 152], it[2][:, k * 256 + 144:k * 256 + 152])
                o = b[:, 8 * qt:8 * qt + 8]
                mm(o, a[0], w[0], qt == 0 and k == 0, False)
                mm(o, a[0], w[1], False, False)
                tok = mm(o, a[1], w[0], False, False, sig=k == 7 and qt == 3)
        done(it, tok)
        t_iw = SC.do(lambda e: e.activation(iw, b[:, 0:32], ACT.Copy, scale=8.0 ** -0.5), tok)
        banks.give(b, t_iw)
        wgu = loc(T)
        load(4, wgu[0:16, :], ins["gate_up"], SC.now(), VE.now())
        tk_gu = (s_in[4], 16)

        la, E1, E2, E3, kd, ke = (loc(T) for _ in range(6))
        vtok = loc(1024)
        AT = loc(T)
        Sst = Slots([loc(256), loc(256)])
        ATv = AT.rearrange("p (t q) -> p t q", t=4)
        t_z = GP.do(lambda e: e.memset(AT, 0.0))
        t_hd = None
        tY = ()
        for h in range(GLA_H):
            it = take("gla")
            bq, tq = projT(it, 0, X, 8, 256)
            bk, tk_ = projT(it, 1, X, 8, 256)
            done(it, tk_)
            bz, free = bank()
            tz = mm(bz, wgu[0:16, h * P:(h + 1) * P], glow[0:16, :], True, True, tk_gu, t_gl, *free, sig=True)
            it = take("gla")
            tv = []
            for t2_ in range(2):
                b, free = bank()
                PE.wait(*free)
                PE.wait(*it[3])
                for half in range(2):
                    qt = 2 * t2_ + half
                    for k in range(8):
                        a = X(k, qt * P, (qt + 1) * P)
                        w = (it[1][:, k * 256:(k + 1) * 256], it[2][:, k * 256:(k + 1) * 256])
                        o = b[:, half * 256:(half + 1) * 256]
                        mm(o, a[0], w[0], half == 0 and k == 0, False)
                        mm(o, a[0], w[1], False, False)
                        tok = mm(o, a[1], w[0], False, False, sig=k == 7 and half == 1)
                tv.append(evac(vtok[:, t2_ * 512:(t2_ + 1) * 512], b, tok, t_hd))
            done(it, tok)
            bg = V("gla_b_gate_2", h)
            t2 = VE.do(lambda e: e.tensor_scalar(E2, bz, bg, None, ALU.add), tz, t_hd)
            banks.give(bz, t2)
            t1 = SC.do(lambda e: e.activation(E1, E2, ACT.Abs), t2, t_hd)
            t1 = SC.do(lambda e: e.activation(E1, E1, ACT.Exp, scale=-1.0), t1)
            t1 = SC.do(lambda e: e.activation(E1, E1, ACT.Ln, bias=1.0), t1)
            t3 = VE.do(lambda e: e.scalar_tensor_tensor(E2, E2, 0.0, E1, ALU.min, ALU.subtract), t1, t2)
            t3 = VE.do(lambda e: e.tensor_tensor_scan(la, C("reset"), E2, 0.0, ALU.mult, ALU.add), t3, tk_c2)
            la_v = la.rearrange("p (c i) -> p c i", c=8)
            E3v = E3.rearrange("p (c i) -> p c i", c=8)
            t4 = VE.do(lambda e: e.tensor_tensor(E3v, la_v[:, :, 63:64].broadcast_to([P, 8, 64]), la_v, ALU.subtract), t3)
            t5 = SC.do(lambda e: e.activation(E1, la, ACT.Exp, scale=1.0 / 16), t3)
            t6 = SC.do(lambda e: e.activation(E2, la, ACT.Exp, scale=-1.0 / 16), t3)
            t7 = SC.do(lambda e: e.activation(E3, E3, ACT.Exp, scale=1.0 / 16), t4)
            t8 = VE.do(lambda e: e.scalar_tensor_tensor(kd, bq, 128.0 ** -0.5, E1, ALU.mult, ALU.mult), tq, t5)
            banks.give(bq, t8)
            t9 = VE.do(lambda e: e.tensor_tensor(E2, bk, E2, ALU.mult), tk_, t6)
            t10 = VE.do(lambda e: e.tensor_tensor(E3, bk, E3, ALU.mult), tk_, t7)
            banks.give(bk, t9, t10)
            b, free = bank()
            PE.wait(*free)
            for c in range(4):
                tt = PE.do(lambda e: e.transpose(b[:, c * P:(c + 1) * P], E3[:, c * P:(c + 1) * P], ident),
                           t10, sig=c == 3)
            tke = evac(ke, b, tt)
            b, free = bank()
            PE.wait(*free)
            for c in range(4):
                tt = mm(b[:, c * P:(c + 1) * P], E2[:, c * P:(c + 1) * P], kd[:, c * P:(c + 1) * P], c == 0, False,
                        t8, t9, sig=c == 3)
            bv = b.rearrange("p (t q) -> p t q", t=4)
            ta = SC.do(lambda e: e.activation(ATv[0:64, :, 0:64], bv[0:64, :, 0:64], ACT.Copy), tt, t_z)
            ta = SC.do(lambda e: e.activation(ATv[64:128, :, 64:128], bv[64:128, :, 64:128], ACT.Copy), tt)
            banks.give(b, ta)
            tg = GP.do(lambda e: e.affine_select(out=ATv, in_=ATv, compare_op=ALU.is_ge, fill=0.0, base=0,
                                                 pattern=[[0, 4], [1, 128]], channel_multiplier=-1), ta)
            ob = [bank(), bank()]
            for vh in range(2):
                PE.wait(*ob[vh][1], tg, *tv)
                for c in range(4):
                    mm(ob[vh][0][:, c * P:(c + 1) * P], vtok[:, c * 256 + vh * P:c * 256 + (vh + 1) * P],
                       ATv[:, c, :], c == 0, False)
            S = None
            for c in range(8):
                if S is not None:
                    for vh in range(2):
                        tO_ = mm(ob[vh][0][:, c * 64:(c + 1) * 64], S[0][:, vh * P:(vh + 1) * P],
                                 kd[:, c * 64:(c + 1) * 64], False, c == 7, S[1], sig=vh == 1)
                    Sst.give(S[0], tO_) if c == 7 else None
                if c == 7:
                    break
                u, free = bank()
                r0 = 64 * (c % 2)
                tu = mm(u[:, 0:256], ke[r0:r0 + 64, (c // 2) * P:(c // 2 + 1) * P],
                        vtok[r0:r0 + 64, (c // 2) * 256:(c // 2 + 1) * 256], True, True, tke, *free, sig=True)
                ns, nf = Sst.take()
                if S is None:
                    tS = VE.do(lambda e: e.tensor_copy(ns, u[:, 0:256]), tu, *nf)
                else:
                    tS = VE.do(lambda e, ns=ns, u=u, c=c, s=S[0]: e.scalar_tensor_tensor(
                        ns, s, E1[:, c * 64 + 63:c * 64 + 64], u[:, 0:256], ALU.mult, ALU.add), tu, S[1], *nf)
                    Sst.give(S[0], tS, tO_)
                banks.give(u, tS)
                S = (ns, tS)
            rr = la
            tr = rstd(lambda k: ob[k][0], 2, 256, rr, vtok, tO_)
            it = take("gla")
            for vh in range(2):
                ch = 2 * h + vh
                b, tok = projT(it, vh, X, 8, 256)
                t_s = SC.do(lambda e: e.activation(ke, b, ACT.Silu), tok, tO_, t_hd)
                banks.give(b, t_s)
                t_n = VE.do(lambda e: e.scalar_tensor_tensor(E2, ob[vh][0], V("gla_norm_g_2", ch), rr,
                                                                           ALU.mult, ALU.mult), tr, t_hd)
                banks.give(ob[vh][0], t_n)
                t_n = VE.do(lambda e: e.tensor_tensor(E2, E2, ke, ALU.mult), t_n, t_s)
                hi, lo = Y(ch)
                th, tl = split(hi, lo, E2, t_n)
                t_hd = tl
                SC.wait(tl)
                tY = (th, tl)
            done(it, tok)
        for i in range(4):
            it = take("za")
            sg = []
            for c in range(2):
                b, tok = projT(it, c, X, 8, 256)
                dst = (E1, E2)[c]
                t = SC.do(lambda e, b=b, d=dst: e.activation(d, b, ACT.Sigmoid), tok, VE.now())
                banks.give(b, t)
                sg.append(t)
            done(it, tok)
            it = take("ba")
            for c in range(2):
                b, tok = projT(it, c, Y, 8, 256, *tY)
                m = 2 * i + c
                t = VE.do(lambda e, b=b, m=m, d=(E1, E2)[c]: e.tensor_tensor(YM[:, m * T:(m + 1) * T], b, d, ALU.mult),
                          tok, sg[c])
                banks.give(b, t)
            done(it, tok)

        loc = phase()
        loc.at = keep
        ck, rt2, tmp2 = loc(1024), loc(T), loc(1024)
        it = take("dkv")
        for c in range(2):
            b, tok = projT(it, c, X, 8, 256)
            t = evac(ck[:, c * T:(c + 1) * T], b, tok)
        done(it, tok)
        tr = rstd(lambda k: ck[:, k * T:(k + 1) * T], 2, 256, rt2, tmp2, t)
        for k in range(2):
            t_ck = VE.do(lambda e: e.scalar_tensor_tensor(ck[:, k * T:(k + 1) * T], ck[:, k * T:(k + 1) * T],
                                                               V("dsa_kv_norm_g_2", k), rt2, ALU.mult, ALU.mult), tr)
        loc.at = keep + 1024
        Mb = loc(1280)
        mo = [0, P, 3 * P, 6 * P]
        keep2 = loc.at
        iq = loc(4 * T)
        work = loc(T)
        rl = Slots([loc(T), loc(T)])
        m8 = loc(8)
        for i in range(2):
            it = take("iq")
            for c in range(2):
                b, tok = projT(it, c, X, 8, 256)
                t_iq = evac(iq[:, (2 * i + c) * T:(2 * i + c + 1) * T], b, tok, t_ck)
            done(it, tok)
        t_mb = GP.do(lambda e: e.memset(Mb[:, 0:P], 0.0), t_ck)
        t_mb = GP.do(lambda e: e.affine_select(out=Mb[:, 0:P], in_=Mb[:, 0:P], compare_op=ALU.is_ge, fill=NEG, base=0,
                                               pattern=[[-1, P]], channel_multiplier=1), t_mb)
        tMb = [t_mb]
        for qt in range(1, NT):
            n = (qt + 1) * P
            acc = Mb[:, mo[qt]:mo[qt] + n]
            ta = None
            for hh in range(8):
                o64 = 64 * (hh % 2)
                b, free = bank()
                ts = mm(b[:, 0:n], iq[o64:o64 + 64, (hh // 2) * T + qt * P:(hh // 2) * T + (qt + 1) * P],
                        ik[o64:o64 + 64, 0:n], True, True, t_iq, t_ik, *free, sig=True)
                r_, rf = rl.take()
                t = SC.do(lambda e: e.activation(r_[:, 0:n], b[:, 0:n], ACT.Relu, scale=64.0 ** -0.5),
                          ts, *rf)
                banks.give(b, t)
                w = iw[:, 8 * qt + hh:8 * qt + hh + 1]
                if hh == 0:
                    ta = VE.do(lambda e: e.tensor_scalar(acc, r_[:, 0:n], w, None, ALU.mult),
                               t, t_iw)
                else:
                    ta = VE.do(lambda e: e.scalar_tensor_tensor(
                        acc, r_[:, 0:n], w, acc, ALU.mult, ALU.add), t, ta)
                rl.give(r_, ta)
            ta = GP.do(lambda e: e.affine_select(
                out=acc[:, n - P:n], in_=acc[:, n - P:n], compare_op=ALU.is_ge, fill=FILL, base=0,
                pattern=[[-1, P]], channel_multiplier=1), ta)
            for r in range(16):
                tm = VE.do(lambda e: e.max(m8, acc), ta)
                ta = VE.do(lambda e: e.match_replace(acc, m8, acc, TAKEN), tm)
            ta = VE.do(lambda e: e.tensor_scalar(acc, acc, TAKEN, NEG, ALU.not_equal, ALU.mult), ta)
            tMb.append(ta)

        phase()
        loc.at = keep2
        attn = Attn(loc, True, 128.0 ** -0.5)
        qd = Slots([loc(1024)])
        kv = Slots([loc(1024), loc(1024)])
        bia = Slots([glow])
        rel = C("rel")
        for i in range(4):
            if i % 2 == 0:
                uk = take("ukuv")
            it = take("dq")
            q, qf = qd.take()
            for c in range(2):
                b, tok = projT(it, c, X, 8, 256)
                tq = evac(q[:, c * T:(c + 1) * T], b, tok, *qf)
            done(it, tok)
            for c in range(2):
                hd = 2 * i + c
                u0 = (hd % 4) * 512
                kvb, kvf = kv.take()
                b, free = bank()
                for k in range(2):
                    tok = mm(b, uk[1][:, u0 + k * 256:u0 + k * 256 + P], ck[:, k * T:(k + 1) * T], k == 0, k == 1,
                             *uk[3], *free, t_ck, sig=k == 1)
                tk1 = evac(kvb[:, 0:T], b, tok, *kvf)
                b, free = bank()
                PE.wait(*free)
                for s_ in range(4):
                    for k in range(2):
                        tok = mm(b[:, s_ * P:(s_ + 1) * P], ck[:, k * T + s_ * P:k * T + (s_ + 1) * P],
                                 uk[1][:, u0 + k * 256 + P:u0 + k * 256 + 2 * P], s_ == 0 and k == 0, False,
                                 sig=s_ == 3 and k == 1)
                tk2 = evac(kvb[:, T:2 * T], b, tok, *kvf)
                slope = float(2.0 ** -(hd + 1))

                def bias(qt, slope=slope):
                    n = (qt + 1) * P
                    bb, bf = bia.take()
                    t = VE.do(lambda e: e.scalar_tensor_tensor(bb[:, 0:n], rel[:, 384 - P * qt:512], -slope,
                                                               Mb[:, mo[qt]:mo[qt] + n], ALU.mult, ALU.add),
                              tMb[qt], tk_c2, *bf)
                    return bb[:, 0:n], t, lambda tok: bia.give(bb, tok)

                rows = attn.scores([(lambda a, b_, c=c: q[:, c * T + a:c * T + b_], lambda n, kvb=kvb: kvb[:, 0:n])],
                                   bias, tq, tk1)
                o, to = attn.values(rows, lambda s_, kvb=kvb: kvb[:, T + s_ * P:T + (s_ + 1) * P], tk2)
                kv.give(kvb, to)
                hi, lo = Y(hd)
                th, tl = split(hi, lo, o, to)
                banks.give(o, th, tl)
            qd.give(q, to)
            if i % 2:
                done(uk, to)
        tY = (th, tl)
        phase()
        loc.at = keep
        E1, E2, E3 = loc(T), loc(T), loc(T)
        for i in range(4):
            it = take("zb")
            sg = []
            for c in range(2):
                b, tok = projT(it, c, X, 8, 256)
                t = SC.do(lambda e, b=b, d=(E1, E2)[c]: e.activation(d, b, ACT.Sigmoid), tok, VE.now())
                banks.give(b, t)
                sg.append(t)
            done(it, tok)
            it = take("bb")
            for c in range(2):
                b, tok = projT(it, c, Y, 8, 256, *tY)
                m = 2 * i + c
                d = (E1, E2)[c]
                t = VE.do(lambda e, b=b, d=d: e.tensor_tensor(d, b, d, ALU.mult), tok, sg[c])
                banks.give(b, t)
                t = VE.do(lambda e, m=m, d=d: e.tensor_tensor(YM[:, m * T:(m + 1) * T], YM[:, m * T:(m + 1) * T], d,
                                                              ALU.add), t)
            done(it, tok)
        for m in range(8):
            hi, lo = X(m)
            tM = split(hi, lo, YM[:, m * T:(m + 1) * T], t, PE.now())
        for i in range(4):
            it = take("w_out")
            for c in range(2):
                b, tok = projT(it, c, X, 8, 256, *tM)
                m = 2 * i + c
                t_x = VE.do(lambda e: e.scalar_tensor_tensor(x_at(m), b, AD(2, m), x_at(m),
                                                                       ALU.mult, ALU.add), tok)
                banks.give(b, t_x)
            done(it, tok)

        loc = phase()
        rt, tmp = loc(T), loc(1024)
        tX = modulated(4, 3, "norm2_g_2", t_x, tmp, rt)
        load(5, skT[:, :], ins["skT"])
        tk_sk = (s_in[5], 16)
        loc = Local()
        iaT, ibT, gT = loc(T), loc(T), loc(T)
        keep = loc.at
        qh = Slots([loc(1024)])
        sS = loc(1024)
        wk = loc(256)
        v16 = loc(2 * 4 * 128)
        i16 = loc(2 * 4 * 128)
        iu = loc(16)
        v16v = v16.rearrange("p (s t h k) -> p s t h k", s=2, t=4, h=8)
        i16v = i16.rearrange("p (s t h k) -> p s t h k", s=2, t=4, h=8)
        VE.wait(*tX)
        SC.wait(*tX)
        t_s = None
        tsel = None
        for h in range(8):
            it = take("pq")
            q, qf = qh.take()
            for c in range(2):
                b, tok = projT(it, c, X, 8, 256, *tX)
                tq = evac(q[:, c * T:(c + 1) * T], b, tok, *qf)
            done(it, tok)
            for c in range(2):
                b, free = bank()
                PE.wait(*free)
                for qt in range(NT):
                    tok = mm(b[:, qt * P:(qt + 1) * P], q[:, c * T + qt * P:c * T + (qt + 1) * P],
                             skT[:, c * P:(c + 1) * P], qt == 0, False, tq, tk_sk, sig=qt == 3)
                if c == 1:
                    qh.give(q, tok)
                t_s = evac(sS[:, c * T:(c + 1) * T], b, tok, tsel)
                for qt in range(NT):
                    s = sS[:, c * T + qt * P:c * T + (qt + 1) * P]
                    va, vb = v16v[:, c, qt, h, 0:8], v16v[:, c, qt, h, 8:16]
                    i_a, i_b = i16v[:, c, qt, h, 0:8].bitcast(U32), i16v[:, c, qt, h, 8:16].bitcast(U32)
                    w_ = wk[:, 0:P]
                    a = VE.do(lambda e: e.max(va, s), t_s)
                    VE.do(lambda e: e.max_index(i_a, va, s), a)
                    a = VE.do(lambda e: e.match_replace(w_, va, s, TAKEN), a)
                    a = VE.do(lambda e: e.max(vb, w_), a)
                    tsel = VE.do(lambda e: e.max_index(i_b, vb, w_), a)
        loc.at = keep
        cand = loc(2048)
        assert loc.at <= keep + 1024 + 1024 + 256
        loc.at = keep + 1024 + 1024 + 256 + 2048 + 16
        big = loc(2048)
        best, cidx, hi16, lo16, fi, fg = (loc(P) for _ in range(6))
        tot = loc(16)
        candw = loc(256)
        i16f = loc(2 * 4 * 128)
        ti = VE.do(lambda e: e.tensor_copy(i16f, i16.bitcast(U32)), tsel)
        i16fv = i16f.rearrange("p (s t h k) -> p s t h k", s=2, t=4, h=8)
        t_prev = None
        for qt in range(NT):
            cv = cand.rearrange("p (h i j) -> p h i j", h=8, i=16)
            for h in range(8):
                t = VE.do(lambda e: e.tensor_tensor(
                    cv[:, h], v16v[:, 0, qt, h, :].unsqueeze(2).broadcast_to([P, 16, 16]),
                    v16v[:, 1, qt, h, :].unsqueeze(1).broadcast_to([P, 16, 16]), ALU.add), tsel, t_prev,
                    PE.now() if qt == 0 else None)
            for h in range(8):
                ch = cand[:, h * 256:(h + 1) * 256]
                ba, bb = best[:, h * 16:h * 16 + 8], best[:, h * 16 + 8:h * 16 + 16]
                ca, cb = (cidx[:, h * 16:h * 16 + 8].bitcast(U32), cidx[:, h * 16 + 8:h * 16 + 16].bitcast(U32))
                a = VE.do(lambda e: e.max(ba, ch), t)
                VE.do(lambda e: e.max_index(ca, ba, ch), a)
                a = VE.do(lambda e: e.match_replace(candw, ba, ch, TAKEN), a)
                a = VE.do(lambda e: e.max(bb, candw), a)
                a = VE.do(lambda e: e.max_index(cb, bb, candw), a)
            a1 = VE.do(lambda e: e.tensor_scalar(hi16.bitcast(U32), cidx.bitcast(U32), 4, None,
                                                 ALU.logical_shift_right), a)
            a2 = VE.do(lambda e: e.tensor_scalar(lo16.bitcast(U32), cidx.bitcast(U32), 15, None,
                                                 ALU.bitwise_and), a)
            fT = []
            for s_, ix in ((0, hi16), (1, lo16)):
                f = VE.do(lambda e: e.tensor_copy(fi, ix.bitcast(U32)), a1, a2, t_prev)
                bgv = big.rearrange("p (h k j) -> p h k j", h=8, k=16)
                o = VE.do(lambda e: e.tensor_tensor(
                    big.rearrange("p (m j) -> p m j", j=16), fi.unsqueeze(2).broadcast_to([P, 128, 16]),
                    iota[:, 0:16].unsqueeze(1).broadcast_to([P, 128, 16]), ALU.is_equal), f, tk_c)
                o = VE.do(lambda e: e.tensor_tensor(
                    bgv, bgv, i16fv[:, s_, qt, :, :].unsqueeze(2).broadcast_to([P, 8, 16, 16]), ALU.mult), o, ti)
                o = VE.do(lambda e: e.tensor_reduce(fg, big.rearrange("p (m j) -> p m j", j=16), AXX, ALU.add), o,
                          t_prev)
                b, free = bank()
                tt = PE.do(lambda e: e.transpose(b[:, 0:P], fg, ident), o, *free)
                dst = (iaT, ibT)[s_][:, qt * P:(qt + 1) * P]
                t_prev = SC.do(lambda e: e.activation(dst, b[:, 0:P], ACT.Copy), tt)
                banks.give(b, t_prev)
                VE.wait(t_prev)
            bv = best.rearrange("p (h k) -> p h k", h=8)
            a = VE.do(lambda e: e.tensor_copy(tot[:, 0:8], bv[:, :, 0]), a)
            a = VE.do(lambda e: e.tensor_tensor(bv, bv, tot[:, 0:8].unsqueeze(2).broadcast_to([P, 8, 16]),
                                                ALU.subtract), a)
            a = SC.do(lambda e: e.activation(fi, best, ACT.Exp), a, t_prev)
            fv = fi.rearrange("p (h k) -> p h k", h=8)
            a = VE.do(lambda e: e.tensor_reduce(tot[:, 0:8], fv, AXX, ALU.add), a)
            a = VE.do(lambda e: e.reciprocal(tot[:, 8:16], tot[:, 0:8]), a)
            a = VE.do(lambda e: e.tensor_tensor(fg.rearrange("p (h k) -> p h k", h=8), fv,
                                                tot[:, 8:16].unsqueeze(2).broadcast_to([P, 8, 16]), ALU.mult), a)
            b, free = bank()
            tt = PE.do(lambda e: e.transpose(b[:, 0:P], fg, ident), a, *free)
            dst = gT[:, qt * P:(qt + 1) * P]
            t_prev = SC.do(lambda e: e.activation(dst, b[:, 0:P], ACT.Copy), tt)
            banks.give(b, t_prev)
        t_idx = t_prev

        loc = phase()
        loc.at = keep
        AB = Slots([loc(2048) for _ in range(AHEAD)])

        def hidden(g):
            ab, af = AB.take()
            for j in range(2):
                it = take("U")
                for bb in range(2):
                    b, free = bank()
                    PE.wait(*free, *it[3])
                    for k in range(8):
                        o = bb * 1024 + k * P
                        xh, xl = X(k)
                        mm(b, it[1][:, o:o + P], xh, k == 0, False)
                        mm(b, it[1][:, o:o + P], xl, False, False)
                        tok = mm(b, it[2][:, o:o + P], xh, False, k == 7, sig=k == 7)
                    q = 2 * j + bb
                    t = SC.do(lambda e: e.activation(ab[:, q * T:(q + 1) * T], b, ACT.Gelu),
                              tok, *af)
                    banks.give(b, t)
                done(it, tok)
            return ab, t

        hid = [hidden(g) for g in range(AHEAD)]
        gd = nc.dram_tensor("gates", (T // CT, P, P * CT), F32).ap()
        stages = Slots([loc(P * CT), loc(P * CT)])
        stage_sem = [sem("s_gw0"), sem("s_gw1")]
        ohA = Slots([loc(P) for _ in range(4)])
        ohB = Slots([loc(P) for _ in range(4)])
        for ch in range(T // CT):
            st, sf = stages.take()
            stv = st.rearrange("p (b t) -> p b t", t=CT)
            for t0 in range(0, CT, 4):
                b, free = bank()
                PE.wait(*free)
                for j in range(4):
                    t = ch * CT + t0 + j
                    oa, fa = ohA.take()
                    ob_, fb = ohB.take()
                    VE.do(lambda e: e.tensor_scalar(oa, iota, iaT[:, t:t + 1], None, ALU.is_equal),
                          t_idx, *fa)
                    to = VE.do(lambda e: e.tensor_scalar(ob_, iota, ibT[:, t:t + 1], gT[:, t:t + 1],
                                                                       ALU.is_equal, ALU.mult), t_idx, *fb)
                    tok = mm(b[:, j * P:(j + 1) * P], oa, ob_, j == 0, False, to, sig=True)
                    ohA.give(oa, tok)
                    ohB.give(ob_, tok)
                te = SC.do(lambda e: e.activation(
                    stv[:, :, t0:t0 + 4], b.rearrange("p (t b) -> p b t", t=4), ACT.Copy), tok, *sf)
                banks.give(b, te)
            SC.wait(te)
            SC.dma(gd[ch], st, stage_sem[ch % 2])
            stages.give(st, (stage_sem[ch % 2], 16 * (ch // 2 + 1)))
        written = [(s, 16 * (T // CT // 2)) for s in stage_sem]

        phase()
        gring = Slots([(stage_buf, i) for i, (stage_buf, _) in enumerate(stages.free)])
        s_gr = [sem("s_gr0"), sem("s_gr1")]
        gn = [0, 0]
        gdv = gd.rearrange("c a (g x) -> g a c x", x=4 * CT)

        def fetch(g):
            (buf, i), gf = gring.take()
            gn[i] += 16
            SP.wait(*written, *gf)
            SP.dma(buf.rearrange("p (c x) -> p c x", c=T // CT), gdv[g], s_gr[i])
            return buf, i, (s_gr[i], gn[i])

        AG = Slots([yhl[:, 0:4096], yhl[:, 4096:8192]])

        def gated(g, gbuf, ab):
            buf, i, tok = gbuf
            ap, t_h = ab
            av = ap.rearrange("p (b c t) -> p b c t", b=4, t=CT)
            gv = buf.rearrange("p (c b t) -> p b c t", b=4, t=CT)
            ag, af = AG.take()
            ths = []
            for q in range(4):
                tm = VE.do(lambda e: e.tensor_tensor(av[:, q], av[:, q], gv[:, q], ALU.mult), tok, t_h)
                th, tl = split(ag[:, q * T:(q + 1) * T], ag[:, 2048 + q * T:2048 + (q + 1) * T],
                               ap[:, q * T:(q + 1) * T], tm, *af)
            gring.give((buf, i), tm)
            AB.give(ap, th, tl)
            return ag, (th, tl)

        gb = fetch(0)
        ag = gated(0, gb, hid.pop(0))
        gb = fetch(1)
        for g in range(NG):
            nxt = None
            if g + 1 < NG:
                nxt = gated(g + 1, gb, hid.pop(0))
                if g + 2 < NG:
                    gb = fetch(g + 2)
            for half in range(2):
                it = take("V")
                for m in range(4):
                    b, free = bank()
                    PE.wait(*free, *it[3], *ag[1])
                    for q in range(4):
                        o = q * 512 + m * P
                        ah, al = ag[0][:, q * T:(q + 1) * T], ag[0][:, 2048 + q * T:2048 + (q + 1) * T]
                        mm(b, it[1][:, o:o + P], ah, q == 0, False)
                        mm(b, it[1][:, o:o + P], al, False, False)
                        tok = mm(b, it[2][:, o:o + P], ah, False, q == 3, sig=q == 3)
                    d = half * 4 + m
                    t_x = VE.do(lambda e, b=b, d=d: e.scalar_tensor_tensor(x_at(d), b, AD(5, d), x_at(d),
                                                                           ALU.mult, ALU.add), tok)
                    banks.give(b, t_x)
                done(it, tok)
            AG.give(ag[0], tok)
            if g + AHEAD < NG:
                hid.append(hidden(g + AHEAD))
            ag = nxt

        loc = phase()
        rt, tmp = loc(T), loc(1024)
        tr = rstd(x_at, 8, 1024, rt, tmp)
        yo = loc(4096)
        for k in range(8):
            tk = VE.do(lambda e: e.scalar_tensor_tensor(x_at(k), x_at(k), V("final_norm_g_2", k), rt,
                                                             ALU.mult, ALU.mult), tr)
        s_out = sem("s_out")
        for qt in range(NT):
            for half in range(2):
                b, free = bank()
                PE.wait(*free, tk)
                for c in range(4):
                    k = 4 * half + c
                    tt = PE.do(lambda e: e.transpose(
                        b[:, c * P:(c + 1) * P], XT[:, k * T + qt * P:k * T + (qt + 1) * P], ident), sig=c == 3)
                t = evac(yo[:, qt * 1024 + half * 512:qt * 1024 + (half + 1) * 512], b, tt, eng=VE if half else None)
                SP.wait(t)
            SP.dma(out[0, qt * P:(qt + 1) * P, :],
                                                       yo[:, qt * 1024:(qt + 1) * 1024], s_out)
        SP.wait((s_out, 64))
        assert state["use"] == len(items)

        block = ctx.enter_context(nc.Block())

        @block.sync
        def _(e):
            SP.run()

        @block.scalar
        def _(e):
            SC.run()

        @block.vector
        def _(e):
            VE.run()

        @block.gpsimd
        def _(e):
            GP.run()

        @block.tensor
        def _(e):
            PE.run()


_INS = ["xT", "consts", "vecs", "rope", "gate_up", "skT", "l0_in", "l0_uq", "l0_ukv", "l0_out", "w_ada", "w_small",
        "w_gla", "w_za", "w_ba", "w_dkv", "w_iq", "w_dq", "w_ukuv", "w_zb", "w_bb", "w_out", "w_pq", "U", "V"]


def layouts(inputs):
    a = {k: np.asarray(v) for k, v in inputs.items()}

    def cols(w, chunks):
        w = np.concatenate([w[:, c] for c in chunks], axis=1)
        n = w.shape[1] // 256
        return w.reshape(8, P, n, 256).transpose(2, 1, 0, 3).reshape(n, P, 2048)

    def sl(a0, n):
        return [slice(a0 + i * P, a0 + (i + 1) * P) for i in range(n // P)]

    r = {}
    r["xT"] = a["x"][0].T
    vecs = []
    for name in VEC:
        vecs.append(a[name].reshape(-1, P).T)
    r["vecs"] = np.concatenate(vecs, axis=1)
    f = np.float32
    i = np.arange(P)
    consts = np.zeros((P, NCONST), f)
    consts[:, 0:128] = np.eye(P)
    consts[:, 128:256] = 1.0
    consts[:, 256:384] = i[None, :]
    consts[:, 384:896] = i[:, None] + 384 - np.arange(512)[None, :]
    consts[:, 896:1408] = (np.arange(512) % 64 != 0)[None, :]
    r["consts"] = consts
    inv = (1.0 / (f(10000.0) ** (np.arange(0, 64, 2, dtype=f) / f(64)))).astype(f)
    ang = (np.arange(T, dtype=f)[:, None] * inv[None, :]).astype(f)
    cos, sin = np.cos(ang).astype(f).T, np.sin(ang).astype(f).T
    r["rope"] = np.concatenate([np.concatenate([cos] * 4), np.concatenate([-sin, sin] * 2)], axis=1)
    w = a["l0_w_in"]
    pe = list(range(640, 704))
    sw = list(range(672, 704)) + list(range(640, 672))
    chunks = sl(0, 640) + [pe + pe, sw + sw] + sl(704, 1024)
    r["l0_in"] = cols(w, chunks + chunks[-1:])
    uq = a["l0_w_uq"].reshape(3, P, 4, 2, 192)
    sw2 = np.concatenate([uq[..., 160:192], uq[..., 128:160]], axis=-1)
    uq = np.concatenate([uq[..., 0:128].reshape(3, P, 4, 256), uq[..., 128:192].reshape(3, P, 4, 128),
                         sw2.reshape(3, P, 4, 128)], axis=-1)
    r["l0_uq"] = uq.transpose(2, 1, 0, 3).reshape(4, P, 1536)
    ukv = a["l0_w_ukv"].reshape(2, P, 4, 2, 2, 128)
    r["l0_ukv"] = ukv.transpose(2, 1, 0, 4, 3, 5).reshape(4, P, 1024)
    r["l0_out"] = cols(a["l0_w_out"], sl(0, 1024))
    r["w_ada"] = cols(a["w_ada_2"][0], sl(0, 6144))
    w = a["w_in_2"][0]
    gq, gk, gv, gr, glow, dq, dkv, iq, ik, iw, za, zb = (
        int(x) for x in np.cumsum([0, 512, 512, 1024, 1024, 16, 1024, 256, 512, 64, 8, 1024]))
    iks = list(range(ik, ik + 64))
    r["w_small"] = cols(w, [iks + iks, list(range(glow, glow + 16)) + list(range(iw, iw + 8)) + [0] * 104])[0]
    ch = []
    for h in range(4):
        ch += [slice(gq + h * P, gq + (h + 1) * P), slice(gk + h * P, gk + (h + 1) * P)]
        ch += sl(gv + h * 256, 256) + sl(gr + h * 256, 256)
    r["w_gla"] = cols(w, ch)
    for name, at, n in (("w_za", za, 1024), ("w_zb", zb, 1024), ("w_dkv", dkv, 256), ("w_iq", iq, 512),
                        ("w_dq", dq, 1024)):
        r[name] = cols(w, sl(at, n))
    r["w_ba"], r["w_bb"], r["w_out"] = (cols(a[n][0], sl(0, 1024)) for n in ("w_branch_a_2", "w_branch_b_2", "w_out_2"))
    r["w_pq"] = cols(a["peer_w_q_2"][0], sl(0, 2048))
    uk = a["dsa_w_uk_2"][0].transpose(0, 2, 1).reshape(2, 4, 2, P, 128)
    uv = a["dsa_w_uv_2"][0].reshape(2, 4, 2, P, 128)
    r["w_ukuv"] = np.concatenate([uk, uv], axis=-1).transpose(0, 3, 1, 2, 4).reshape(2, P, 2048)
    r["gate_up"] = a["gla_w_gate_up_2"][0]
    r["skT"] = np.concatenate([a["peer_sub_keys_1_2"][0].T, a["peer_sub_keys_2_2"][0].T], axis=1)
    r["U"] = a["peer_u_2"][0].reshape(P, 64, 2, 8, P).transpose(1, 4, 2, 3, 0).reshape(64, P, 2048)
    r["V"] = a["peer_v_2"][0].reshape(P, 32, 4, 2, 512).transpose(1, 3, 0, 2, 4).reshape(64, P, 2048)
    return {k: np.ascontiguousarray(v) for k, v in r.items()}


def kernel(**inputs):
    import concourse.bacc as bacc
    from concourse.bass_utils import run_bass_kernel_spmd as run

    nc = bacc.Bacc("TRN2", target_bir_lowering=False, num_devices=1)
    arrays = layouts(inputs)
    args = {k: nc.dram_tensor("in_" + k, v.shape, F32, kind="ExternalInput").ap() for k, v in arrays.items()}
    out = nc.dram_tensor("out_0", (1, T, 1024), F32, kind="ExternalOutput").ap()
    build(nc, args, out)
    r = run(nc, [{"in_" + k: v for k, v in arrays.items()}], core_ids=[0])
    return r.results[0]["out_0"]
```

```python
from contextlib import ExitStack

import numpy as np

import concourse.bass as bass
from concourse import mybir

F32 = mybir.dt.float32
F32R = mybir.dt.float32r
U32 = mybir.dt.uint32
ALU = mybir.AluOpType
ACT = mybir.ActivationFunctionType
AXX = mybir.AxisListType.X

P = 128
T = 512
NT = 4
EPS = 1e-6
ITEM = 2048
GLA_H = 4
H = 8
NEG = -1e30
FILL = -1e38
TAKEN = -3e38
CT = 16
NR = 3
ADA_L0 = (1, 1, 1, 1, 1, 1, 1, 1)
ADA_GAP = 12
GLA_STEPS = [("project", 0), ("project", 1), ("mix", 0), ("project", 2), ("mix", 1), ("project", 3), ("mix", 2),
             ("mix", 3)]

VEC = {}
_at = 0
for _name, _n in (("l0_norm", 8), ("l0_q_norm", 3), ("l0_kv_norm", 2), ("final_norm", 8), ("c_2", 8),
                  ("b_ada_2", 48), ("norm1_g_2", 8), ("gla_b_gate_2", 4), ("gla_norm_g_2", 8),
                  ("dsa_kv_norm_g_2", 2), ("norm2_g_2", 8), ("final_norm_g_2", 8)):
    VEC[_name] = (_at, _n)
    _at += _n
NVEC = _at
CONST = {"ident": (0, 128), "ones": (128, 128), "iota": (256, 128), "rel": (384, 512), "reset": (896, 512)}
NCONST = 1408


class Calls:

    def __init__(self, **methods):
        self.methods = methods

    def hold(self, name, args, kwargs):
        method = self.methods[name]
        return lambda: method(*args, **kwargs)

    def activation(self, *args, **kwargs):
        return self.hold("activation", args, kwargs)

    def tensor_copy(self, *args, **kwargs):
        return self.hold("tensor_copy", args, kwargs)

    def tensor_tensor(self, *args, **kwargs):
        return self.hold("tensor_tensor", args, kwargs)

    def tensor_scalar(self, *args, **kwargs):
        return self.hold("tensor_scalar", args, kwargs)

    def scalar_tensor_tensor(self, *args, **kwargs):
        return self.hold("scalar_tensor_tensor", args, kwargs)

    def tensor_tensor_scan(self, *args, **kwargs):
        return self.hold("tensor_tensor_scan", args, kwargs)

    def tensor_reduce(self, *args, **kwargs):
        return self.hold("tensor_reduce", args, kwargs)

    def reciprocal(self, *args, **kwargs):
        return self.hold("reciprocal", args, kwargs)

    def max(self, *args, **kwargs):
        return self.hold("max", args, kwargs)

    def max_index(self, *args, **kwargs):
        return self.hold("max_index", args, kwargs)

    def match_replace(self, *args, **kwargs):
        return self.hold("match_replace", args, kwargs)

    def memset(self, *args, **kwargs):
        return self.hold("memset", args, kwargs)

    def affine_select(self, *args, **kwargs):
        return self.hold("affine_select", args, kwargs)

    def matmul(self, *args, **kwargs):
        return self.hold("matmul", args, kwargs)

    def transpose(self, *args, **kwargs):
        return self.hold("transpose", args, kwargs)

    def dma_start(self, *args, **kwargs):
        return self.hold("dma_start", args, kwargs)

    def wait_ge(self, *args, **kwargs):
        return self.hold("wait_ge", args, kwargs)


class Engine:

    def __init__(self, sem, **methods):
        self.sem, self.n, self.seen, self.ops, self.open = sem, 0, {}, [], False
        self.calls = Calls(**methods)

    def wait(self, *tokens):
        for tok in tokens:
            if tok is None:
                continue
            sem, value = tok
            if self.seen.get(sem.name, 0) < value:
                self.seen[sem.name] = value
                self.ops.append((self.calls.wait_ge(sem, value), None, 0))

    def do(self, fn, *tokens, sig=True):
        self.wait(*tokens)
        if sig:
            self.n += 1
        self.ops.append((fn(self.calls), self.sem if sig else None, 1))
        self.open = not sig
        return (self.sem, self.n)

    def dma(self, dst, src, sem):
        self.ops.append((self.calls.dma_start(dst, src), sem, 16))

    def now(self):
        assert not self.open
        return (self.sem, self.n) if self.n else None

    def run(self):
        for call, sem, by in self.ops:
            instruction = call()
            if sem is not None:
                instruction.then_inc(sem, by)


class Slots:

    def __init__(self, aps):
        self.free = [(ap, ()) for ap in aps]

    def take(self):
        return self.free.pop(0)

    def give(self, ap, *tokens):
        self.free.append((ap, tokens))


def build(nc, ins, out):
    ctx = ExitStack()
    with ctx:
        def sb(name, n, dt=F32):
            return ctx.enter_context(nc.sbuf_tensor(name, [P, n], dt))

        def sem(name):
            return ctx.enter_context(nc.semaphore(name))

        PE = Engine(sem("s_pe"), matmul=nc.tensor.matmul, transpose=nc.tensor.transpose, wait_ge=nc.tensor.wait_ge)
        SC = Engine(sem("s_act"), activation=nc.scalar.activation, dma_start=nc.scalar.dma_start,
                    wait_ge=nc.scalar.wait_ge)
        v = nc.vector
        VE = Engine(sem("s_dve"), tensor_copy=v.tensor_copy, tensor_tensor=v.tensor_tensor,
                    tensor_scalar=v.tensor_scalar, scalar_tensor_tensor=v.scalar_tensor_tensor,
                    tensor_tensor_scan=v.tensor_tensor_scan, tensor_reduce=v.tensor_reduce,
                    reciprocal=v.reciprocal, max=v.max, max_index=v.max_index, match_replace=v.match_replace,
                    wait_ge=v.wait_ge)
        GP = Engine(sem("s_pool"), memset=nc.gpsimd.memset, affine_select=nc.gpsimd.affine_select,
                    wait_ge=nc.gpsimd.wait_ge)
        SP = Engine(sem("s_sp"), dma_start=nc.sync.dma_start, wait_ge=nc.sync.wait_ge)

        raw = sb("raw", NR * ITEM)
        whl = sb("whl", 4 * ITEM, F32R)
        xhl = sb("xhl", 8192, F32R)
        yhl = sb("yhl", 8192, F32R)
        XT = sb("XT", 4096)
        cst = sb("cst", NCONST)
        vec = sb("vec", NVEC)
        ada = sb("ada", 48)
        mod = sb("mod", 16)
        sc8 = sb("sc8", 8)
        skT = sb("skT", 256)
        LN = 16448
        L = sb("L", LN)
        banks = Slots([ctx.enter_context(nc.psum_tensor(f"bank{i}", [P, 512], F32))[:, :] for i in range(8)])

        def C(name):
            o, n = CONST[name]
            return cst[:, o:o + n]

        def V(name, j):
            o, _ = VEC[name]
            return vec[:, o + j:o + j + 1]

        def F(ap):
            return ap.bitcast(F32)

        ident, ones, iota = C("ident"), C("ones"), C("iota")

        class Local:
            def __init__(self):
                self.at = 0

            def __call__(self, n):
                ap = L[:, self.at:self.at + n]
                self.at += n
                assert self.at <= LN, self.at
                return ap

        def phase():
            toks = [e.now() for e in (PE, SC, VE, GP)]
            for e in (PE, SC, VE, GP):
                e.wait(*toks)
            return Local()

        s_in = [sem(f"s_in{i}") for i in range(6)]

        def load(i, dst, src, *tokens):
            SP.wait(*tokens)
            SP.dma(dst, src, s_in[i])

        load(0, XT[:, :].rearrange("p (k t) -> p k t", k=8), ins["xT"].rearrange("(k p) t -> p k t", p=P))
        load(1, cst[:, 0:384], ins["consts"][:, 0:384])
        load(2, vec[:, :], ins["vecs"])
        tk_x, tk_c, tk_v = (s_in[0], 16), (s_in[1], 16), (s_in[2], 16)

        items = []
        for i in range(8):
            items.append(("l0_in", ins["l0_in"][i], ITEM, True))
        def ada_items(n):
            for _ in range(n):
                items.append(("ada", ins["w_ada"][n_ada[0]], ITEM, False))
                n_ada[0] += 1

        n_ada = [0]
        for h in range(H):
            if h % 2 == 0:
                items.append(("uq", ins["l0_uq"][h // 2], 1536, True))
                items.append(("ukv", ins["l0_ukv"][h // 2], 1024, True))
            ada_items(ADA_L0[h])
        for i in range(4):
            items.append(("l0_out", ins["l0_out"][i], ITEM, True))
        ada_items(ADA_GAP)
        items.append(("small", ins["w_small"], ITEM, True))
        for step in GLA_STEPS:
            for j in (range(2) if step[0] == "project" else (2,)):
                items.append(("gla", ins["w_gla"][3 * step[1] + j], ITEM, True))
        for i in range(2):
            items.append(("iq", ins["w_iq"][i], ITEM, True))
        items.append(("dkv", ins["w_dkv"][0], ITEM, True))
        for i in range(4):
            items.append(("za", ins["w_za"][i], ITEM, True))
            items.append(("ba", ins["w_ba"][i], ITEM, True))
        for i in range(4):
            if i % 2 == 0:
                items.append(("ukuv", ins["w_ukuv"][i // 2], ITEM, False))
            items.append(("dq", ins["w_dq"][i], ITEM, True))
        for name in ("zb", "bb", "w_out"):
            for i in range(4):
                items.append((name, ins[name if name == "w_out" else "w_" + name][i], ITEM, True))
        ada_items(24 - n_ada[0])
        for i in range(8):
            items.append(("pq", ins["w_pq"][i], ITEM, True))
        NG = 32
        items += [("U", ins["U"][i], ITEM, True) for i in range(2 * NG)]
        items += [("V", ins["V"][i], ITEM, True) for i in range(2 * NG)]

        s_raw = [sem(f"s_raw{i}") for i in range(NR)]
        raw_free = [()] * NR
        landed = {}
        state = {"dma": 0, "conv": 0, "use": 0}

        def pump():
            while state["dma"] < len(items) and raw_free[state["dma"] % NR] is not None:
                i = state["dma"]
                r = i % NR
                name, src, n, _ = items[i]
                SP.wait(*raw_free[r])
                raw_free[r] = None
                SP.dma(raw[:, r * ITEM:r * ITEM + n], src, s_raw[r])
                landed[i] = (s_raw[r], 16 * (i // NR + 1))
                state["dma"] += 1

        whl_free = [(), ()]
        ready = {}
        nconv = [0]

        def convert():
            i = state["conv"]
            if i >= len(items):
                return
            name, src, n, conv = items[i]
            if i not in landed:
                return
            r = i % NR
            src_ap = raw[:, r * ITEM:r * ITEM + n]
            if conv:
                w = nconv[0] % 2
                if whl_free[w] is None:
                    return
                nconv[0] += 1
                hi = whl[:, 2 * w * ITEM:2 * w * ITEM + n]
                lo = whl[:, (2 * w + 1) * ITEM:(2 * w + 1) * ITEM + n]
                h = n // 2
                th = None
                for a, b in ((0, h), (h, n)):
                    th = SC.do(lambda e: e.activation(hi[:, a:b], src_ap[:, a:b], ACT.Copy),
                               landed[i], *whl_free[w])
                    tl = VE.do(lambda e: e.tensor_tensor(lo[:, a:b], src_ap[:, a:b], F(hi[:, a:b]),
                                                                   ALU.subtract),
                               landed[i], th, *whl_free[w])
                whl_free[w] = None
                raw_free[r] = (th, tl)
                ready[i] = (hi, lo, (th, tl), w)
            else:
                ready[i] = (src_ap, None, (landed[i],), r)
            state["conv"] += 1
            pump()

        def take(name):
            i = state["use"]
            assert items[i][0] == name, (items[i][0], name)
            while state["conv"] <= min(i + 1, len(items) - 1):
                before = state["conv"]
                convert()
                if state["conv"] == before:
                    break
            assert i in ready
            state["use"] += 1
            return (i,) + ready.pop(i)

        def done(item, *tokens):
            i, _, _, _, where = item
            if items[i][3]:
                whl_free[where] = tokens
            else:
                raw_free[where] = tokens
                pump()

        pump()

        def mm(bank, lhsT, rhs, start, stop, *tokens, sig=False):
            return PE.do(lambda e: e.matmul(bank, lhsT, rhs, start=start, stop=stop, skip_group_check=True),
                         *tokens, sig=sig)

        def mm3(o, a, b, nk, *tokens):
            PE.wait(*tokens)
            for k in range(nk):
                (ah, al), (bh, bl) = a(k), b(k)
                mm(o, ah, bh, k == 0, False)
                mm(o, ah, bl, False, False)
                tok = mm(o, al, bh, False, k == nk - 1, sig=k == nk - 1)
            return tok

        def split(hi, lo, src, tok, *waits):
            th = SC.do(lambda e: e.activation(hi, src, ACT.Copy), tok, *waits)
            tl = VE.do(lambda e: e.tensor_tensor(lo, src, F(hi), ALU.subtract), tok, th, *waits)
            return th, tl

        def hl(base, n):
            def at(k, a=0, b=T):
                return base[:, k * T + a:k * T + b], base[:, n + k * T + a:n + k * T + b]
            return at

        X = hl(xhl, 4096)
        Y = hl(yhl, 4096)

        def wchunk(item, nk, width, c):
            _, hi, lo, _, _ = item
            def at(k):
                o = k * width + c * P
                return hi[:, o:o + P], lo[:, o:o + P]
            return at

        def bank():
            return banks.take()

        def projT(item, c, src, nk=8, width=256, *tokens):
            b, free = bank()
            tok = mm3(b, wchunk(item, nk, width, c), lambda k: src(k), nk, *item[3], *free, *tokens)
            return b, tok

        def rstd(sq_src, nk, width, r, sq, *tokens):
            b, free = bank()
            PE.wait(*free)
            sqs = Slots([sq[:, 0:T], sq[:, T:2 * T]])
            for k in range(nk):
                s, fr = sqs.take()
                src = sq_src(k)
                t = SC.do(lambda e, s=s, src=src: e.activation(s, src, ACT.Square), *tokens, *fr)
                tp = mm(b, ones, s, k == 0, k == nk - 1, t, tk_c, sig=True)
                sqs.give(s, tp)
            t0 = VE.do(lambda e: e.tensor_scalar(r, b, 1.0 / width, EPS, ALU.mult, ALU.add), tp, *tokens)
            banks.give(b, t0)
            t = SC.do(lambda e: e.activation(r, r, ACT.Sqrt), t0)
            return VE.do(lambda e: e.reciprocal(r, r), t)

        loc = Local()
        cq, ckv, kpe, gate = loc(1536), loc(1024), loc(512), loc(4096)
        rt, tmp = loc(T), loc(1024)
        rope = cst[:, 384:1408]
        load(3, rope, ins["rope"])
        tk_r = (s_in[3], 16)
        cosT, sinT = rope[:, 0:T], rope[:, T:2 * T]

        def x_at(k):
            return XT[:, k * T:(k + 1) * T]

        def norm_into(dst, src, nk, r, tr, gain, tmps, *tokens):
            toks = []
            tm = Slots([tmps[:, 0:T], tmps[:, T:2 * T]])
            for k in range(nk):
                t_, fr = tm.take()
                hi, lo = dst(k)
                a = VE.do(lambda e: e.scalar_tensor_tensor(t_, src(k), gain(k), r, ALU.mult, ALU.mult),
                          tr, tk_v, *fr, *tokens)
                th, tl = split(hi, lo, t_, a)
                tm.give(t_, th, tl)
                toks = [th, tl]
            return toks

        tr = rstd(x_at, 8, 1024, rt, tmp, tk_x)
        tX = norm_into(X, x_at, 8, rt, tr, lambda k: V("l0_norm", k), tmp, tr)

        it = None
        t_l = None
        for ch in range(15):
            if ch % 2 == 0:
                it = take("l0_in")
            b, tok = projT(it, ch % 2, X, 8, 256, *tX)
            if ch % 2 == 1 or ch == 14:
                done(it, tok)
            if ch < 5:
                dst = cq[:, ch * T:(ch + 1) * T] if ch < 3 else ckv[:, (ch - 3) * T:(ch - 2) * T]
                t = SC.do(lambda e, d=dst, b=b: e.activation(d, b, ACT.Copy), tok)
                banks.give(b, t)
                t_l = t
            elif ch == 5:
                t_k = VE.do(lambda e: e.tensor_tensor(kpe, b, cosT, ALU.mult), tok, tk_r)
                banks.give(b, t_k)
            elif ch == 6:
                t2 = VE.do(lambda e: e.tensor_tensor(tmp[:, 0:T], b, sinT, ALU.mult), tok, tk_r, *tX)
                banks.give(b, t2)
                t_k = VE.do(lambda e: e.tensor_tensor(kpe, kpe, tmp[:, 0:T], ALU.add), t2, t_k)
            else:
                g = gate[:, (ch - 7) * T:(ch - 6) * T]
                t = SC.do(lambda e: e.activation(g, b, ACT.Silu), tok)
                banks.give(b, t)
        last_pe = tok
        CQ = hl(xhl, 2560)
        CK = lambda k, a=0, b_=T: CQ(k + 3, a, b_)
        tr = rstd(lambda k: cq[:, k * T:(k + 1) * T], 3, 384, rt, tmp, t_l, t_k)
        t1 = norm_into(CQ, lambda k: cq[:, k * T:(k + 1) * T], 3, rt, tr, lambda k: V("l0_q_norm", k), tmp, tr, last_pe)
        tr = rstd(lambda k: ckv[:, k * T:(k + 1) * T], 2, 256, rt, tmp, *t1)
        t2 = norm_into(CK, lambda k: ckv[:, k * T:(k + 1) * T], 2, rt, tr, lambda k: V("l0_kv_norm", k), tmp, tr)

        silc = sc8[:, 0:8]
        o_, n_ = VEC["c_2"]
        t_c = SC.do(lambda e: e.activation(silc, vec[:, o_:o_ + 8], ACT.Silu), tk_v)

        class Ada:

            def __init__(self):
                self.next = 0

            def open(self):
                self.b, free = bank()
                PE.wait(*free, t_c)
                self.first = self.next

            def step(self, n):
                for _ in range(n):
                    it = take("ada")
                    for c in range(2):
                        col = 2 * self.next + c
                        for k in range(8):
                            tok = mm(self.b[:, col:col + 1], it[1][:, k * 256 + c * P:k * 256 + (c + 1) * P],
                                     silc[:, k:k + 1], c == 0 and k == 0 and self.next == self.first, False, *it[3],
                                     sig=k == 7)
                    done(it, tok)
                    self.next += 1
                    self.tok = tok

            def close(self):
                a, b_ = 2 * self.first, 2 * self.next
                o, _ = VEC["b_ada_2"]
                t = VE.do(lambda e: e.tensor_tensor(ada[:, a:b_], self.b[:, a:b_], vec[:, o + a:o + b_], ALU.add),
                          self.tok, tk_v)
                banks.give(self.b, t)
                return t

        adas = Ada()
        adas.open()

        class Attn:

            def __init__(self, loc, causal, scale):
                self.causal, self.scale = causal, scale
                self.P = [Slots([loc((qt + 1) * P if causal else T) for _ in range(2)]) for qt in range(NT)]
                self.PT = Slots([loc(4 * T)])
                self.st = Slots([loc(4) for _ in range(8)])

            def scores(self, parts, bias=None, *tokens):
                rows = []
                for qt in range(NT):
                    n = (qt + 1) * P if self.causal else T
                    b, free = bank()
                    PE.wait(*free, *tokens)
                    for j, (q, k) in enumerate(parts):
                        ts = mm(b[:, 0:n], q(qt * P, (qt + 1) * P), k(n), j == 0, j == len(parts) - 1,
                                sig=j == len(parts) - 1)
                    p, pf = self.P[qt].take()
                    st, sf = self.st.take()
                    pn = p[:, 0:n]
                    if bias is None:
                        tm = VE.do(lambda e: e.tensor_reduce(st[:, 0:1], b, AXX, ALU.max, negate=True),
                                   ts, *sf)
                        tm = VE.do(lambda e: e.tensor_scalar(st[:, 1:2], st[:, 0:1], self.scale, None,
                                                                    ALU.mult), tm)
                        te = SC.do(lambda e: e.activation(
                            pn, b, ACT.Exp, bias=st[:, 1:2], scale=self.scale, accum_out=st[:, 2:3]), tm, *pf)
                        banks.give(b, te)
                    else:
                        bb, tb, bfree = bias(qt)
                        t0 = VE.do(lambda e: e.scalar_tensor_tensor(
                            pn, b[:, 0:n], self.scale, bb, ALU.mult, ALU.add), ts, tb, *pf)
                        banks.give(b, t0)
                        bfree(t0)
                        tm = VE.do(lambda e: e.tensor_reduce(st[:, 1:2], pn, AXX, ALU.max,
                                                                           negate=True), t0, *sf)
                        te = SC.do(lambda e: e.activation(
                            pn, pn, ACT.Exp, bias=st[:, 1:2], scale=1.0, accum_out=st[:, 2:3]), tm)
                    ti = VE.do(lambda e: e.reciprocal(st[:, 3:4], st[:, 2:3]), te)
                    tn = VE.do(lambda e: e.tensor_scalar(pn, pn, st[:, 3:4], None, ALU.mult), ti)
                    self.st.give(st, tn)
                    rows.append((p, tn))
                return rows

            def values(self, rows, v, *tokens):
                pt, ptf = self.PT.take()
                ptv = pt.rearrange("p (c q) -> p c q", c=4)
                toks = []
                for qt in range(NT):
                    p, tn = rows[qt]
                    nc_ = qt + 1 if self.causal else NT
                    b, free = bank()
                    PE.wait(*free)
                    for c in range(nc_):
                        tt = PE.do(lambda e: e.transpose(b[:, c * P:(c + 1) * P],
                                                                        p[:, c * P:(c + 1) * P], ident),
                                   tn, tk_c, sig=c == nc_ - 1)
                    self.P[qt].give(p, tt)
                    cp = lambda e: e.tensor_copy(
                        ptv[:, 0:nc_, qt * P:(qt + 1) * P], b[:, 0:nc_ * P].rearrange("p (c q) -> p c q", c=nc_))
                    ca = lambda e: e.activation(
                        ptv[:, 0:nc_, qt * P:(qt + 1) * P], b[:, 0:nc_ * P].rearrange("p (c q) -> p c q", c=nc_),
                        ACT.Copy)
                    tc = VE.do(cp, tt, *ptf) if qt % 2 else SC.do(ca, tt, *ptf)
                    banks.give(b, tc)
                    toks.append(tc)
                o, free = bank()
                PE.wait(*free, *toks, *tokens)
                for c in range(4):
                    a = c * P if self.causal else 0
                    to = mm(o[:, a:T], v(c), ptv[:, c, a:T], c == 0, c == 3, sig=c == 3)
                self.PT.give(pt, to)
                return o, to

        loc = phase()
        loc(2560)
        kpe_keep = loc(512)
        gate_keep = loc(4096)
        qn = Slots([L[:, 0:1024]])
        kn = Slots([L[:, 1024:2048]])
        qp = Slots([L[:, 2048:2560]])
        rtmp, og = loc(T), loc(T)
        vv = Slots([loc(1024), loc(1024)])
        attn = Attn(loc, False, (128 + 64) ** -0.5)

        def evac(dst, b, tok, *waits, eng=None):
            if eng is VE:
                t = VE.do(lambda e: e.tensor_copy(dst, b), tok, *waits)
            else:
                t = SC.do(lambda e: e.activation(dst, b, ACT.Copy), tok, *waits)
            banks.give(b, t)
            return t

        og_free = [()]

        def finish(hd, rows, vb, tv):
            j = hd % 2
            o, to = attn.values(rows, lambda c: vb[:, c * 256 + j * P:c * 256 + (j + 1) * P], tv)
            if j == 1:
                vv.give(vb, to)
            t = VE.do(lambda e: e.tensor_tensor(og, o, gate_keep[:, hd * T:(hd + 1) * T], ALU.mult), to, *og_free[0])
            banks.give(o, t)
            og_free[0] = split(*Y(hd), og, t)
            return og_free[0]

        before = None
        for hd in range(H):
            j, o64 = hd % 2, 64 * (hd % 2)
            if j == 0:
                it = take("uq")
                qb, qf = qn.take()
                for c in range(2):
                    b, tok = projT(it, c, CQ, 3, 512, *t1)
                    tq = evac(qb[:, c * T:(c + 1) * T], b, tok, *qf)
                b, tok = projT(it, 2, CQ, 3, 512)
                pb, pf = qp.take()
                ta = VE.do(lambda e: e.tensor_tensor(pb, b, cosT, ALU.mult), tok, *pf)
                banks.give(b, ta)
                b, tok = projT(it, 3, CQ, 3, 512)
                done(it, tok)
                tb = VE.do(lambda e: e.tensor_tensor(rtmp, b, sinT, ALU.mult), tok)
                banks.give(b, tb)
                tp = VE.do(lambda e: e.tensor_tensor(pb, pb, rtmp, ALU.add), ta, tb)
                it = take("ukv")
                kb, kf = kn.take()
                for c in range(2):
                    b, tok = projT(it, c, CK, 2, 512, *t2)
                    tkk = evac(kb[:, c * T:(c + 1) * T], b, tok, *kf)
                vb, vf = vv.take()
                for pair in range(2):
                    b, free = bank()
                    PE.wait(*free)
                    _, hi, lo, _, _ = it
                    for half in range(2):
                        qt = 2 * pair + half
                        for k in range(2):
                            a = CK(k, qt * P, (qt + 1) * P)
                            w = (hi[:, k * 512 + 256:k * 512 + 512], lo[:, k * 512 + 256:k * 512 + 512])
                            o = b[:, half * 256:(half + 1) * 256]
                            mm(o, a[0], w[0], half == 0 and k == 0, False)
                            mm(o, a[0], w[1], False, False)
                            tok = mm(o, a[1], w[0], False, k == 1 and half == 1, sig=k == 1 and half == 1)
                    tv = evac(vb[:, pair * 512:(pair + 1) * 512], b, tok, *vf, eng=VE)
                done(it, tok)
            rows = attn.scores([(lambda a, b: qb[:, j * T + a:j * T + b], lambda n: kb[:, j * T:j * T + n]),
                                (lambda a, b: pb[o64:o64 + 64, a:b], lambda n: kpe_keep[o64:o64 + 64, 0:n])],
                               None, tq, tp, tkk)
            if j == 1:
                for slot, ap in ((qn, qb), (kn, kb), (qp, pb)):
                    slot.give(ap, PE.now())
            if before:
                finish(*before)
            before = (hd, rows, vb, tv)
            adas.step(ADA_L0[hd])
        tO = finish(*before)
        t_ada = adas.close()

        def AD(part, k):
            return ada[:, part * 8 + k:part * 8 + k + 1]

        for i in range(4):
            it = take("l0_out")
            for c in range(2):
                b, tok = projT(it, c, Y, 8, 256, *tO)
                m = 2 * i + c
                t_x = VE.do(lambda e: e.tensor_tensor(x_at(m), x_at(m), b, ALU.add), tok)
                banks.give(b, t_x)
            done(it, tok)

        load(1, cst[:, 384:NCONST], ins["consts"][:, 384:NCONST], VE.now())
        tk_c2 = (s_in[1], 32)
        loc = phase()
        rt, tmp = loc(T), loc(1024)
        adas.open()
        adas.step(ADA_GAP // 3)
        tr = rstd(x_at, 8, 1024, rt, tmp, t_x)
        tk = None
        for k in range(8):
            tk = VE.do(lambda e: e.scalar_tensor_tensor(x_at(k), x_at(k), V("final_norm", k), rt,
                                                             ALU.mult, ALU.mult), tr)

        def modulated(scale_part, shift_part, gname, tk, tmp, rt, gap):
            g0, _ = VEC[gname]
            t_m = VE.do(lambda e: e.scalar_tensor_tensor(mod[:, 0:8], ada[:, scale_part * 8:scale_part * 8 + 8], 1.0,
                                                         vec[:, g0:g0 + 8], ALU.add, ALU.mult), t_ada, SC.now())
            gap()
            tr = rstd(x_at, 8, 1024, rt, tmp, tk)
            gap()
            tm = Slots([tmp[:, 0:T], tmp[:, T:2 * T]])
            for k in range(8):
                t_, fr = tm.take()
                hi, lo = X(k)
                a = VE.do(lambda e: e.tensor_tensor(t_, x_at(k), rt, ALU.mult), tr, *fr)
                a = SC.do(lambda e: e.activation(t_, t_, ACT.Identity, bias=AD(shift_part, k),
                                                             scale=mod[:, k:k + 1]), a, t_m)
                th, tl = split(hi, lo, t_, a)
                tm.give(t_, th, tl)
            return th, tl

        tX = modulated(1, 0, "norm1_g_2", tk, tmp, rt, lambda: adas.step(ADA_GAP // 3))
        t_ada = adas.close()

        loc = Local()
        YM = loc(4096)
        glow = loc(T)
        iw = loc(32)
        ik = loc(T)
        keep = loc.at
        it = take("small")
        b, tok = projT(it, 0, X, 8, 256, *tX)
        t_ik = evac(ik, b, tok)
        b, free = bank()
        tok = mm3(b, lambda k: (it[1][:, k * 256 + 128:k * 256 + 256], it[2][:, k * 256 + 128:k * 256 + 256]),
                  X, 8, *free)
        t_gl = evac(glow, b, tok)
        b, free = bank()
        PE.wait(*free)
        for qt in range(NT):
            for k in range(8):
                a = X(k, qt * P, (qt + 1) * P)
                w = (it[1][:, k * 256 + 144:k * 256 + 152], it[2][:, k * 256 + 144:k * 256 + 152])
                o = b[:, 8 * qt:8 * qt + 8]
                mm(o, a[0], w[0], qt == 0 and k == 0, False)
                mm(o, a[0], w[1], False, False)
                tok = mm(o, a[1], w[0], False, False, sig=k == 7 and qt == 3)
        done(it, tok)
        t_iw = SC.do(lambda e: e.activation(iw, b[:, 0:32], ACT.Copy, scale=8.0 ** -0.5), tok)
        banks.give(b, t_iw)
        wgu = loc(T)
        load(4, wgu[0:16, :], ins["gate_up"], SC.now(), VE.now())
        tk_gu = (s_in[4], 16)

        la = loc(T)
        sets = Slots([tuple(loc(T) for _ in range(5)) + (loc(1024),) for _ in range(2)])
        ATs = Slots([loc(T), loc(T)])
        states = Slots([tuple(loc(256) for _ in range(7))])
        t_z = None
        for at, _ in ATs.free:
            t_z = GP.do(lambda e: e.memset(at, 0.0))
        la_free = ()

        def tokens_by_features(it, dst, *waits):
            toks = []
            for pair in range(2):
                b, free = bank()
                PE.wait(*free, *it[3])
                for half in range(2):
                    qt = 2 * pair + half
                    for k in range(8):
                        a = X(k, qt * P, (qt + 1) * P)
                        w = (it[1][:, k * 256:(k + 1) * 256], it[2][:, k * 256:(k + 1) * 256])
                        o = b[:, half * 256:(half + 1) * 256]
                        mm(o, a[0], w[0], half == 0 and k == 0, False)
                        mm(o, a[0], w[1], False, False)
                        tok = mm(o, a[1], w[0], False, False, sig=k == 7 and half == 1)
                toks.append(evac(dst[:, pair * 512:(pair + 1) * 512], b, tok, *waits))
            done(it, tok)
            return toks

        def project(h):
            bufs, free_set = sets.take()
            E1, E2, E3, kd, ke, vtok = bufs
            it = take("gla")
            bq, tq = projT(it, 0, X, 8, 256)
            bk, tk_ = projT(it, 1, X, 8, 256)
            done(it, tk_)
            bz, free = bank()
            tz = mm(bz, wgu[0:16, h * P:(h + 1) * P], glow[0:16, :], True, True, tk_gu, t_gl, *free, sig=True)
            bg = V("gla_b_gate_2", h)
            t2 = VE.do(lambda e: e.tensor_scalar(E2, bz, bg, None, ALU.add), tz, *free_set)
            banks.give(bz, t2)
            t1 = SC.do(lambda e: e.activation(E1, E2, ACT.Abs), t2, *free_set)
            t1 = SC.do(lambda e: e.activation(E1, E1, ACT.Exp, scale=-1.0), t1)
            t1 = SC.do(lambda e: e.activation(E1, E1, ACT.Ln, bias=1.0), t1)
            t3 = VE.do(lambda e: e.scalar_tensor_tensor(E2, E2, 0.0, E1, ALU.min, ALU.subtract), t1, t2)
            t3 = VE.do(lambda e: e.tensor_tensor_scan(la, C("reset"), E2, 0.0, ALU.mult, ALU.add), t3, tk_c2,
                       *la_free)
            la_v = la.rearrange("p (c i) -> p c i", c=8)
            E3v = E3.rearrange("p (c i) -> p c i", c=8)
            t4 = VE.do(lambda e: e.tensor_tensor(E3v, la_v[:, :, 63:64].broadcast_to([P, 8, 64]), la_v,
                                                 ALU.subtract), t3)
            t5 = SC.do(lambda e: e.activation(E1, la, ACT.Exp, scale=1.0 / 16), t3)
            t6 = SC.do(lambda e: e.activation(E2, la, ACT.Exp, scale=-1.0 / 16), t3)
            t7 = SC.do(lambda e: e.activation(E3, E3, ACT.Exp, scale=1.0 / 16), t4)
            t8 = VE.do(lambda e: e.scalar_tensor_tensor(kd, bq, 128.0 ** -0.5, E1, ALU.mult, ALU.mult), tq, t5)
            banks.give(bq, t8)
            t9 = VE.do(lambda e: e.tensor_tensor(E2, bk, E2, ALU.mult), tk_, t6)
            t10 = VE.do(lambda e: e.tensor_tensor(E3, bk, E3, ALU.mult), tk_, t7)
            banks.give(bk, t9, t10)
            tv = tokens_by_features(take("gla"), vtok, *free_set)
            return bufs, (t8, t9, t10), tv, (t4, t6)

        def mix(h, bufs, toks, tv):
            E1, E2, E3, kd, ke, vtok = bufs
            t8, t9, t10 = toks
            b, free = bank()
            PE.wait(*free)
            for c in range(4):
                tt = PE.do(lambda e: e.transpose(b[:, c * P:(c + 1) * P], E3[:, c * P:(c + 1) * P], ident),
                           t10, sig=c == 3)
            tke = evac(ke, b, tt)
            AT, at_free = ATs.take()
            ATv = AT.rearrange("p (t q) -> p t q", t=4)
            b, free = bank()
            PE.wait(*free)
            for c in range(4):
                tt = mm(b[:, c * P:(c + 1) * P], E2[:, c * P:(c + 1) * P], kd[:, c * P:(c + 1) * P], c == 0, False,
                        t8, t9, sig=c == 3)
            bv = b.rearrange("p (t q) -> p t q", t=4)
            SC.do(lambda e: e.activation(ATv[0:64, :, 0:64], bv[0:64, :, 0:64], ACT.Copy), tt, t_z, *at_free)
            ta = SC.do(lambda e: e.activation(ATv[64:128, :, 64:128], bv[64:128, :, 64:128], ACT.Copy), tt)
            banks.give(b, ta)
            tg = GP.do(lambda e: e.affine_select(out=ATv, in_=ATv, compare_op=ALU.is_ge, fill=0.0, base=0,
                                                 pattern=[[0, 4], [1, 128]], channel_multiplier=-1), ta)
            it = take("gla")
            br, tr_ = projT(it, 0, X, 8, 256)
            ub = [bank() for _ in range(4)]
            for c in range(7):
                i = c % 2 + 2 * (c // 4)
                o = 256 * (c // 2 % 2)
                r0 = 64 * (c % 2)
                tu = mm(ub[i][0][:, o:o + 256], ke[r0:r0 + 64, (c // 2) * P:(c // 2 + 1) * P],
                        vtok[r0:r0 + 64, (c // 2) * 256:(c // 2 + 1) * 256], o == 0, False, tke, *tv, *ub[i][1],
                        sig=True)
            S, s_free = states.take()
            tS = VE.do(lambda e: e.tensor_copy(S[0], ub[0][0][:, 0:256]), tu, *s_free)
            for c in range(1, 7):
                i = c % 2 + 2 * (c // 4)
                o = 256 * (c // 2 % 2)
                tS = VE.do(lambda e: e.scalar_tensor_tensor(
                    S[c], S[c - 1], E1[:, c * 64 + 63:c * 64 + 64], ub[i][0][:, o:o + 256], ALU.mult, ALU.add), tS)
            for ap, _ in ub:
                banks.give(ap, tS)
            br2, tr2 = projT(it, 1, X, 8, 256)
            done(it, tr2)
            t_s0 = SC.do(lambda e: e.activation(ke, br, ACT.Silu), tr_, tu)
            banks.give(br, t_s0)
            t_s1 = SC.do(lambda e: e.activation(E3, br2, ACT.Silu), tr2, tke)
            banks.give(br2, t_s1)
            ob = [bank(), bank()]
            for vh in range(2):
                PE.wait(*ob[vh][1], tg)
                for c in range(4):
                    mm(ob[vh][0][:, c * P:(c + 1) * P], vtok[:, c * 256 + vh * P:c * 256 + (vh + 1) * P],
                       ATv[:, c, :], c == 0, False)
                for c in range(1, 8):
                    to = mm(ob[vh][0][:, c * 64:(c + 1) * 64], S[c - 1][:, vh * P:(vh + 1) * P],
                            kd[:, c * 64:(c + 1) * 64], False, c == 7, tS, sig=c == 7)
            ATs.give(AT, to)
            states.give(S, to)
            tr = rstd(lambda k: ob[k][0], 2, 256, E2, vtok, to)
            for vh in range(2):
                ch = 2 * h + vh
                prod = vtok[:, vh * T:(vh + 1) * T]
                t_n = VE.do(lambda e: e.scalar_tensor_tensor(prod, ob[vh][0], V("gla_norm_g_2", ch), E2,
                                                             ALU.mult, ALU.mult), tr)
                banks.give(ob[vh][0], t_n)
                t_n = VE.do(lambda e: e.tensor_tensor(prod, prod, (ke, E3)[vh], ALU.mult), t_n, (t_s0, t_s1)[vh])
                tY = split(*Y(ch), prod, t_n)
            sets.give(bufs, PE.now(), *tY)
            return tY

        projected = {}
        for what, h in GLA_STEPS:
            if what == "project":
                bufs, toks, tv, la_free = project(h)
                projected[h] = (bufs, toks, tv)
            else:
                tY = mix(h, *projected.pop(h))

        loc = phase()
        loc.at = keep
        ck, rt2, tmp2 = loc(1024), loc(T), loc(1024)
        loc.at = keep + 1024
        Mb = loc(1280)
        mo = [0, P, 3 * P, 6 * P]
        keep2 = loc.at
        loc.at = keep + 1024 + T + 1024
        iq = loc(4 * T)
        rl = Slots([loc(T) for _ in range(3)])
        sgs = Slots([loc(T) for _ in range(2)])
        m8 = loc(8)
        for i in range(2):
            it = take("iq")
            for c in range(2):
                b, tok = projT(it, c, X, 8, 256)
                t_iq = evac(iq[:, (2 * i + c) * T:(2 * i + c + 1) * T], b, tok)
            done(it, tok)
        it = take("dkv")
        for c in range(2):
            b, tok = projT(it, c, X, 8, 256)
            t = evac(ck[:, c * T:(c + 1) * T], b, tok)
        done(it, tok)
        tr = rstd(lambda k: ck[:, k * T:(k + 1) * T], 2, 256, rt2, tmp2, t)
        for k in range(2):
            t_ck = VE.do(lambda e: e.scalar_tensor_tensor(ck[:, k * T:(k + 1) * T], ck[:, k * T:(k + 1) * T],
                                                          V("dsa_kv_norm_g_2", k), rt2, ALU.mult, ALU.mult), tr)
        t_mb = GP.do(lambda e: e.memset(Mb[:, 0:P], 0.0), t_ck)
        t_mb = GP.do(lambda e: e.affine_select(out=Mb[:, 0:P], in_=Mb[:, 0:P], compare_op=ALU.is_ge, fill=NEG, base=0,
                                               pattern=[[-1, P]], channel_multiplier=1), t_mb)
        tMb = [t_mb]
        scored = []
        for qt in range(NT - 1, 0, -1):
            n = (qt + 1) * P
            acc = Mb[:, mo[qt]:mo[qt] + n]
            ta = None
            for hh in range(8):
                o64 = 64 * (hh % 2)
                b, free = bank()
                ts = mm(b[:, 0:n], iq[o64:o64 + 64, (hh // 2) * T + qt * P:(hh // 2) * T + (qt + 1) * P],
                        ik[o64:o64 + 64, 0:n], True, True, t_iq, t_ik, *free, sig=True)
                r_, rf = rl.take()
                t = SC.do(lambda e: e.activation(r_[:, 0:n], b[:, 0:n], ACT.Relu, scale=64.0 ** -0.5), ts, *rf)
                banks.give(b, t)
                w = iw[:, 8 * qt + hh:8 * qt + hh + 1]
                if hh == 0:
                    ta = VE.do(lambda e: e.tensor_scalar(acc, r_[:, 0:n], w, None, ALU.mult), t, t_iw, t_ck)
                else:
                    ta = VE.do(lambda e: e.scalar_tensor_tensor(acc, r_[:, 0:n], w, acc, ALU.mult, ALU.add), t, ta)
                rl.give(r_, ta)
            ta = GP.do(lambda e: e.affine_select(
                out=acc[:, n - P:n], in_=acc[:, n - P:n], compare_op=ALU.is_ge, fill=FILL, base=0,
                pattern=[[-1, P]], channel_multiplier=1), ta)
            scored.append((qt, acc, ta))

        def select():
            for qt, acc, ta in scored:
                for r in range(16):
                    tm = VE.do(lambda e: e.max(m8, acc), ta)
                    ta = VE.do(lambda e: e.match_replace(acc, m8, acc, TAKEN), tm)
                    yield
                ta = VE.do(lambda e: e.tensor_scalar(acc, acc, TAKEN, NEG, ALU.not_equal, ALU.mult), ta)
                tMb.insert(1, ta)

        marks = select()
        for i in range(4):
            it = take("za")
            sg = []
            for c in range(2):
                b, tok = projT(it, c, X, 8, 256)
                d, df = sgs.take()
                t = SC.do(lambda e: e.activation(d, b, ACT.Sigmoid), tok, *df)
                banks.give(b, t)
                sg.append((d, t))
                for _ in range(3):
                    next(marks, None)
            done(it, tok)
            it = take("ba")
            for c in range(2):
                b, tok = projT(it, c, Y, 8, 256, *tY)
                m = 2 * i + c
                d, t = sg[c]
                t = VE.do(lambda e: e.tensor_tensor(YM[:, m * T:(m + 1) * T], b, d, ALU.mult), tok, t)
                banks.give(b, t)
                sgs.give(d, t)
                for _ in range(3):
                    next(marks, None)
            done(it, tok)
        for _ in marks:
            pass

        phase()
        loc.at = keep2
        attn = Attn(loc, True, 128.0 ** -0.5)
        qd = Slots([loc(1024)])
        kv = Slots([loc(1024), loc(1024)])
        bia = Slots([glow])
        rel = C("rel")

        def finish(hd, rows, kvb, tk2):
            o, to = attn.values(rows, lambda s_: kvb[:, T + s_ * P:T + (s_ + 1) * P], tk2)
            kv.give(kvb, to)
            tY = split(*Y(hd), o, to)
            banks.give(o, *tY)
            return tY

        before = None
        for hd in range(H):
            c = hd % 2
            if hd % 4 == 0:
                uk = take("ukuv")
            if c == 0:
                it = take("dq")
                q, qf = qd.take()
                for c_ in range(2):
                    b, tok = projT(it, c_, X, 8, 256)
                    tq = evac(q[:, c_ * T:(c_ + 1) * T], b, tok, *qf)
                done(it, tok)
            u0 = (hd % 4) * 512
            kvb, kvf = kv.take()
            b, free = bank()
            for k in range(2):
                tok = mm(b, uk[1][:, u0 + k * 256:u0 + k * 256 + P], ck[:, k * T:(k + 1) * T], k == 0, k == 1,
                         *uk[3], *free, t_ck, sig=k == 1)
            tk1 = evac(kvb[:, 0:T], b, tok, *kvf)
            b, free = bank()
            PE.wait(*free)
            for s_ in range(4):
                for k in range(2):
                    tok = mm(b[:, s_ * P:(s_ + 1) * P], ck[:, k * T + s_ * P:k * T + (s_ + 1) * P],
                             uk[1][:, u0 + k * 256 + P:u0 + k * 256 + 2 * P], s_ == 0 and k == 0, False,
                             sig=s_ == 3 and k == 1)
            tk2 = evac(kvb[:, T:2 * T], b, tok, *kvf)
            if hd % 4 == 3:
                done(uk, tok)
            slope = float(2.0 ** -(hd + 1))

            def bias(qt):
                n = (qt + 1) * P
                bb, bf = bia.take()
                t = VE.do(lambda e: e.scalar_tensor_tensor(bb[:, 0:n], rel[:, 384 - P * qt:512], -slope,
                                                           Mb[:, mo[qt]:mo[qt] + n], ALU.mult, ALU.add),
                          tMb[qt], tk_c2, *bf)
                return bb[:, 0:n], t, lambda tok: bia.give(bb, tok)

            rows = attn.scores([(lambda a, b_: q[:, c * T + a:c * T + b_], lambda n: kvb[:, 0:n])], bias, tq, tk1)
            if c == 1:
                qd.give(q, PE.now())
            if before:
                finish(*before)
            before = (hd, rows, kvb, tk2)
        tY = finish(*before)
        phase()
        loc.at = keep
        G = loc(4096)
        for i in range(4):
            it = take("zb")
            for c in range(2):
                b, tok = projT(it, c, X, 8, 256)
                m = 2 * i + c
                t_g = SC.do(lambda e: e.activation(G[:, m * T:(m + 1) * T], b, ACT.Sigmoid), tok)
                banks.give(b, t_g)
            done(it, tok)
        x_read = tok
        for i in range(4):
            it = take("bb")
            for c in range(2):
                b, tok = projT(it, c, Y, 8, 256, *tY)
                m = 2 * i + c
                gm, ym = G[:, m * T:(m + 1) * T], YM[:, m * T:(m + 1) * T]
                t = VE.do(lambda e: e.tensor_tensor(gm, b, gm, ALU.mult), tok, t_g)
                banks.give(b, t)
                t = VE.do(lambda e: e.tensor_tensor(ym, ym, gm, ALU.add), t)
                tM = split(*X(m), ym, t, x_read)
            done(it, tok)
        for i in range(4):
            it = take("w_out")
            for c in range(2):
                b, tok = projT(it, c, X, 8, 256, *tM)
                m = 2 * i + c
                t_x = VE.do(lambda e: e.scalar_tensor_tensor(x_at(m), b, AD(2, m), x_at(m), ALU.mult, ALU.add),
                            tok, t_ada)
                banks.give(b, t_x)
            done(it, tok)

        loc = phase()
        rt, tmp = loc(T), loc(1024)
        adas.open()
        tX = modulated(4, 3, "norm2_g_2", t_x, tmp, rt, lambda: adas.step(2))
        t_ada = adas.close()
        load(5, skT[:, :], ins["skT"])
        tk_sk = (s_in[5], 16)
        loc = Local()
        iaT, ibT, gT = loc(T), loc(T), loc(T)
        room = loc(2048)
        qh = Slots([room[:, 0:1024]])
        sS = room[:, 1024:2048]
        cand, big = room[:, 0:1024], room[:, 1024:2048]
        wk = loc(256)
        v16 = loc(2 * 4 * 128)
        i16 = loc(2 * 4 * 128)
        best, cidx, hi16, lo16, fi, fg = (loc(P) for _ in range(6))
        tot = loc(16)
        v16v = v16.rearrange("p (s t h k) -> p s t h k", s=2, t=4, h=8)
        i16v = i16.rearrange("p (s t h k) -> p s t h k", s=2, t=4, h=8)
        ohA = Slots([loc(P) for _ in range(6)])
        ohB = Slots([loc(P) for _ in range(6)])
        hstage = Slots([(loc(2048), i) for i in range(2)])
        gstage = Slots([(loc(P * CT), i) for i in range(2)])
        VE.wait(*tX)
        SC.wait(*tX)
        tsel = None
        for h in range(8):
            it = take("pq")
            q, qf = qh.take()
            for c in range(2):
                b, tok = projT(it, c, X, 8, 256, *tX)
                tq = evac(q[:, c * T:(c + 1) * T], b, tok, *qf)
            done(it, tok)
            for c in range(2):
                b, free = bank()
                PE.wait(*free)
                for qt in range(NT):
                    tok = mm(b[:, qt * P:(qt + 1) * P], q[:, c * T + qt * P:c * T + (qt + 1) * P],
                             skT[:, c * P:(c + 1) * P], qt == 0, False, tq, tk_sk, sig=qt == 3)
                if c == 1:
                    qh.give(q, tok)
                t_s = evac(sS[:, c * T:(c + 1) * T], b, tok, tsel)
                for qt in range(NT):
                    s = sS[:, c * T + qt * P:c * T + (qt + 1) * P]
                    va, vb = v16v[:, c, qt, h, 0:8], v16v[:, c, qt, h, 8:16]
                    i_a, i_b = i16v[:, c, qt, h, 0:8].bitcast(U32), i16v[:, c, qt, h, 8:16].bitcast(U32)
                    w_ = wk[:, 0:P]
                    a = VE.do(lambda e: e.max(va, s), t_s)
                    VE.do(lambda e: e.max_index(i_a, va, s), a)
                    a = VE.do(lambda e: e.match_replace(w_, va, s, TAKEN), a)
                    a = VE.do(lambda e: e.max(vb, w_), a)
                    tsel = VE.do(lambda e: e.max_index(i_b, vb, w_), a)
        t_q = tok

        gd = nc.dram_tensor("gates", (T // CT, P, P * CT), F32).ap()
        hd_ = nc.dram_tensor("hidden", (NG, P, 2048), F32).ap()
        s_gw = [sem("s_gw0"), sem("s_gw1")]
        s_hw = [sem("s_hw0"), sem("s_hw1")]
        t_gates = []

        def selection():
            VE.do(lambda e: e.tensor_copy(i16, i16.bitcast(U32)), tsel)
            ti = VE.now()
            t_prev = None
            n_chunk = 0
            for qt in range(NT):
                cv = cand.rearrange("p (h i j) -> p h i j", h=4, i=16)
                for h in range(8):
                    t = VE.do(lambda e: e.tensor_tensor(
                        cv[:, h % 4], v16v[:, 0, qt, h, :].unsqueeze(2).broadcast_to([P, 16, 16]),
                        v16v[:, 1, qt, h, :].unsqueeze(1).broadcast_to([P, 16, 16]), ALU.add), ti, t_q, t_prev)
                    ch = cand[:, (h % 4) * 256:(h % 4 + 1) * 256]
                    ba, bb = best[:, h * 16:h * 16 + 8], best[:, h * 16 + 8:h * 16 + 16]
                    ca, cb = cidx[:, h * 16:h * 16 + 8].bitcast(U32), cidx[:, h * 16 + 8:h * 16 + 16].bitcast(U32)
                    a = VE.do(lambda e: e.max(ba, ch), t)
                    VE.do(lambda e: e.max_index(ca, ba, ch), a)
                    a = VE.do(lambda e: e.match_replace(wk, ba, ch, TAKEN), a)
                    a = VE.do(lambda e: e.max(bb, wk), a)
                    a = VE.do(lambda e: e.max_index(cb, bb, wk), a)
                    yield
                a1 = VE.do(lambda e: e.tensor_scalar(hi16.bitcast(U32), cidx.bitcast(U32), 4, None,
                                                     ALU.logical_shift_right), a)
                a2 = VE.do(lambda e: e.tensor_scalar(lo16.bitcast(U32), cidx.bitcast(U32), 15, None,
                                                     ALU.bitwise_and), a)
                bgv = big.rearrange("p (h k j) -> p h k j", h=4, k=16)
                bg3 = big.rearrange("p (m j) -> p m j", j=16)
                for s_, ix in ((0, hi16), (1, lo16)):
                    f = VE.do(lambda e: e.tensor_copy(fi, ix.bitcast(U32)), a1, a2)
                    for half in range(2):
                        hs = slice(64 * half, 64 * half + 64)
                        o = VE.do(lambda e: e.tensor_tensor(
                            bg3, fi[:, hs].unsqueeze(2).broadcast_to([P, 64, 16]),
                            iota[:, 0:16].unsqueeze(1).broadcast_to([P, 64, 16]), ALU.is_equal), f, VE.now())
                        o = VE.do(lambda e: e.tensor_tensor(
                            bgv, bgv, i16v[:, s_, qt, 4 * half:4 * half + 4, :].unsqueeze(2)
                            .broadcast_to([P, 4, 16, 16]), ALU.mult), o)
                        o = VE.do(lambda e: e.tensor_reduce(fg[:, hs], bg3, AXX, ALU.add), o, t_prev)
                        yield
                    b, free = bank()
                    tt = PE.do(lambda e: e.transpose(b[:, 0:P], fg, ident), o, *free)
                    dst = (iaT, ibT)[s_][:, qt * P:(qt + 1) * P]
                    t_prev = SC.do(lambda e: e.activation(dst, b[:, 0:P], ACT.Copy), tt)
                    banks.give(b, t_prev)
                bv = best.rearrange("p (h k) -> p h k", h=8)
                a = VE.do(lambda e: e.tensor_copy(tot[:, 0:8], bv[:, :, 0]), a)
                a = VE.do(lambda e: e.tensor_tensor(bv, bv, tot[:, 0:8].unsqueeze(2).broadcast_to([P, 8, 16]),
                                                    ALU.subtract), a)
                yield
                a = SC.do(lambda e: e.activation(fi, best, ACT.Exp), a, VE.now())
                yield
                fv = fi.rearrange("p (h k) -> p h k", h=8)
                a = VE.do(lambda e: e.tensor_reduce(tot[:, 0:8], fv, AXX, ALU.add), a)
                a = VE.do(lambda e: e.reciprocal(tot[:, 8:16], tot[:, 0:8]), a)
                a = VE.do(lambda e: e.tensor_tensor(fg.rearrange("p (h k) -> p h k", h=8), fv,
                                                    tot[:, 8:16].unsqueeze(2).broadcast_to([P, 8, 16]), ALU.mult),
                          a, t_prev)
                yield
                b, free = bank()
                tt = PE.do(lambda e: e.transpose(b[:, 0:P], fg, ident), a, *free)
                dst = gT[:, qt * P:(qt + 1) * P]
                t_prev = SC.do(lambda e: e.activation(dst, b[:, 0:P], ACT.Copy), tt)
                banks.give(b, t_prev)
                yield
                for ch in range(qt * P // CT, (qt + 1) * P // CT):
                    (st, si), sf = gstage.take()
                    stv = st.rearrange("p (b t) -> p b t", t=CT)
                    for t0 in range(0, CT, 4):
                        pairs = []
                        for j in range(4):
                            t = ch * CT + t0 + j
                            oa, fa = ohA.take()
                            ob_, fb = ohB.take()
                            VE.do(lambda e: e.tensor_scalar(oa, iota, iaT[:, t:t + 1], None, ALU.is_equal),
                                  t_prev, *fa)
                            to = VE.do(lambda e: e.tensor_scalar(ob_, iota, ibT[:, t:t + 1], gT[:, t:t + 1],
                                                                 ALU.is_equal, ALU.mult), t_prev, *fb)
                            pairs.append((oa, ob_, to))
                        yield
                        b, free = bank()
                        PE.wait(*free)
                        for j, (oa, ob_, to) in enumerate(pairs):
                            tok = mm(b[:, j * P:(j + 1) * P], oa, ob_, j == 0, False, to, sig=True)
                            ohA.give(oa, tok)
                            ohB.give(ob_, tok)
                        te = SC.do(lambda e: e.activation(
                            stv[:, :, t0:t0 + 4], b.rearrange("p (t b) -> p b t", t=4), ACT.Copy), tok, *sf)
                        banks.give(b, te)
                    SC.wait(te)
                    SC.dma(gd[ch], st, s_gw[si])
                    n_chunk += 1
                    gstage.give((st, si), (s_gw[si], 16 * ((n_chunk + 1) // 2)))
            t_gates.extend((te, PE.now(), VE.now()))

        work_ = selection()
        s_gr = [sem(f"s_gr{i}") for i in range(3)]
        s_hr = [sem(f"s_hr{i}") for i in range(3)]
        gdv = gd.rearrange("c a (g x) -> g a c x", x=4 * CT)

        def fetch(g):
            (gbuf, i), gf = gring.take()
            (hbuf, i2), hf = hring.take()
            SP.wait(*gf, *hf, (s_hw[g % 2], 16 * (g // 2 + 1)))
            SP.dma(hbuf, hd_[g], s_hr[i2])
            SP.dma(gbuf.rearrange("p (c x) -> p c x", c=T // CT), gdv[g], s_gr[i])
            n = 16 * (g // RING + 1)
            return (gbuf, i), (hbuf, i2), ((s_gr[i], n), (s_hr[i2], n))

        RING = 3
        for g in range(NG):
            if g == NG - 2:
                for _ in work_:
                    pass
                written = [(s_, 16 * (T // CT // 2)) for s_ in s_gw]
                loc = Local()
                gring = Slots([(loc(2048), i) for i in range(RING)])
                hring = Slots([])
                for i in range(2):
                    (ap, _), toks = gstage.free[i]
                    hring.give((ap, i), *toks)
                SP.wait(*t_gates, *written)
                fetched = [fetch(0), fetch(1)]
            (ab, si), af = hstage.take()
            for j in range(2):
                it = take("U")
                for bb in range(2):
                    b, free = bank()
                    PE.wait(*free, *it[3])
                    for k in range(8):
                        o = bb * 1024 + k * P
                        xh, xl = X(k)
                        mm(b, it[1][:, o:o + P], xh, k == 0, False)
                        mm(b, it[1][:, o:o + P], xl, False, False)
                        tok = mm(b, it[2][:, o:o + P], xh, False, k == 7, sig=k == 7)
                        if k == 3:
                            next(work_, None)
                    q = 2 * j + bb
                    t = SC.do(lambda e: e.activation(ab[:, q * T:(q + 1) * T], b, ACT.Gelu), tok, *af)
                    banks.give(b, t)
                    if bb == 1:
                        done(it, tok)
                    if bb + j != 1 or bb:
                        next(work_, None)
            SC.wait(t)
            SC.dma(hd_[g], ab, s_hw[si])
            hstage.give((ab, si), (s_hw[si], 16 * (g // 2 + 1)))
        for _ in work_:
            pass
        written += [(s_, 16 * (NG // 2)) for s_ in s_hw]

        (ap, _), toks = hstage.free[0]
        hring.give((ap, 2), *toks)
        fetched.append(fetch(2))
        AG = Slots([yhl[:, 0:4096], yhl[:, 4096:8192]])

        def gated(fetched):
            gslot, hslot, toks = fetched
            ap = hslot[0]
            av = ap.rearrange("p (b c t) -> p b c t", b=4, t=CT)
            gv = gslot[0].rearrange("p (c b t) -> p b c t", b=4, t=CT)
            ag, af = AG.take()
            for q in range(4):
                tm = VE.do(lambda e: e.tensor_tensor(av[:, q], av[:, q], gv[:, q], ALU.mult), *toks)
                th, tl = split(ag[:, q * T:(q + 1) * T], ag[:, 2048 + q * T:2048 + (q + 1) * T],
                               ap[:, q * T:(q + 1) * T], tm, *af)
                yield
            gring.give(gslot, tm)
            hring.give(hslot, th, tl)
            ready_ag.append((ag, (th, tl)))

        ready_ag = []
        for _ in gated(fetched.pop(0)):
            pass
        for g in range(NG):
            ag = ready_ag.pop(0)
            prep = gated(fetched.pop(0)) if g + 1 < NG else iter(())
            for half in range(2):
                it = take("V")
                for m in range(4):
                    b, free = bank()
                    PE.wait(*free, *it[3], *ag[1])
                    for q in range(4):
                        o = q * 512 + m * P
                        ah, al = ag[0][:, q * T:(q + 1) * T], ag[0][:, 2048 + q * T:2048 + (q + 1) * T]
                        mm(b, it[1][:, o:o + P], ah, q == 0, False)
                        mm(b, it[1][:, o:o + P], al, False, False)
                        tok = mm(b, it[2][:, o:o + P], ah, False, q == 3, sig=q == 3)
                    dd = half * 4 + m
                    t_x = VE.do(lambda e: e.scalar_tensor_tensor(x_at(dd), b, AD(5, dd), x_at(dd),
                                                                 ALU.mult, ALU.add), tok)
                    banks.give(b, t_x)
                    next(prep, None)
                done(it, tok)
            AG.give(ag[0], tok)
            if g + RING < NG:
                fetched.append(fetch(g + RING))

        loc = phase()
        rt, tmp = loc(T), loc(1024)
        tr = rstd(x_at, 8, 1024, rt, tmp)
        yo = loc(4096)
        for k in range(8):
            tk = VE.do(lambda e: e.scalar_tensor_tensor(x_at(k), x_at(k), V("final_norm_g_2", k), rt,
                                                             ALU.mult, ALU.mult), tr)
        s_out = sem("s_out")
        for qt in range(NT):
            for half in range(2):
                b, free = bank()
                PE.wait(*free, tk)
                for c in range(4):
                    k = 4 * half + c
                    tt = PE.do(lambda e: e.transpose(
                        b[:, c * P:(c + 1) * P], XT[:, k * T + qt * P:k * T + (qt + 1) * P], ident), sig=c == 3)
                t = evac(yo[:, qt * 1024 + half * 512:qt * 1024 + (half + 1) * 512], b, tt, eng=VE if half else None)
                SP.wait(t)
            SP.dma(out[0, qt * P:(qt + 1) * P, :],
                                                       yo[:, qt * 1024:(qt + 1) * 1024], s_out)
        SP.wait((s_out, 64), *written)
        assert state["use"] == len(items)

        block = ctx.enter_context(nc.Block())

        @block.sync
        def _(e):
            SP.run()

        @block.scalar
        def _(e):
            SC.run()

        @block.vector
        def _(e):
            VE.run()

        @block.gpsimd
        def _(e):
            GP.run()

        @block.tensor
        def _(e):
            PE.run()


_INS = ["xT", "consts", "vecs", "rope", "gate_up", "skT", "l0_in", "l0_uq", "l0_ukv", "l0_out", "w_ada", "w_small",
        "w_gla", "w_za", "w_ba", "w_dkv", "w_iq", "w_dq", "w_ukuv", "w_zb", "w_bb", "w_out", "w_pq", "U", "V"]


def layouts(inputs):
    a = {k: np.asarray(v) for k, v in inputs.items()}

    def cols(w, chunks):
        w = np.concatenate([w[:, c] for c in chunks], axis=1)
        n = w.shape[1] // 256
        return w.reshape(8, P, n, 256).transpose(2, 1, 0, 3).reshape(n, P, 2048)

    def sl(a0, n):
        return [slice(a0 + i * P, a0 + (i + 1) * P) for i in range(n // P)]

    r = {}
    r["xT"] = a["x"][0].T
    vecs = []
    for name in VEC:
        vecs.append(a[name].reshape(-1, P).T)
    r["vecs"] = np.concatenate(vecs, axis=1)
    f = np.float32
    i = np.arange(P)
    consts = np.zeros((P, NCONST), f)
    consts[:, 0:128] = np.eye(P)
    consts[:, 128:256] = 1.0
    consts[:, 256:384] = i[None, :]
    consts[:, 384:896] = i[:, None] + 384 - np.arange(512)[None, :]
    consts[:, 896:1408] = (np.arange(512) % 64 != 0)[None, :]
    r["consts"] = consts
    inv = (1.0 / (f(10000.0) ** (np.arange(0, 64, 2, dtype=f) / f(64)))).astype(f)
    ang = (np.arange(T, dtype=f)[:, None] * inv[None, :]).astype(f)
    cos, sin = np.cos(ang).astype(f).T, np.sin(ang).astype(f).T
    r["rope"] = np.concatenate([np.concatenate([cos] * 4), np.concatenate([-sin, sin] * 2)], axis=1)
    w = a["l0_w_in"]
    pe = list(range(640, 704))
    sw = list(range(672, 704)) + list(range(640, 672))
    chunks = sl(0, 640) + [pe + pe, sw + sw] + sl(704, 1024)
    r["l0_in"] = cols(w, chunks + chunks[-1:])
    uq = a["l0_w_uq"].reshape(3, P, 4, 2, 192)
    sw2 = np.concatenate([uq[..., 160:192], uq[..., 128:160]], axis=-1)
    uq = np.concatenate([uq[..., 0:128].reshape(3, P, 4, 256), uq[..., 128:192].reshape(3, P, 4, 128),
                         sw2.reshape(3, P, 4, 128)], axis=-1)
    r["l0_uq"] = uq.transpose(2, 1, 0, 3).reshape(4, P, 1536)
    ukv = a["l0_w_ukv"].reshape(2, P, 4, 2, 2, 128)
    r["l0_ukv"] = ukv.transpose(2, 1, 0, 4, 3, 5).reshape(4, P, 1024)
    r["l0_out"] = cols(a["l0_w_out"], sl(0, 1024))
    r["w_ada"] = cols(a["w_ada_2"][0], sl(0, 6144))
    w = a["w_in_2"][0]
    gq, gk, gv, gr, glow, dq, dkv, iq, ik, iw, za, zb = (
        int(x) for x in np.cumsum([0, 512, 512, 1024, 1024, 16, 1024, 256, 512, 64, 8, 1024]))
    iks = list(range(ik, ik + 64))
    r["w_small"] = cols(w, [iks + iks, list(range(glow, glow + 16)) + list(range(iw, iw + 8)) + [0] * 104])[0]
    ch = []
    for h in range(4):
        ch += [slice(gq + h * P, gq + (h + 1) * P), slice(gk + h * P, gk + (h + 1) * P)]
        ch += sl(gv + h * 256, 256) + sl(gr + h * 256, 256)
    r["w_gla"] = cols(w, ch)
    for name, at, n in (("w_za", za, 1024), ("w_zb", zb, 1024), ("w_dkv", dkv, 256), ("w_iq", iq, 512),
                        ("w_dq", dq, 1024)):
        r[name] = cols(w, sl(at, n))
    r["w_ba"], r["w_bb"], r["w_out"] = (cols(a[n][0], sl(0, 1024)) for n in ("w_branch_a_2", "w_branch_b_2", "w_out_2"))
    r["w_pq"] = cols(a["peer_w_q_2"][0], sl(0, 2048))
    uk = a["dsa_w_uk_2"][0].transpose(0, 2, 1).reshape(2, 4, 2, P, 128)
    uv = a["dsa_w_uv_2"][0].reshape(2, 4, 2, P, 128)
    r["w_ukuv"] = np.concatenate([uk, uv], axis=-1).transpose(0, 3, 1, 2, 4).reshape(2, P, 2048)
    r["gate_up"] = a["gla_w_gate_up_2"][0]
    r["skT"] = np.concatenate([a["peer_sub_keys_1_2"][0].T, a["peer_sub_keys_2_2"][0].T], axis=1)
    r["U"] = a["peer_u_2"][0].reshape(P, 64, 2, 8, P).transpose(1, 4, 2, 3, 0).reshape(64, P, 2048)
    r["V"] = a["peer_v_2"][0].reshape(P, 32, 4, 2, 512).transpose(1, 3, 0, 2, 4).reshape(64, P, 2048)
    return {k: np.ascontiguousarray(v) for k, v in r.items()}


def kernel(**inputs):
    import concourse.bacc as bacc
    from concourse.bass_utils import run_bass_kernel_spmd as run

    nc = bacc.Bacc("TRN2", target_bir_lowering=False, num_devices=1)
    arrays = layouts(inputs)
    args = {k: nc.dram_tensor("in_" + k, v.shape, F32, kind="ExternalInput").ap() for k, v in arrays.items()}
    out = nc.dram_tensor("out_0", (1, T, 1024), F32, kind="ExternalOutput").ap()
    build(nc, args, out)
    r = run(nc, [{"in_" + k: v for k, v in arrays.items()}], core_ids=[0])
    return r.results[0]["out_0"]
```

```python
from contextlib import ExitStack

import numpy as np

import concourse.bass as bass
from concourse import mybir

F32 = mybir.dt.float32
F32R = mybir.dt.float32r
U32 = mybir.dt.uint32
ALU = mybir.AluOpType
ACT = mybir.ActivationFunctionType
AXX = mybir.AxisListType.X

P = 128
T = 512
NT = 4
EPS = 1e-6
ITEM = 2048
H = 8
NEG = -1e30
FILL = -1e38
TAKEN = -3e38
CT = 16
NR = 3
GLA_STEPS = [("project", 0), ("project", 1), ("mix", 0), ("project", 2), ("mix", 1), ("project", 3), ("mix", 2),
             ("mix", 3)]

VEC = {}
_at = 0
for _name, _n in (("l0_norm", 8), ("l0_q_norm", 3), ("l0_kv_norm", 2), ("final_norm", 8), ("c_2", 8),
                  ("b_ada_2", 48), ("norm1_g_2", 8), ("gla_b_gate_2", 4), ("gla_norm_g_2", 8),
                  ("dsa_kv_norm_g_2", 2), ("norm2_g_2", 8), ("final_norm_g_2", 8)):
    VEC[_name] = (_at, _n)
    _at += _n
NVEC = _at
CONST = {"ident": (0, 128), "ones": (128, 128), "iota": (256, 128), "rel": (384, 512), "reset": (896, 512)}
NCONST = 1408


class Calls:

    def __init__(self, **methods):
        self.methods = methods

    def hold(self, name, args, kwargs):
        method = self.methods[name]
        return lambda: method(*args, **kwargs)

    def activation(self, *args, **kwargs):
        return self.hold("activation", args, kwargs)

    def tensor_copy(self, *args, **kwargs):
        return self.hold("tensor_copy", args, kwargs)

    def tensor_tensor(self, *args, **kwargs):
        return self.hold("tensor_tensor", args, kwargs)

    def tensor_scalar(self, *args, **kwargs):
        return self.hold("tensor_scalar", args, kwargs)

    def scalar_tensor_tensor(self, *args, **kwargs):
        return self.hold("scalar_tensor_tensor", args, kwargs)

    def tensor_tensor_scan(self, *args, **kwargs):
        return self.hold("tensor_tensor_scan", args, kwargs)

    def tensor_reduce(self, *args, **kwargs):
        return self.hold("tensor_reduce", args, kwargs)

    def reciprocal(self, *args, **kwargs):
        return self.hold("reciprocal", args, kwargs)

    def max(self, *args, **kwargs):
        return self.hold("max", args, kwargs)

    def max_index(self, *args, **kwargs):
        return self.hold("max_index", args, kwargs)

    def match_replace(self, *args, **kwargs):
        return self.hold("match_replace", args, kwargs)

    def memset(self, *args, **kwargs):
        return self.hold("memset", args, kwargs)

    def affine_select(self, *args, **kwargs):
        return self.hold("affine_select", args, kwargs)

    def matmul(self, *args, **kwargs):
        return self.hold("matmul", args, kwargs)

    def transpose(self, *args, **kwargs):
        return self.hold("transpose", args, kwargs)

    def dma_start(self, *args, **kwargs):
        return self.hold("dma_start", args, kwargs)

    def wait_ge(self, *args, **kwargs):
        return self.hold("wait_ge", args, kwargs)


class Engine:

    def __init__(self, sem, **methods):
        self.sem, self.n, self.seen, self.ops, self.open = sem, 0, {}, [], False
        self.calls = Calls(**methods)

    def wait(self, *tokens):
        for tok in tokens:
            if tok is None:
                continue
            sem, value = tok
            if self.seen.get(sem.name, 0) < value:
                self.seen[sem.name] = value
                self.ops.append((self.calls.wait_ge(sem, value), None, 0))

    def do(self, fn, *tokens, sig=True):
        self.wait(*tokens)
        if sig:
            self.n += 1
        self.ops.append((fn(self.calls), self.sem if sig else None, 1))
        self.open = not sig
        return (self.sem, self.n)

    def dma(self, dst, src, sem):
        self.ops.append((self.calls.dma_start(dst, src), sem, 16))

    def now(self):
        assert not self.open
        return (self.sem, self.n) if self.n else None

    def run(self):
        for call, sem, by in self.ops:
            instruction = call()
            if sem is not None:
                instruction.then_inc(sem, by)


class Slots:

    def __init__(self, aps):
        self.free = [(ap, ()) for ap in aps]

    def take(self):
        return self.free.pop(0)

    def give(self, ap, *tokens):
        self.free.append((ap, tokens))


def build(nc, ins, out):
    ctx = ExitStack()
    with ctx:
        def sb(name, n, dt=F32):
            return ctx.enter_context(nc.sbuf_tensor(name, [P, n], dt))

        def sem(name):
            return ctx.enter_context(nc.semaphore(name))

        PE = Engine(sem("s_pe"), matmul=nc.tensor.matmul, transpose=nc.tensor.transpose, wait_ge=nc.tensor.wait_ge)
        SC = Engine(sem("s_act"), activation=nc.scalar.activation, dma_start=nc.scalar.dma_start,
                    wait_ge=nc.scalar.wait_ge)
        v = nc.vector
        VE = Engine(sem("s_dve"), tensor_copy=v.tensor_copy, tensor_tensor=v.tensor_tensor,
                    tensor_scalar=v.tensor_scalar, scalar_tensor_tensor=v.scalar_tensor_tensor,
                    tensor_tensor_scan=v.tensor_tensor_scan, tensor_reduce=v.tensor_reduce,
                    reciprocal=v.reciprocal, max=v.max, max_index=v.max_index, match_replace=v.match_replace,
                    wait_ge=v.wait_ge)
        GP = Engine(sem("s_pool"), tensor_scalar=nc.gpsimd.tensor_scalar,
                    tensor_tensor=nc.gpsimd.tensor_tensor, memset=nc.gpsimd.memset,
                    affine_select=nc.gpsimd.affine_select,
                    wait_ge=nc.gpsimd.wait_ge)
        SP = Engine(sem("s_sp"), dma_start=nc.sync.dma_start, wait_ge=nc.sync.wait_ge)

        raw = sb("raw", NR * ITEM)
        whl = sb("whl", 4 * ITEM, F32R)
        xhl = sb("xhl", 8192, F32R)
        yhl = sb("yhl", 8192, F32R)
        XT = sb("XT", 4096)
        cst = sb("cst", NCONST)
        vec = sb("vec", NVEC)
        ada = sb("ada", 48)
        mod = sb("mod", 16)
        stat = sb("stat", 32)
        skT = sb("skT", 256)
        LN = 16448
        L = sb("L", LN)
        banks = Slots([ctx.enter_context(nc.psum_tensor(f"bank{i}", [P, 512], F32))[:, :] for i in range(8)])

        def C(name):
            o, n = CONST[name]
            return cst[:, o:o + n]

        def V(name, j):
            o, _ = VEC[name]
            return vec[:, o + j:o + j + 1]

        def F(ap):
            return ap.bitcast(F32)

        ident, ones, iota = C("ident"), C("ones"), C("iota")

        class Local:
            def __init__(self):
                self.at = 0

            def __call__(self, n):
                ap = L[:, self.at:self.at + n]
                self.at += n
                assert self.at <= LN, self.at
                return ap

        def phase():
            toks = [e.now() for e in (PE, SC, VE, GP)]
            for e in (SC, VE, GP):
                e.wait(*toks)
            return Local()

        s_in = [sem(f"s_in{i}") for i in range(9)]

        def load(i, dst, src, *tokens):
            SP.wait(*tokens)
            SP.dma(dst, src, s_in[i])

        load(2, vec[:, :], ins["vecs"])
        tk_x = []

        def load_x(i):
            at = (0, 6, 7, 8)[i]
            load(at, XT[:, i * 1024:(i + 1) * 1024].rearrange("p (k t) -> p k t", k=2),
                 ins["xT"][i * 256:(i + 1) * 256].rearrange("(k p) t -> p k t", p=P))
            tk_x.append((s_in[at], 16))

        load_x(0)
        tk_c, tk_v = (s_in[1], 16), (s_in[2], 16)

        items = []
        ADA0 = 24
        n_ada = [ADA0 // 2]

        def ada_items(n):
            for _ in range(n):
                items.append(("ada", ins["w_ada"][n_ada[0]], ITEM, False))
                n_ada[0] += 1

        for i in range(8):
            items.append(("l0_in", ins["l0_in"][i], ITEM, True))
        for h in range(H):
            if h % 2 == 0:
                items.append(("uq", ins["l0_uq"][h // 2], 1536, True))
                items.append(("ukv", ins["l0_ukv"][h // 2], 1024, True))
        for i in range(4):
            items.append(("l0_out", ins["l0_out"][i], ITEM, True))
        items.append(("small", ins["w_small"], ITEM, True))
        for step in GLA_STEPS:
            for j in (range(2) if step[0] == "project" else (2,)):
                items.append(("gla", ins["w_gla"][3 * step[1] + j], ITEM, True))
        for i in range(2):
            items.append(("iq", ins["w_iq"][i], ITEM, True))
        items.append(("dkv", ins["w_dkv"][0], ITEM, True))
        for i in range(4):
            items.append(("za", ins["w_za"][i], ITEM, True))
            items.append(("ba", ins["w_ba"][i], ITEM, True))
        for i in range(4):
            items.append(("dq", ins["w_dq"][i], ITEM, True))
            ada_items(3)
        for name in ("zb", "bb", "w_out"):
            for i in range(4):
                items.append((name, ins[name if name == "w_out" else "w_" + name][i], ITEM, True))
        assert n_ada[0] == 24
        for i in range(8):
            items.append(("pq", ins["w_pq"][i], ITEM, True))
        NG = 32
        items += [("U", ins["U"][i], ITEM, True) for i in range(2 * NG)]
        items += [("V", ins["V"][i], ITEM, True) for i in range(2 * NG)]

        s_raw = [sem(f"s_raw{i}") for i in range(NR)]
        raw_free = [()] * NR
        landed = {}
        state = {"dma": 0, "conv": 0, "use": 0}

        def pump(limit=len(items)):
            while state["dma"] < limit and raw_free[state["dma"] % NR] is not None:
                i = state["dma"]
                r = i % NR
                name, src, n, _ = items[i]
                SP.wait(*raw_free[r])
                raw_free[r] = None
                SP.dma(raw[:, r * ITEM:r * ITEM + n], src, s_raw[r])
                landed[i] = (s_raw[r], 16 * (i // NR + 1))
                state["dma"] += 1

        whl_free = [(), ()]
        ready = {}
        nconv = [0]

        def convert():
            i = state["conv"]
            if i >= len(items):
                return
            name, src, n, conv = items[i]
            if i not in landed:
                return
            r = i % NR
            src_ap = raw[:, r * ITEM:r * ITEM + n]
            if conv:
                w = nconv[0] % 2
                if whl_free[w] is None:
                    return
                nconv[0] += 1
                hi = whl[:, 2 * w * ITEM:2 * w * ITEM + n]
                lo = whl[:, (2 * w + 1) * ITEM:(2 * w + 1) * ITEM + n]
                h = n // 2
                th = None
                for a, b in ((0, h), (h, n)):
                    th = SC.do(lambda e: e.activation(hi[:, a:b], src_ap[:, a:b], ACT.Copy),
                               landed[i], *whl_free[w])
                    tl = VE.do(lambda e: e.tensor_tensor(lo[:, a:b], src_ap[:, a:b], F(hi[:, a:b]),
                                                                   ALU.subtract),
                               landed[i], th, *whl_free[w])
                whl_free[w] = None
                raw_free[r] = (th, tl)
                ready[i] = (hi, lo, (th, tl), w)
            else:
                ready[i] = (src_ap, None, (landed[i],), r)
            state["conv"] += 1
            pump()

        def take(name):
            i = state["use"]
            assert items[i][0] == name, (items[i][0], name)
            ahead = i + 1
            while ahead < len(items) - 1 and not items[ahead][3]:
                ahead += 1
            while state["conv"] <= min(ahead, len(items) - 1):
                before = state["conv"]
                convert()
                if state["conv"] == before:
                    break
            assert i in ready
            state["use"] += 1
            return (i,) + ready.pop(i)

        def done(item, *tokens):
            i, _, _, _, where = item
            if items[i][3]:
                whl_free[where] = tokens
            else:
                raw_free[where] = tokens
                pump()

        def prefetch():
            for _ in range(2):
                convert()

        pump(1)
        load_x(1)
        load_x(2)
        load_x(3)
        load(1, cst[:, 0:384], ins["consts"][:, 0:384])
        pump()

        def mm(bank, lhsT, rhs, start, stop, *tokens, sig=False):
            return PE.do(lambda e: e.matmul(bank, lhsT, rhs, start=start, stop=stop, skip_group_check=True),
                         *tokens, sig=sig)

        def mm3(o, a, b, nk, *tokens):
            PE.wait(*tokens)
            for k in range(nk):
                PE.wait(*b.ready[k])
                (ah, al), (bh, bl) = a(k), b(k)
                mm(o, ah, bh, k == 0, False)
                mm(o, ah, bl, False, False)
                tok = mm(o, al, bh, False, k == nk - 1, sig=k == nk - 1)
            return tok

        def mm3_part(o, a, b, ks, nk, *tokens):
            PE.wait(*tokens)
            for k in ks:
                PE.wait(*b.ready[k])
                (ah, al), (bh, bl) = a(k), b(k)
                mm(o, ah, bh, k == 0, False)
                mm(o, ah, bl, False, False)
                tok = mm(o, al, bh, False, k == nk - 1, sig=k == ks[-1])
            return tok

        def split(hi, lo, src, tok, *waits):
            th = SC.do(lambda e: e.activation(hi, src, ACT.Copy), tok, *waits)
            tl = VE.do(lambda e: e.tensor_tensor(lo, src, F(hi), ALU.subtract), tok, th, *waits)
            return th, tl

        class Parts:

            def __init__(self, base, n, first=0):
                self.base, self.n, self.first = base, n, first
                self.ready = [()] * 8

            def __call__(self, k, a=0, b=T):
                o = (self.first + k) * T
                return self.base[:, o + a:o + b], self.base[:, self.n + o + a:self.n + o + b]

            def put(self, k, src, tok, *waits):
                self.ready[k] = split(*self(k), src, tok, *waits)
                return self.ready[k]

        X = Parts(xhl, 4096)
        Y = Parts(yhl, 4096)

        def wchunk(item, nk, width, c):
            _, hi, lo, _, _ = item
            def at(k):
                o = k * width + c * P
                return hi[:, o:o + P], lo[:, o:o + P]
            return at

        def bank():
            return banks.take()

        def projT(item, c, src, nk=8, width=256, *tokens):
            b, free = bank()
            tok = mm3(b, wchunk(item, nk, width, c), src, nk, *item[3], *free, *tokens)
            return b, tok

        def evac(dst, b, tok, *waits, eng=None, slot=None):
            if eng is VE:
                t = VE.do(lambda e: e.tensor_copy(dst, b), tok, *waits)
            else:
                t = SC.do(lambda e: e.activation(dst, b, ACT.Copy), tok, *waits)
            banks.give(b if slot is None else slot, t)
            return t

        stats = Slots([stat[:, 0:16], stat[:, 16:32]])

        class Norm:

            def __init__(self, widths, sq, sums=None):
                self.sums = sums
                self.at, self.t_sum = [0] * len(widths), [None] * len(widths)
                self.widths, self.sq, self.queue, self.started = widths, Slots(sq), [], set()
                self.b, self.free = bank()

            def add(self, src, *tokens, group=0, gain=1.0):
                first = self.sums is not None and self.at[group] == 0
                s, fr = (self.sums[group], ()) if first else self.sq.take()
                t = SC.do(lambda e: e.activation(s, src, ACT.Square, scale=gain), *tokens, *fr)
                self.at[group] += 1
                if first:
                    self.t_sum[group] = t
                elif self.sums is not None and self.at[group] * P < self.widths[group]:
                    acc = self.sums[group]
                    self.t_sum[group] = GP.do(lambda e: e.tensor_tensor(acc, acc, s, ALU.add), t, self.t_sum[group])
                    self.sq.give(s, self.t_sum[group])
                else:
                    if self.sums is not None:
                        self.queue.append((group, self.sums[group], self.t_sum[group]))
                    self.queue.append((group, s, t))
                    if self.sums is None and len(self.sq.free) == 0:
                        self.flush(1)
                return t

            def flush(self, keep=0):
                while len(self.queue) > keep:
                    g, s, t = self.queue.pop(0)
                    PE.wait(*self.free, tk_c)
                    for qt in range(NT):
                        self.tok = mm(self.b[:, 4 * g + qt:4 * g + qt + 1], s[:, qt * P:(qt + 1) * P], ones[:, 0:1],
                                      not self.started, False, t, sig=qt == NT - 1)
                        self.started.add(g)
                    self.sq.give(s, self.tok)

            def means(self, eps=(EPS, EPS)):
                self.flush()
                self.st, fr = stats.take()
                for g, w in enumerate(self.widths):
                    t = VE.do(lambda e: e.tensor_scalar(self.st[:, 4 * g:4 * g + 4], self.b[:, 4 * g:4 * g + 4],
                                                        1.0 / w, eps[g], ALU.mult, ALU.add), self.tok, *fr)
                banks.give(self.b, t)
                return t

            def root(self, a, b, t):
                t = SC.do(lambda e: e.activation(self.st[:, a:b], self.st[:, a:b], ACT.Sqrt), t)
                return VE.do(lambda e: e.reciprocal(self.st[:, a:b], self.st[:, a:b]), t)

            def spread(self, o, t, dg, *waits):
                b, free = bank()
                PE.wait(*free)
                for qt in range(NT):
                    d = dg[:, qt * P:(qt + 1) * P]
                    td = VE.do(lambda e: e.tensor_scalar(d, ident, self.st[:, o + qt:o + qt + 1], None, ALU.mult),
                               t, tk_c, *waits)
                    tok = mm(b[:, qt * P:(qt + 1) * P], ones, d, qt == 0, False, td, sig=qt == NT - 1)
                self.last = td
                return b, tok

            def rows(self, dg, *waits):
                t = self.root(0, 4 * len(self.widths), self.means())
                out = [self.spread(4 * g, t, dg[:, g * T:(g + 1) * T], *waits) for g in range(len(self.widths))]
                stats.give(self.st, self.last)
                return out

        def halves(ap, n=2):
            return [ap[:, i * T:(i + 1) * T] for i in range(n)]

        loc = Local()
        cq, ckv, kpe, gate = loc(1536), loc(1024), loc(512), loc(4096)
        dg, dg2, tmp, pet = loc(T), loc(1024), loc(4 * T), loc(T)
        rope = cst[:, 384:1408]
        n_c = [0]
        s_c = sem("s_c")

        def silu_c(dst, *waits):
            SP.wait(*waits)
            n_c[0] += 16
            SP.dma(dst, ins["c_rows"], s_c)
            return SC.do(lambda e: e.activation(dst, dst, ACT.Silu), (s_c, n_c[0]), *waits)

        load(3, rope, ins["rope"])
        tk_r = (s_in[3], 16)
        cosT, sinT = rope[:, 0:T], rope[:, T:2 * T]

        def x_at(k):
            return XT[:, k * T:(k + 1) * T]

        norm = Norm([1024], halves(tmp, 2), [loc(T)])
        tm = Slots(halves(tmp[:, 1024:2048]))
        for k in range(8):
            t_, fr = tm.take()
            a = VE.do(lambda e: e.tensor_scalar(t_, x_at(k), V("l0_norm", k), None, ALU.mult), tk_x[k // 2], tk_v, *fr)
            toks = X.put(k, t_, a)
            tm.give(t_, *toks)
            if k == 1:
                convert()
        for k in range(8):
            norm.add(x_at(k), tk_x[k // 2])

        def ada_chunk(w, silc, *tokens):
            i = n_ada_done[0]
            n_ada_done[0] += 1
            t = VE.do(lambda e: e.scalar_tensor_tensor(w, w, 1.0, silc, ALU.mult, ALU.mult,
                                                       accum_out=ada[:, i:i + 1]), *tokens)
            o, _ = VEC["b_ada_2"]
            t_ada[:] = [VE.do(lambda e: e.tensor_tensor(ada[:, i:i + 1], ada[:, i:i + 1],
                                                        vec[:, o + i:o + i + 1], ALU.add), t, tk_v)]
            return t

        def ada_step(silc, t_c):
            it = take("ada")
            for c in range(2):
                t = ada_chunk(it[1][:, c * 1024:(c + 1) * 1024], silc, t_c, *it[3])
            done(it, t)

        n_ada_done = [0]
        t_ada = []
        silc = loc(1024)
        t_c = silu_c(silc)
        ada_slots = Slots([(loc(1024), i) for i in range(3)])
        s_ada = [sem(f"s_ada{i}") for i in range(3)]
        ada_queue = []
        n_fetched = [0]

        def ada_fetch():
            i = n_fetched[0]
            if i == ADA0:
                return
            n_fetched[0] += 1
            (w, r), free = ada_slots.take()
            SP.wait(*free)
            SP.dma(w, ins["w_ada"][i // 2][:, i % 2 * 1024:(i % 2 + 1) * 1024], s_ada[r])
            ada_queue.append((w, r, (s_ada[r], 16 * (i // 3 + 1))))

        def ada_early(n):
            for _ in range(n):
                if ada_queue:
                    w, r, tok = ada_queue.pop(0)
                    ada_slots.give((w, r), ada_chunk(w, silc, t_c, tok))
                    ada_fetch()

        for _ in range(3):
            ada_fetch()

        CQ = Parts(yhl, 2560)
        norm2 = Norm([384, 256], halves(tmp, 2))
        R = dg
        waiting = []

        def leave(ch, b, tok):
            if ch < 5:
                dst = cq[:, ch * T:(ch + 1) * T] if ch < 3 else ckv[:, (ch - 3) * T:(ch - 2) * T]
                t = VE.do(lambda e: e.tensor_tensor(dst, b, R, ALU.mult), tok, tR)
                banks.give(b, t)
                norm2.add(dst, t, group=ch // 3)
            elif ch == 5:
                t = VE.do(lambda e: e.tensor_tensor(kpe, b, cosT, ALU.mult), tok, tk_r)
                banks.give(b, t)
            elif ch == 6:
                t2 = VE.do(lambda e: e.tensor_tensor(pet, b, sinT, ALU.mult), tok, tk_r)
                banks.give(b, t2)
                t = VE.do(lambda e: e.tensor_tensor(kpe, kpe, pet, ALU.add), t2)
                VE.do(lambda e: e.tensor_tensor(kpe, kpe, R, ALU.mult), t)
            else:
                g = gate[:, (ch - 7) * T:(ch - 6) * T]
                t = VE.do(lambda e: e.tensor_tensor(g, b, R, ALU.mult), tok)
                banks.give(b, t)
                SC.do(lambda e: e.activation(g, g, ACT.Silu), t)

        for ch in range(15):
            if ch % 2 == 0:
                it = take("l0_in")
            b, tok = projT(it, ch % 2, X)
            if ch % 2 == 1 or ch == 14:
                done(it, tok)
            waiting.append((ch, b, tok))
            if ch == 1:
                (b, tR), = norm.rows(dg)
                tR = evac(dg, b, tR)
                norm2.sq = norm.sq
            if ch > 0:
                for w in waiting:
                    leave(*w)
                waiting = []
            if ch > 1:
                ada_early(1 if ch in (8, 9) else 2)
            if ch == 8:
                (R1, tR1), (R2, tR2) = norm2.rows(dg2)
                for j in range(5):
                    c_ = cq[:, j * T:(j + 1) * T] if j < 3 else ckv[:, (j - 3) * T:(j - 2) * T]
                    gain = V("l0_q_norm", j) if j < 3 else V("l0_kv_norm", j - 3)
                    t_n = VE.do(lambda e: e.scalar_tensor_tensor(c_, c_, gain, (R1, R2)[j // 3], ALU.mult,
                                                                 ALU.mult), tR1, tR2)
                    CQ.put(j, c_, t_n)
                    if j == 2:
                        banks.give(R1, t_n)
                banks.give(R2, t_n)
        assert not ada_queue
        prefetch()
        CK = Parts(yhl, 2560, 3)
        CK.ready = CQ.ready[3:]
        Y0 = Parts(xhl, 4096)

        class Attn:

            def __init__(self, loc, causal, scale):
                self.causal, self.scale = causal, scale
                self.P = [Slots([loc((qt + 1) * P if causal else T) for _ in range(2)]) for qt in range(NT)]
                self.PT = Slots([loc(4 * T)])
                self.st = Slots([loc(4) for _ in range(8)])

            def scores(self, parts, *tokens):
                out = []
                for qt in range(NT):
                    n = (qt + 1) * P if self.causal else T
                    b, free = bank()
                    PE.wait(*free, *tokens)
                    for j, (q, k) in enumerate(parts):
                        ts = mm(b[:, 0:n], q(qt * P, (qt + 1) * P), k(n), j == 0, j == len(parts) - 1,
                                sig=j == len(parts) - 1)
                    out.append((b, n, ts))
                return out

            def biases(self, write):
                self.rows = []
                for qt in range(NT):
                    p, pf = self.P[qt].take()
                    self.rows.append((p, write(qt, p, *pf)))

            def soften(self, scored):
                exps = []
                for qt, (b, n, ts) in enumerate(scored):
                    st, sf = self.st.take()
                    if self.causal:
                        p, tb = self.rows[qt]
                        tm = VE.do(lambda e: e.scalar_tensor_tensor(p, b[:, 0:n], self.scale, p, ALU.mult, ALU.add),
                                   ts, tb)
                        banks.give(b, tm)
                        tm = VE.do(lambda e: e.tensor_reduce(st[:, 1:2], p, AXX, ALU.max, negate=True), tm, *sf)
                        te = SC.do(lambda e: e.activation(p, p, ACT.Exp, bias=st[:, 1:2], scale=1.0,
                                                          accum_out=st[:, 2:3]), tm)
                    else:
                        p, pf = self.P[qt].take()
                        tm = VE.do(lambda e: e.tensor_reduce(st[:, 0:1], b, AXX, ALU.max, negate=True), ts, *sf)
                        tm = VE.do(lambda e: e.tensor_scalar(st[:, 1:2], st[:, 0:1], self.scale, None, ALU.mult), tm)
                        te = SC.do(lambda e: e.activation(p, b, ACT.Exp, bias=st[:, 1:2], scale=self.scale,
                                                          accum_out=st[:, 2:3]), tm, *pf)
                        banks.give(b, te)
                    exps.append((p, st, te))
                rows = []
                for p, st, te in exps:
                    ti = VE.do(lambda e: e.reciprocal(st[:, 3:4], st[:, 2:3]), te)
                    tn = VE.do(lambda e: e.tensor_scalar(p, p, st[:, 3:4], None, ALU.mult), ti)
                    self.st.give(st, tn)
                    rows.append((p, tn))
                return rows

            def flip(self, rows):
                pt, ptf = self.PT.take()
                ptv = pt.rearrange("p (c q) -> p c q", c=4)
                toks = []
                for qt, (p, tn) in enumerate(rows):
                    n = qt + 1 if self.causal else NT
                    b, free = bank()
                    PE.wait(*free)
                    for c in range(n):
                        tt = PE.do(lambda e: e.transpose(b[:, c * P:(c + 1) * P], p[:, c * P:(c + 1) * P], ident),
                                   tn, tk_c, sig=c == n - 1)
                    self.P[qt].give(p, tt)
                    toks.append(evac(ptv[:, 0:n, qt * P:(qt + 1) * P],
                                     b[:, 0:n * P].rearrange("p (c q) -> p c q", c=n), tt, *ptf,
                                     eng=VE if qt % 2 else None, slot=b))
                return pt, ptv, toks

            def weigh(self, flipped, v, *tokens):
                pt, ptv, toks = flipped
                o, free = bank()
                PE.wait(*free, *toks, *tokens)
                for c in range(4):
                    a = c * P if self.causal else 0
                    to = mm(o[:, a:T], v(c), ptv[:, c, a:T], c == 0, c == 3, sig=c == 3)
                self.PT.give(pt, to)
                return o, to

        loc = phase()
        loc(2560)
        kpe_keep = loc(512)
        gate_keep = loc(4096)
        qn = [Slots([L[:, i * T:(i + 1) * T]]) for i in range(2)]
        kn = [Slots([L[:, 1024 + i * T:1024 + (i + 1) * T]]) for i in range(2)]
        qp = Slots([L[:, 2048:2560]])
        rtmp, og = loc(T), loc(T)
        vv = Slots([loc(1024), loc(1024)])
        attn = Attn(loc, False, (128 + 64) ** -0.5)

        og_free = [()]

        heads = {}
        x_read = PE.now()

        def project_pair(hd):
            pb, pf = qp.take()
            it = heads["uq"] = take("uq")
            b, tok = projT(it, 2, CQ, 3, 512)
            ta = VE.do(lambda e: e.tensor_tensor(pb, b, cosT, ALU.mult), tok, *pf)
            banks.give(b, ta)
            b, tok = projT(it, 3, CQ, 3, 512)
            tb = VE.do(lambda e: e.tensor_tensor(rtmp, b, sinT, ALU.mult), tok)
            banks.give(b, tb)
            heads["qp"] = (pb, VE.do(lambda e: e.tensor_tensor(pb, pb, rtmp, ALU.add), ta, tb))
            heads["ukv"] = take("ukv")

        def project_values():
            it = heads["ukv"]
            vb, vf = vv.take()
            for pair in range(2):
                b, free = bank()
                PE.wait(*free)
                _, hi, lo, _, _ = it
                for half in range(2):
                    qt = 2 * pair + half
                    for k in range(2):
                        PE.wait(*CK.ready[k])
                        a = CK(k, qt * P, (qt + 1) * P)
                        w = (hi[:, k * 512 + 256:k * 512 + 512], lo[:, k * 512 + 256:k * 512 + 512])
                        o = b[:, half * 256:(half + 1) * 256]
                        mm(o, a[0], w[0], half == 0 and k == 0, False)
                        mm(o, a[0], w[1], False, False)
                        tok = mm(o, a[1], w[0], False, k == 1 and half == 1, sig=k == 1 and half == 1)
                tv = evac(vb[:, pair * 512:(pair + 1) * 512], b, tok, *vf, eng=VE)
            heads["v"] = (vb, tv)

        def project_head(hd):
            j = hd % 2
            if j == 0:
                project_pair(hd)
            it = heads["uq"]
            qb, qf = qn[j].take()
            b, tok = projT(it, j, CQ, 3, 512)
            if j == 1:
                done(it, tok)
            tq = evac(qb, b, tok, *qf)
            it = heads["ukv"]
            kb, kf = kn[j].take()
            b, tok = projT(it, j, CK, 2, 512)
            tk = evac(kb, b, tok, *kf)
            if j == 1:
                project_values()
                done(it, PE.now())
            return qb, kb, *heads["qp"], tq, tk

        def score_head(hd, qb, kb, pb, tp, tq, tk):
            j, o64 = hd % 2, 64 * (hd % 2)
            out = attn.scores([(lambda a, b: qb[:, a:b], lambda n: kb[:, 0:n]),
                               (lambda a, b: pb[o64:o64 + 64, a:b], lambda n: kpe_keep[o64:o64 + 64, 0:n])],
                              tq, tp, tk)
            qn[j].give(qb, PE.now())
            kn[j].give(kb, PE.now())
            if j == 1:
                qp.give(pb, PE.now())
            return out

        def finish(hd, flipped):
            j = hd % 2
            vb, tv = heads["v"] if j == 0 else heads["v_now"]
            heads["v_now"] = (vb, tv)
            o, to = attn.weigh(flipped, lambda c: vb[:, c * 256 + j * P:c * 256 + (j + 1) * P], tv)
            if j == 1:
                vv.give(vb, to)
            t = VE.do(lambda e: e.tensor_tensor(og, o, gate_keep[:, hd * T:(hd + 1) * T], ALU.mult), to, *og_free[0])
            banks.give(o, t)
            og_free[0] = Y0.put(hd, og, t, x_read)

        ready_head = project_head(0)
        for hd in range(H + 1):
            if hd == H:
                first_out = take("l0_out")
                opened = []

                def open_chunk(c):
                    b, free = bank()
                    mm3_part(b, wchunk(first_out, 8, 256, c), Y0, range(7), 8, *first_out[3], *free)
                    opened.append(b)

                open_chunk(0)
            if hd > 0:
                flipped = attn.flip(rows)
            if hd == H:
                open_chunk(1)
            if hd < H:
                rows = attn.soften(score_head(hd, *ready_head))
            if hd + 1 < H and hd % 2 == 0:
                ready_head = project_head(hd + 1)
            if hd > 0:
                finish(hd - 1, flipped)
            if hd + 1 < H and hd % 2 == 1:
                ready_head = project_head(hd + 1)
            elif hd + 1 < H:
                prefetch()

        def AD(part, k):
            return ada[:, part * 8 + k:part * 8 + k + 1]

        loc = phase()
        dg, tmp = loc(T), loc(4 * T)
        norm = Norm([1024, 1024], halves(tmp, 4), [loc(T), loc(T)])
        for i in range(4):
            it = take("l0_out") if i else first_out
            for c in range(2):
                if i:
                    b, tok = projT(it, c, Y0)
                else:
                    b = opened[c]
                    tok = mm3_part(b, wchunk(it, 8, 256, c), Y0, range(7, 8), 8)
                m = 2 * i + c
                t_x = VE.do(lambda e: e.tensor_tensor(x_at(m), x_at(m), b, ALU.add), tok)
                banks.give(b, t_x)
                norm.add(x_at(m), t_x)
                norm.add(x_at(m), t_x, group=1, gain=V("final_norm", m))
            done(it, tok)

        load(1, cst[:, 384:NCONST], ins["consts"][:, 384:NCONST], VE.now())
        tk_c2 = (s_in[1], 32)
        def fold(scale_part, gname, extra):
            g0, _ = VEC[gname]
            t = VE.do(lambda e: e.scalar_tensor_tensor(mod[:, 0:8], ada[:, scale_part * 8:scale_part * 8 + 8], 1.0,
                                                       vec[:, g0:g0 + 8], ALU.add, ALU.mult), *t_ada, SC.now())
            if extra:
                g1, _ = VEC[extra]
                t = VE.do(lambda e: e.tensor_tensor(mod[:, 0:8], mod[:, 0:8], vec[:, g1:g1 + 8], ALU.mult), t)
            return t

        def modulated(R, tR, shift_part, t_m, tmps, waits):
            tm = Slots(tmps)
            made, half = [], []
            for k in range(10):
                if k < 8:
                    t_, fr = tm.take()
                    a = VE.do(lambda e: e.tensor_tensor(t_, x_at(k), R, ALU.mult), tR, *fr)
                    a = SC.do(lambda e: e.activation(t_, t_, ACT.Identity, bias=AD(shift_part, k),
                                                     scale=mod[:, k:k + 1]), a, t_m)
                    made.append((k, t_, a))
                if 1 <= k < 9:
                    j, t_, a = made.pop(0)
                    hi, _ = X(j)
                    half.append((j, t_, SC.do(lambda e: e.activation(hi, t_, ACT.Copy), a, *waits)))
                if k >= 2:
                    j, t_, th = half.pop(0)
                    hi, lo = X(j)
                    tl = VE.do(lambda e: e.tensor_tensor(lo, t_, F(hi), ALU.subtract), th, *waits)
                    tm.give(t_, th, tl)
                    X.ready[j] = (th, tl)

        x_read = PE.now()
        t_m = fold(1, "norm1_g_2", "final_norm")
        norm.flush()
        t = norm.means((EPS, 0.0))
        st = norm.st
        t = norm.root(0, 4, t)
        R1, tR1 = norm.spread(0, t, dg)
        t = VE.do(lambda e: e.tensor_tensor(st[:, 4:8], st[:, 4:8], st[:, 0:4], ALU.mult), t)
        t = VE.do(lambda e: e.tensor_tensor(st[:, 4:8], st[:, 4:8], st[:, 0:4], ALU.mult), t)
        t = VE.do(lambda e: e.tensor_scalar(st[:, 4:8], st[:, 4:8], EPS, None, ALU.add), t)
        t = norm.root(4, 8, t)
        t = VE.do(lambda e: e.tensor_tensor(st[:, 8:12], st[:, 4:8], st[:, 0:4], ALU.mult), t)
        R12, tR12 = norm.spread(8, t, dg, tR1)
        stats.give(norm.st, norm.last)
        modulated(R12, tR12, 0, t_m, halves(tmp, 4), [x_read])
        banks.give(R12, VE.now())
        for k in range(8):
            tk = VE.do(lambda e: e.scalar_tensor_tensor(x_at(k), x_at(k), V("final_norm", k), R1,
                                                        ALU.mult, ALU.mult), tR1)
        banks.give(R1, tk)

        loc = Local()
        YM = loc(4096)
        VE.wait(*X.ready[7])
        glow = loc(T)
        iw = loc(32)
        ik = loc(T)
        keep = loc.at
        it = take("small")
        b, tok = projT(it, 0, X)
        t_ik = evac(ik, b, tok)
        b, free = bank()
        tok = mm3(b, lambda k: (it[1][:, k * 256 + 128:k * 256 + 256], it[2][:, k * 256 + 128:k * 256 + 256]),
                  X, 8, *free)
        t_gl = evac(glow, b, tok)
        done(it, tok)
        b, free = bank()
        PE.wait(*free)
        for qt in range(NT):
            tok = PE.do(lambda e: e.transpose(b[:, 32 * qt:32 * qt + 32], glow[0:32, qt * P:(qt + 1) * P],
                                              ident[0:32, 0:32]), t_gl, sig=qt == NT - 1)
        t_iw = SC.do(lambda e: e.activation(iw.rearrange("p (t h) -> p t h", t=4),
                                            b[:, 0:P].rearrange("p (t h) -> p t h", t=4)[:, :, 16:24], ACT.Copy,
                                            scale=8.0 ** -0.5), tok)
        banks.give(b, t_iw)
        wgu = loc(T)
        load(4, wgu[0:16, :], ins["gate_up"], SC.now(), VE.now())
        tk_gu = (s_in[4], 16)

        la = loc(T)
        sets = Slots([tuple(loc(T) for _ in range(5)) + (loc(1024),) for _ in range(2)])
        ATs = Slots([loc(T), loc(T)])
        states = Slots([tuple(loc(256) for _ in range(7))])
        t_z = None
        for at, _ in ATs.free:
            t_z = GP.do(lambda e: e.memset(at, 0.0))
        la_free = ()

        def tokens_by_features(it, dst, *waits):
            toks = []
            for pair in range(2):
                b, free = bank()
                PE.wait(*free, *it[3])
                for half in range(2):
                    qt = 2 * pair + half
                    for k in range(8):
                        a = X(k, qt * P, (qt + 1) * P)
                        w = (it[1][:, k * 256:(k + 1) * 256], it[2][:, k * 256:(k + 1) * 256])
                        o = b[:, half * 256:(half + 1) * 256]
                        mm(o, a[0], w[0], half == 0 and k == 0, False)
                        mm(o, a[0], w[1], False, False)
                        tok = mm(o, a[1], w[0], False, False, sig=k == 7 and half == 1)
                toks.append(evac(dst[:, pair * 512:(pair + 1) * 512], b, tok, *waits))
            done(it, tok)
            return toks

        def project(h):
            bufs, free_set = sets.take()
            E1, E2, E3, kd, ke, vtok = bufs
            it = take("gla")
            bq, tq = projT(it, 0, X)
            bk, tk_ = projT(it, 1, X)
            done(it, tk_)
            bz, free = bank()
            tz = mm(bz, wgu[0:16, h * P:(h + 1) * P], glow[0:16, :], True, True, tk_gu, t_gl, *free, sig=True)
            bg = V("gla_b_gate_2", h)
            t2 = VE.do(lambda e: e.tensor_scalar(E2, bz, bg, None, ALU.add), tz, *free_set)
            banks.give(bz, t2)
            t1 = SC.do(lambda e: e.activation(E1, E2, ACT.Abs), t2, *free_set)
            t1 = SC.do(lambda e: e.activation(E1, E1, ACT.Exp, scale=-1.0), t1)
            t1 = SC.do(lambda e: e.activation(E1, E1, ACT.Ln, bias=1.0), t1)
            t3 = VE.do(lambda e: e.scalar_tensor_tensor(E2, E2, 0.0, E1, ALU.min, ALU.subtract), t1, t2)
            t3 = VE.do(lambda e: e.tensor_tensor_scan(la, C("reset"), E2, 0.0, ALU.mult, ALU.add), t3, tk_c2,
                       *la_free)
            la_v = la.rearrange("p (c i) -> p c i", c=8)
            E3v = E3.rearrange("p (c i) -> p c i", c=8)
            t4 = VE.do(lambda e: e.tensor_tensor(E3v, la_v[:, :, 63:64].broadcast_to([P, 8, 64]), la_v,
                                                 ALU.subtract), t3)
            t5 = SC.do(lambda e: e.activation(E1, la, ACT.Exp, scale=1.0 / 16), t3)
            t6 = SC.do(lambda e: e.activation(E2, la, ACT.Exp, scale=-1.0 / 16), t3)
            t7 = SC.do(lambda e: e.activation(E3, E3, ACT.Exp, scale=1.0 / 16), t4)
            t8 = VE.do(lambda e: e.scalar_tensor_tensor(kd, bq, 128.0 ** -0.5, E1, ALU.mult, ALU.mult), tq, t5)
            banks.give(bq, t8)
            t9 = VE.do(lambda e: e.tensor_tensor(E2, bk, E2, ALU.mult), tk_, t6)
            t10 = VE.do(lambda e: e.tensor_tensor(E3, bk, E3, ALU.mult), tk_, t7)
            banks.give(bk, t9, t10)
            tv = tokens_by_features(take("gla"), vtok, *free_set)
            return bufs, (t8, t9, t10), tv, (t4, t6)

        def mix(h, bufs, toks, tv):
            E1, E2, E3, kd, ke, vtok = bufs
            t8, t9, t10 = toks
            b, free = bank()
            PE.wait(*free)
            for c in range(4):
                tt = PE.do(lambda e: e.transpose(b[:, c * P:(c + 1) * P], E3[:, c * P:(c + 1) * P], ident),
                           t10, sig=c == 3)
            tke = evac(ke, b, tt)
            AT, at_free = ATs.take()
            ATv = AT.rearrange("p (t q) -> p t q", t=4)
            b, free = bank()
            PE.wait(*free)
            for c in range(4):
                tt = mm(b[:, c * P:(c + 1) * P], E2[:, c * P:(c + 1) * P], kd[:, c * P:(c + 1) * P], c == 0, False,
                        t8, t9, sig=c == 3)
            bv = b.rearrange("p (t q) -> p t q", t=4)
            SC.do(lambda e: e.activation(ATv[0:64, :, 0:64], bv[0:64, :, 0:64], ACT.Copy), tt, t_z, *at_free)
            ta = SC.do(lambda e: e.activation(ATv[64:128, :, 64:128], bv[64:128, :, 64:128], ACT.Copy), tt)
            banks.give(b, ta)
            tg = GP.do(lambda e: e.affine_select(out=ATv, in_=ATv, compare_op=ALU.is_ge, fill=0.0, base=0,
                                                 pattern=[[0, 4], [1, 128]], channel_multiplier=-1), ta)
            it = take("gla")
            br, tr_ = projT(it, 0, X)
            ub = [bank() for _ in range(4)]
            for c in range(7):
                i = c % 2 + 2 * (c // 4)
                o = 256 * (c // 2 % 2)
                r0 = 64 * (c % 2)
                tu = mm(ub[i][0][:, o:o + 256], ke[r0:r0 + 64, (c // 2) * P:(c // 2 + 1) * P],
                        vtok[r0:r0 + 64, (c // 2) * 256:(c // 2 + 1) * 256], o == 0, False, tke, *tv, *ub[i][1],
                        sig=True)
            S, s_free = states.take()
            tS = VE.do(lambda e: e.tensor_copy(S[0], ub[0][0][:, 0:256]), tu, *s_free)
            for c in range(1, 7):
                i = c % 2 + 2 * (c // 4)
                o = 256 * (c // 2 % 2)
                tS = VE.do(lambda e: e.scalar_tensor_tensor(
                    S[c], S[c - 1], E1[:, c * 64 + 63:c * 64 + 64], ub[i][0][:, o:o + 256], ALU.mult, ALU.add), tS)
            for ap, _ in ub:
                banks.give(ap, tS)
            br2, tr2 = projT(it, 1, X)
            done(it, tr2)
            t_s0 = SC.do(lambda e: e.activation(ke, br, ACT.Silu), tr_, tu)
            banks.give(br, t_s0)
            t_s1 = SC.do(lambda e: e.activation(E3, br2, ACT.Silu), tr2, tke)
            banks.give(br2, t_s1)
            ob = [bank(), bank()]
            for vh in range(2):
                PE.wait(*ob[vh][1], tg)
                for c in range(4):
                    mm(ob[vh][0][:, c * P:(c + 1) * P], vtok[:, c * 256 + vh * P:c * 256 + (vh + 1) * P],
                       ATv[:, c, :], c == 0, False)
                for c in range(1, 8):
                    to = mm(ob[vh][0][:, c * 64:(c + 1) * 64], S[c - 1][:, vh * P:(vh + 1) * P],
                            kd[:, c * 64:(c + 1) * 64], False, c == 7, tS, sig=c == 7)
            ATs.give(AT, to)
            states.give(S, to)
            norm = Norm([256], halves(vtok))
            for vh in range(2):
                norm.add(ob[vh][0], to)
            (R, tr), = norm.rows(E2, to)
            tr = evac(E2, R, tr)
            for vh in range(2):
                ch = 2 * h + vh
                prod = vtok[:, vh * T:(vh + 1) * T]
                t_n = VE.do(lambda e: e.scalar_tensor_tensor(prod, ob[vh][0], V("gla_norm_g_2", ch), E2,
                                                             ALU.mult, ALU.mult), tr)
                banks.give(ob[vh][0], t_n)
                t_n = VE.do(lambda e: e.tensor_tensor(prod, prod, (ke, E3)[vh], ALU.mult), t_n, (t_s0, t_s1)[vh])
                tY = Y.put(ch, prod, t_n)
            sets.give(bufs, PE.now(), *tY)

        projected = {}
        for what, h in GLA_STEPS:
            if what == "project":
                bufs, toks, tv, la_free = project(h)
                projected[h] = (bufs, toks, tv)
            else:
                mix(h, *projected.pop(h))

        loc = phase()
        loc.at = keep
        ck, dg, tmp = loc(1024), loc(T), loc(1024)
        loc.at = keep + 1024
        Mb = loc(1280)
        mo = [0, P, 3 * P, 6 * P]
        keep2 = loc.at
        loc.at = keep + 1024 + T + 1024
        iq = loc(4 * T)
        rl = Slots([loc(T) for _ in range(3)])
        sgs = Slots([loc(T) for _ in range(2)])
        m8 = loc(8)
        for i in range(2):
            it = take("iq")
            for c in range(2):
                b, tok = projT(it, c, X)
                t_iq = evac(iq[:, (2 * i + c) * T:(2 * i + c + 1) * T], b, tok)
            done(it, tok)
        it = take("dkv")
        for c in range(2):
            b, tok = projT(it, c, X)
            t = evac(ck[:, c * T:(c + 1) * T], b, tok)
        done(it, tok)
        norm = Norm([256], halves(tmp))
        for k in range(2):
            norm.add(ck[:, k * T:(k + 1) * T], t)
        (R, tr), = norm.rows(dg)
        for k in range(2):
            t_ck = VE.do(lambda e: e.scalar_tensor_tensor(ck[:, k * T:(k + 1) * T], ck[:, k * T:(k + 1) * T],
                                                          V("dsa_kv_norm_g_2", k), R, ALU.mult, ALU.mult), tr)
        banks.give(R, t_ck)
        t_mb = GP.do(lambda e: e.memset(Mb[:, 0:P], 0.0), t_ck)
        t_mb = GP.do(lambda e: e.affine_select(out=Mb[:, 0:P], in_=Mb[:, 0:P], compare_op=ALU.is_ge, fill=NEG, base=0,
                                               pattern=[[-1, P]], channel_multiplier=1), t_mb)
        tMb = [t_mb]
        scored = []
        for qt in range(NT - 1, 0, -1):
            n = (qt + 1) * P
            acc = Mb[:, mo[qt]:mo[qt] + n]
            ta = None
            for hh in range(8):
                o64 = 64 * (hh % 2)
                b, free = bank()
                ts = mm(b[:, 0:n], iq[o64:o64 + 64, (hh // 2) * T + qt * P:(hh // 2) * T + (qt + 1) * P],
                        ik[o64:o64 + 64, 0:n], True, True, t_iq, t_ik, *free, sig=True)
                r_, rf = rl.take()
                t = SC.do(lambda e: e.activation(r_[:, 0:n], b[:, 0:n], ACT.Relu, scale=64.0 ** -0.5), ts, *rf)
                banks.give(b, t)
                w = iw[:, 8 * qt + hh:8 * qt + hh + 1]
                if hh == 0:
                    ta = VE.do(lambda e: e.tensor_scalar(acc, r_[:, 0:n], w, None, ALU.mult), t, t_iw, t_ck)
                else:
                    ta = VE.do(lambda e: e.scalar_tensor_tensor(acc, r_[:, 0:n], w, acc, ALU.mult, ALU.add), t, ta)
                rl.give(r_, ta)
            ta = GP.do(lambda e: e.affine_select(
                out=acc[:, n - P:n], in_=acc[:, n - P:n], compare_op=ALU.is_ge, fill=FILL, base=0,
                pattern=[[-1, P]], channel_multiplier=1), ta)
            scored.append((qt, acc, ta))

        def select():
            for qt, acc, ta in scored:
                for r in range(16):
                    tm = VE.do(lambda e: e.max(m8, acc), ta)
                    ta = VE.do(lambda e: e.match_replace(acc, m8, acc, TAKEN), tm)
                    yield
                ta = VE.do(lambda e: e.tensor_scalar(acc, acc, TAKEN, NEG, ALU.not_equal, ALU.mult), ta)
                tMb.insert(1, ta)

        marks = select()
        for i in range(4):
            it = take("za")
            sg = []
            for c in range(2):
                b, tok = projT(it, c, X)
                d, df = sgs.take()
                t = SC.do(lambda e: e.activation(d, b, ACT.Sigmoid), tok, *df)
                banks.give(b, t)
                sg.append((d, t))
                for _ in range(3):
                    next(marks, None)
            done(it, tok)
            it = take("ba")
            for c in range(2):
                b, tok = projT(it, c, Y)
                m = 2 * i + c
                d, t = sg[c]
                t = VE.do(lambda e: e.tensor_tensor(YM[:, m * T:(m + 1) * T], b, d, ALU.mult), tok, t)
                banks.give(b, t)
                sgs.give(d, t)
                for _ in range(3):
                    next(marks, None)
            done(it, tok)
        for _ in marks:
            pass

        phase()
        loc.at = keep2
        attn = Attn(loc, True, 128.0 ** -0.5)
        qd = Slots([loc(1024)])
        kv = Slots([loc(1024), loc(1024)])
        uks = Slots([ik, C("reset")])
        spent = (VE.now(), SC.now(), PE.now())
        silc = loc(1024)
        t_c = silu_c(silc, *spent)
        SP.wait(*spent)
        rel = C("rel")

        s_uk = [sem("s_uk0"), sem("s_uk1")]
        heads = {}

        uk_next = []

        def fetch_uk(hd):
            uk, free = uks.take()
            SP.wait(*free)
            SP.dma(uk, ins["w_ukuv"][hd], s_uk[hd % 2])
            uk_next.append((uk, (s_uk[hd % 2], 16 * (hd // 2 + 1))))

        fetch_uk(0)

        def project_head(hd):
            c = hd % 2
            uk, tk_uk = uk_next.pop()
            if hd + 1 < H:
                fetch_uk(hd + 1)
            if c == 0:
                it = take("dq")
                q, qf = qd.take()
                for c_ in range(2):
                    b, tok = projT(it, c_, X)
                    tq = evac(q[:, c_ * T:(c_ + 1) * T], b, tok, *qf)
                done(it, tok)
                heads["q"] = (q, tq)
            kvb, kvf = kv.take()
            b, free = bank()
            for k in range(2):
                tok = mm(b, uk[:, k * 256:k * 256 + P], ck[:, k * T:(k + 1) * T], k == 0, k == 1, tk_uk, *free,
                         t_ck, sig=k == 1)
            tk1 = evac(kvb[:, 0:T], b, tok, *kvf)
            b, free = bank()
            PE.wait(*free)
            for s_ in range(4):
                for k in range(2):
                    tok = mm(b[:, s_ * P:(s_ + 1) * P], ck[:, k * T + s_ * P:k * T + (s_ + 1) * P],
                             uk[:, k * 256 + P:k * 256 + 2 * P], s_ == 0 and k == 0, False,
                             sig=s_ == 3 and k == 1)
            tk2 = evac(kvb[:, T:2 * T], b, tok, *kvf)
            uks.give(uk, tok)
            return *heads["q"], kvb, tk1, tk2

        def score_head(hd, q, tq, kvb, tk1, tk2):
            c = hd % 2
            slope = float(2.0 ** -(hd + 1))

            def write(qt, p, *free):
                n = (qt + 1) * P
                t = GP.do(lambda e: e.tensor_scalar(p, rel[:, 384 - P * qt:512], -slope, None, ALU.mult), tk_c2,
                          *free)
                return GP.do(lambda e: e.tensor_tensor(p, p, Mb[:, mo[qt]:mo[qt] + n], ALU.add), t, tMb[qt])

            attn.biases(write)
            out = attn.scores([(lambda a, b_: q[:, c * T + a:c * T + b_], lambda n: kvb[:, 0:n])], tq, tk1)
            if c == 1:
                qd.give(q, PE.now())
            return out

        def finish(hd, flipped, kvb, tk2):
            o, to = attn.weigh(flipped, lambda s_: kvb[:, T + s_ * P:T + (s_ + 1) * P], tk2)
            kv.give(kvb, to)
            banks.give(o, *Y.put(hd, o, to))

        ready_head = project_head(0)
        for hd in range(H + 1):
            if hd == H:
                first_zb = take("zb")
                opened = [projT(first_zb, 0, X)]
            if hd > 0:
                flipped = attn.flip(rows)
            if hd == H:
                opened.append(projT(first_zb, 1, X))
                done(first_zb, opened[1][1])
            if hd > 0:
                values = ready_head[2], ready_head[4]
                ready_head = next_head
                for _ in range((1 + hd % 2) if hd < H else 0):
                    ada_step(silc, t_c)
            if hd < H:
                rows = attn.soften(score_head(hd, *ready_head))
            if hd > 0:
                finish(hd - 1, flipped, *values)
            if hd + 1 < H:
                next_head = project_head(hd + 1)
            if hd == 0:
                ada_step(silc, t_c)
        phase()
        loc.at = keep
        G = loc(4096)
        for i in range(4):
            if i:
                it = take("zb")
            for c in range(2):
                b, tok = projT(it, c, X) if i else opened[c]
                m = 2 * i + c
                t_g = SC.do(lambda e: e.activation(G[:, m * T:(m + 1) * T], b, ACT.Sigmoid), tok)
                banks.give(b, t_g)
            if i:
                done(it, tok)
        x_read = tok
        for i in range(4):
            it = take("bb")
            for c in range(2):
                b, tok = projT(it, c, Y)
                m = 2 * i + c
                gm, ym = G[:, m * T:(m + 1) * T], YM[:, m * T:(m + 1) * T]
                t = VE.do(lambda e: e.tensor_tensor(gm, b, gm, ALU.mult), tok, t_g)
                banks.give(b, t)
                t = VE.do(lambda e: e.tensor_tensor(ym, ym, gm, ALU.add), t)
                X.put(m, ym, t, x_read)
            done(it, tok)
        dg, tmp = loc(T), loc(4 * T)
        norm = Norm([1024], halves(tmp, 3), [loc(T)])
        for i in range(4):
            it = take("w_out")
            for c in range(2):
                b, tok = projT(it, c, X)
                m = 2 * i + c
                t_x = VE.do(lambda e: e.scalar_tensor_tensor(x_at(m), b, AD(2, m), x_at(m), ALU.mult, ALU.add),
                            tok, *t_ada)
                banks.give(b, t_x)
                norm.add(x_at(m), t_x)
            done(it, tok)

        x_read = PE.now()
        t_m = fold(4, "norm2_g_2", None)
        (R, tR), = norm.rows(dg)
        modulated(R, tR, 3, t_m, halves(tmp, 4), [x_read])
        banks.give(R, VE.now())
        load(5, skT[:, :], ins["skT"])
        tk_sk = (s_in[5], 16)
        loc = Local()
        iaT, ibT, gT = loc(T), loc(T), loc(T)
        room = loc(2048)
        cand, big = room[:, 0:1024], room[:, 1024:2048]
        wk = loc(256)
        v16 = loc(2 * 4 * 128)
        i16 = loc(2 * 4 * 128)
        best, cidx, hi16, lo16, fi, fg = (loc(P) for _ in range(6))
        tot = loc(16)
        v16v = v16.rearrange("p (s t h k) -> p s t h k", s=2, t=4, h=8)
        i16v = i16.rearrange("p (s t h k) -> p s t h k", s=2, t=4, h=8)
        ohA = Slots([loc(P) for _ in range(6)])
        ohB = Slots([loc(P) for _ in range(6)])
        hstage = Slots([(loc(2048), i) for i in range(2)])
        gstage = Slots([(loc(P * CT), i) for i in range(2)])
        VE.wait(*X.ready[7])
        SC.wait(*X.ready[7])
        def pick16(rows, *tokens):
            toks = [VE.do(lambda e: e.max(best[:, 0:8], x), *tokens) for x, best, ix, w in rows]
            for (x, best, ix, w), t in zip(rows, toks):
                VE.do(lambda e: e.max_index(ix[:, 0:8], best[:, 0:8], x), t)
            toks = [VE.do(lambda e: e.match_replace(w, best[:, 0:8], x, TAKEN), t)
                    for (x, best, ix, w), t in zip(rows, toks)]
            toks = [VE.do(lambda e: e.max(best[:, 8:16], w), t) for (x, best, ix, w), t in zip(rows, toks)]
            for (x, best, ix, w), t in zip(rows, toks):
                t = VE.do(lambda e: e.max_index(ix[:, 8:16], best[:, 8:16], w), t)
            return t

        stage0 = hstage.free[0][0][0]
        qh = Slots([stage0[:, 0:1024], room[:, 0:1024]])
        sS = Slots([stage0[:, 1024:2048], room[:, 1024:2048]])

        def best_keys(h, q, tq):
            sk, sf = sS.take()
            ts = []
            for c in range(2):
                b, free = bank()
                PE.wait(*free)
                for qt in range(NT):
                    tok = mm(b[:, qt * P:(qt + 1) * P], q[:, c * T + qt * P:c * T + (qt + 1) * P],
                             skT[:, c * P:(c + 1) * P], qt == 0, False, tq, tk_sk, sig=qt == 3)
                ts.append(evac(sk[:, c * T:(c + 1) * T], b, tok, *sf))
            qh.give(q, tok)
            t_q[:] = [tok]
            for c in range(2):
                for q0 in range(0, NT, 2):
                    pick16([(sk[:, c * T + qt * P:c * T + (qt + 1) * P], v16v[:, c, qt, h, :],
                             i16v[:, c, qt, h, :].bitcast(U32), w_)
                            for qt, w_ in ((q0, wk[:, 0:P]), (q0 + 1, wk[:, P:2 * P]))], ts[c])
                    yield
            sS.give(sk, VE.now())

        t_q = []

        asked = None
        for h in range(9):
            if h < 8:
                it = take("pq")
                q, qf = qh.take()
                for c in range(2):
                    b, tok = projT(it, c, X)
                    tq = evac(q[:, c * T:(c + 1) * T], b, tok, *qf)
                done(it, tok)
            if asked:
                picking = best_keys(*asked)
                if h < 8:
                    for _ in picking:
                        pass
                else:
                    next(picking)
            asked = (h, q, tq)
        (stage, _) = hstage.take()
        hstage.free.insert(0, (stage, sS.free[0][1] + tuple(t_q)))

        gd = nc.dram_tensor("gates", (T // CT, P, P * CT), F32).ap()
        hd_ = nc.dram_tensor("hidden", (NG, P, 2048), F32).ap()
        s_gw = [sem("s_gw0"), sem("s_gw1")]
        s_hw = [sem("s_hw0"), sem("s_hw1")]
        t_gates = []

        def selection():
            for _ in picking:
                yield
            VE.do(lambda e: e.tensor_copy(i16, i16.bitcast(U32)), VE.now())
            ti = VE.now()
            t_prev = None
            n_chunk = 0
            for qt in range(NT):
                cv = cand.rearrange("p (h i j) -> p h i j", h=4, i=16)
                for h0 in range(0, 8, 2):
                    rows = []
                    for h, w_ in ((h0, wk), (h0 + 1, skT[:, :])):
                        t = VE.do(lambda e: e.tensor_tensor(
                            cv[:, h % 4], v16v[:, 0, qt, h, :].unsqueeze(2).broadcast_to([P, 16, 16]),
                            v16v[:, 1, qt, h, :].unsqueeze(1).broadcast_to([P, 16, 16]), ALU.add), ti, *t_q, t_prev)
                        rows.append((cand[:, (h % 4) * 256:(h % 4 + 1) * 256], best[:, h * 16:(h + 1) * 16],
                                     cidx[:, h * 16:(h + 1) * 16].bitcast(U32), w_))
                    yield
                    a = pick16(rows, t)
                    yield
                a1 = VE.do(lambda e: e.tensor_scalar(hi16.bitcast(U32), cidx.bitcast(U32), 4, None,
                                                     ALU.logical_shift_right), a)
                a2 = VE.do(lambda e: e.tensor_scalar(lo16.bitcast(U32), cidx.bitcast(U32), 15, None,
                                                     ALU.bitwise_and), a)
                bgv = big.rearrange("p (h k j) -> p h k j", h=4, k=16)
                bg3 = big.rearrange("p (m j) -> p m j", j=16)
                for s_, ix in ((0, hi16), (1, lo16)):
                    f = VE.do(lambda e: e.tensor_copy(fi, ix.bitcast(U32)), a1, a2)
                    for half in range(2):
                        hs = slice(64 * half, 64 * half + 64)
                        o = VE.do(lambda e: e.tensor_tensor(
                            bg3, fi[:, hs].unsqueeze(2).broadcast_to([P, 64, 16]),
                            iota[:, 0:16].unsqueeze(1).broadcast_to([P, 64, 16]), ALU.is_equal), f, VE.now())
                        o = VE.do(lambda e: e.tensor_tensor(
                            bgv, bgv, i16v[:, s_, qt, 4 * half:4 * half + 4, :].unsqueeze(2)
                            .broadcast_to([P, 4, 16, 16]), ALU.mult), o)
                        o = VE.do(lambda e: e.tensor_reduce(fg[:, hs], bg3, AXX, ALU.add), o, t_prev)
                        yield
                    yield
                    yield
                    b, free = bank()
                    tt = PE.do(lambda e: e.transpose(b[:, 0:P], fg, ident), o, *free)
                    dst = (iaT, ibT)[s_][:, qt * P:(qt + 1) * P]
                    t_prev = SC.do(lambda e: e.activation(dst, b[:, 0:P], ACT.Copy), tt)
                    banks.give(b, t_prev)
                bv = best.rearrange("p (h k) -> p h k", h=8)
                a = VE.do(lambda e: e.tensor_copy(tot[:, 0:8], bv[:, :, 0]), a)
                a = VE.do(lambda e: e.tensor_tensor(bv, bv, tot[:, 0:8].unsqueeze(2).broadcast_to([P, 8, 16]),
                                                    ALU.subtract), a)
                yield
                a = SC.do(lambda e: e.activation(fi, best, ACT.Exp), a, VE.now())
                yield
                fv = fi.rearrange("p (h k) -> p h k", h=8)
                a = VE.do(lambda e: e.tensor_reduce(tot[:, 0:8], fv, AXX, ALU.add), a)
                a = VE.do(lambda e: e.reciprocal(tot[:, 8:16], tot[:, 0:8]), a)
                a = VE.do(lambda e: e.tensor_tensor(fg.rearrange("p (h k) -> p h k", h=8), fv,
                                                    tot[:, 8:16].unsqueeze(2).broadcast_to([P, 8, 16]), ALU.mult),
                          a, t_prev)
                yield
                yield
                yield
                b, free = bank()
                tt = PE.do(lambda e: e.transpose(b[:, 0:P], fg, ident), a, *free)
                dst = gT[:, qt * P:(qt + 1) * P]
                t_prev = SC.do(lambda e: e.activation(dst, b[:, 0:P], ACT.Copy), tt)
                banks.give(b, t_prev)
                yield
                for ch in range(qt * P // CT, (qt + 1) * P // CT):
                    (st, si), sf = gstage.take()
                    stv = st.rearrange("p (b t) -> p b t", t=CT)
                    for t0 in range(0, CT, 4):
                        pairs = []
                        for j in range(4):
                            t = ch * CT + t0 + j
                            oa, fa = ohA.take()
                            ob_, fb = ohB.take()
                            VE.do(lambda e: e.tensor_scalar(oa, iota, iaT[:, t:t + 1], None, ALU.is_equal),
                                  t_prev, *fa)
                            to = VE.do(lambda e: e.tensor_scalar(ob_, iota, ibT[:, t:t + 1], gT[:, t:t + 1],
                                                                 ALU.is_equal, ALU.mult), t_prev, *fb)
                            pairs.append((oa, ob_, to))
                        yield
                        b, free = bank()
                        PE.wait(*free)
                        for j, (oa, ob_, to) in enumerate(pairs):
                            tok = mm(b[:, j * P:(j + 1) * P], oa, ob_, j == 0, False, to, sig=True)
                            ohA.give(oa, tok)
                            ohB.give(ob_, tok)
                        te = SC.do(lambda e: e.activation(
                            stv[:, :, t0:t0 + 4], b.rearrange("p (t b) -> p b t", t=4), ACT.Copy), tok, *sf)
                        banks.give(b, te)
                    SC.wait(te)
                    SC.dma(gd[ch], st, s_gw[si])
                    n_chunk += 1
                    gstage.give((st, si), (s_gw[si], 16 * ((n_chunk + 1) // 2)))
            t_gates.extend((te, PE.now(), VE.now()))

        work_ = selection()
        s_gr = [sem(f"s_gr{i}") for i in range(3)]
        s_hr = [sem(f"s_hr{i}") for i in range(3)]
        gdv = gd.rearrange("c a (g x) -> g a c x", x=4 * CT)

        def fetch(g):
            (gbuf, i), gf = gring.take()
            (hbuf, i2), hf = hring.take()
            SP.wait(*gf, *hf, (s_hw[g % 2], 16 * (g // 2 + 1)))
            SP.dma(hbuf, hd_[g], s_hr[i2])
            SP.dma(gbuf.rearrange("p (c x) -> p c x", c=T // CT), gdv[g], s_gr[i])
            n = 16 * (g // RING + 1)
            return (gbuf, i), (hbuf, i2), ((s_gr[i], n), (s_hr[i2], n))

        RING = 3
        AG = Slots([yhl[:, 0:4096], yhl[:, 4096:8192]])
        ready_ag = []
        prep = None

        def gated(fetched):
            gslot, hslot, toks = fetched
            ap = hslot[0]
            av = ap.rearrange("p (b c t) -> p b c t", b=4, t=CT)
            gv = gslot[0].rearrange("p (c b t) -> p b c t", b=4, t=CT)
            ag, af = AG.take()
            for q in range(4):
                tm = VE.do(lambda e: e.tensor_tensor(av[:, q], av[:, q], gv[:, q], ALU.mult), *toks)
                th, tl = split(ag[:, q * T:(q + 1) * T], ag[:, 2048 + q * T:2048 + (q + 1) * T],
                               ap[:, q * T:(q + 1) * T], tm, *af)
                yield
            gring.give(gslot, tm)
            hring.give(hslot, th, tl)
            ready_ag.append((ag, (th, tl)))

        for g in range(NG):
            if g == NG - 2:
                for _ in work_:
                    pass
                written = [(s_, 16 * (T // CT // 2)) for s_ in s_gw]
                loc = Local()
                gring = Slots([(loc(2048), i) for i in range(RING)])
                hring = Slots([])
                for i in range(2):
                    (ap, _), toks = gstage.free[i]
                    hring.give((ap, i), *toks)
                SP.wait(*t_gates, *written)
                fetched = [fetch(0), fetch(1)]
            if g == NG - 1:
                prep = gated(fetched.pop(0))
            (ab, si), af = hstage.take()
            for j in range(2):
                it = take("U")
                for bb in range(2):
                    b, free = bank()
                    PE.wait(*free, *it[3])
                    for k in range(8):
                        o = bb * 1024 + k * P
                        xh, xl = X(k)
                        mm(b, it[1][:, o:o + P], xh, k == 0, False)
                        mm(b, it[1][:, o:o + P], xl, False, False)
                        tok = mm(b, it[2][:, o:o + P], xh, False, k == 7, sig=k == 7)
                        if k == 3:
                            next(work_, None)
                    q = 2 * j + bb
                    t = SC.do(lambda e: e.activation(ab[:, q * T:(q + 1) * T], b, ACT.Gelu), tok, *af)
                    banks.give(b, t)
                    if bb == 1:
                        done(it, tok)
                    if bb + j != 1 or bb:
                        next(work_, None)
                    if prep:
                        next(prep, None)
            SC.wait(t)
            SC.dma(hd_[g], ab, s_hw[si])
            hstage.give((ab, si), (s_hw[si], 16 * (g // 2 + 1)))
        for _ in work_:
            pass
        written += [(s_, 16 * (NG // 2)) for s_ in s_hw]

        (ap, _), toks = hstage.free[0]
        hring.give((ap, 2), *toks)
        fetched.append(fetch(2))
        norm = Norm([1024], halves(loc(1024)), [loc(T)])
        SC.wait(*t_gates)
        t_g = []
        for _ in prep:
            pass
        for g in range(NG):
            ag = ready_ag.pop(0)
            prep = gated(fetched.pop(0)) if g + 1 < NG else iter(())
            for half in range(2):
                it = take("V")
                for m in range(4):
                    b, free = bank()
                    PE.wait(*free, *it[3], *ag[1])
                    for q in range(4):
                        o = q * 512 + m * P
                        ah, al = ag[0][:, q * T:(q + 1) * T], ag[0][:, 2048 + q * T:2048 + (q + 1) * T]
                        mm(b, it[1][:, o:o + P], ah, q == 0, False)
                        mm(b, it[1][:, o:o + P], al, False, False)
                        tok = mm(b, it[2][:, o:o + P], ah, False, q == 3, sig=q == 3)
                    dd = half * 4 + m
                    t_x = VE.do(lambda e: e.scalar_tensor_tensor(x_at(dd), b, AD(5, dd), x_at(dd),
                                                                 ALU.mult, ALU.add), tok)
                    banks.give(b, t_x)
                    if g == NG - 1:
                        ts = norm.add(x_at(dd), t_x)
                        t_g.append(VE.do(lambda e: e.tensor_scalar(x_at(dd), x_at(dd), V("final_norm_g_2", dd), None,
                                                                   ALU.mult), ts))
                    next(prep, None)
                done(it, tok)
            AG.give(ag[0], tok)
            if g + RING < NG:
                fetched.append(fetch(g + RING))

        s_out = sem("s_out")
        t = norm.root(0, 4, norm.means())
        st = norm.st
        yo = raw[:, 0:4096]
        for e in (SC, VE):
            e.wait(*raw_free[0], *raw_free[1])
        for qt in range(NT):
            for half in range(2):
                b, free = bank()
                PE.wait(*free)
                for c in range(4):
                    k = 4 * half + c
                    tt = PE.do(lambda e: e.transpose(b[:, c * P:(c + 1) * P], x_at(k)[:, qt * P:(qt + 1) * P], ident),
                               t_g[k], sig=c == 3)
                y = yo[:, qt * 1024 + half * 512:qt * 1024 + (half + 1) * 512]
                r = st[:, qt:qt + 1]
                if half:
                    ty = VE.do(lambda e: e.tensor_scalar(y, b, r, None, ALU.mult), tt, t)
                else:
                    ty = SC.do(lambda e: e.activation(y, b, ACT.Copy, scale=r), tt, t)
                banks.give(b, ty)
                SP.wait(ty)
            SP.dma(out[0, qt * P:(qt + 1) * P, :], yo[:, qt * 1024:(qt + 1) * 1024], s_out)
        SP.wait((s_out, 64), *written)
        assert state["use"] == len(items)

        block = ctx.enter_context(nc.Block())

        @block.sync
        def _(e):
            SP.run()

        @block.scalar
        def _(e):
            SC.run()

        @block.vector
        def _(e):
            VE.run()

        @block.gpsimd
        def _(e):
            GP.run()

        @block.tensor
        def _(e):
            PE.run()


_INS = ["xT", "consts", "vecs", "rope", "gate_up", "skT", "l0_in", "l0_uq", "l0_ukv", "l0_out", "w_ada", "c_rows", "w_small",
        "w_gla", "w_za", "w_ba", "w_dkv", "w_iq", "w_dq", "w_ukuv", "w_zb", "w_bb", "w_out", "w_pq", "U", "V"]


def layouts(inputs):
    a = {k: np.asarray(v) for k, v in inputs.items()}

    def cols(w, chunks):
        w = np.concatenate([w[:, c] for c in chunks], axis=1)
        n = w.shape[1] // 256
        return w.reshape(8, P, n, 256).transpose(2, 1, 0, 3).reshape(n, P, 2048)

    def sl(a0, n):
        return [slice(a0 + i * P, a0 + (i + 1) * P) for i in range(n // P)]

    r = {}
    r["xT"] = a["x"][0].T
    vecs = []
    for name in VEC:
        vecs.append(a[name].reshape(-1, P).T)
    r["vecs"] = np.concatenate(vecs, axis=1)
    f = np.float32
    i = np.arange(P)
    consts = np.zeros((P, NCONST), f)
    consts[:, 0:128] = np.eye(P)
    consts[:, 128:256] = 1.0
    consts[:, 256:384] = i[None, :]
    consts[:, 384:896] = i[:, None] + 384 - np.arange(512)[None, :]
    consts[:, 896:1408] = (np.arange(512) % 64 != 0)[None, :]
    r["consts"] = consts
    inv = (1.0 / (f(10000.0) ** (np.arange(0, 64, 2, dtype=f) / f(64)))).astype(f)
    ang = (np.arange(T, dtype=f)[:, None] * inv[None, :]).astype(f)
    cos, sin = np.cos(ang).astype(f).T, np.sin(ang).astype(f).T
    r["rope"] = np.concatenate([np.concatenate([cos] * 4), np.concatenate([-sin, sin] * 2)], axis=1)
    w = a["l0_w_in"]
    pe = list(range(640, 704))
    sw = list(range(672, 704)) + list(range(640, 672))
    chunks = sl(0, 640) + [pe + pe, sw + sw] + sl(704, 1024)
    r["l0_in"] = cols(w, chunks + chunks[-1:])
    uq = a["l0_w_uq"].reshape(3, P, 4, 2, 192)
    sw2 = np.concatenate([uq[..., 160:192], uq[..., 128:160]], axis=-1)
    uq = np.concatenate([uq[..., 0:128].reshape(3, P, 4, 256), uq[..., 128:192].reshape(3, P, 4, 128),
                         sw2.reshape(3, P, 4, 128)], axis=-1)
    r["l0_uq"] = uq.transpose(2, 1, 0, 3).reshape(4, P, 1536)
    ukv = a["l0_w_ukv"].reshape(2, P, 4, 2, 2, 128)
    r["l0_ukv"] = ukv.transpose(2, 1, 0, 4, 3, 5).reshape(4, P, 1024)
    r["l0_out"] = cols(a["l0_w_out"], sl(0, 1024))
    r["w_ada"] = a["w_ada_2"][0].T.reshape(24, 2, P, 1024).transpose(0, 2, 1, 3).reshape(24, P, 2048)
    r["c_rows"] = np.broadcast_to(a["c_2"], (P, 1024))
    w = a["w_in_2"][0]
    gq, gk, gv, gr, glow, dq, dkv, iq, ik, iw, za, zb = (
        int(x) for x in np.cumsum([0, 512, 512, 1024, 1024, 16, 1024, 256, 512, 64, 8, 1024]))
    iks = list(range(ik, ik + 64))
    r["w_small"] = cols(w, [iks + iks, list(range(glow, glow + 16)) + list(range(iw, iw + 8)) + [0] * 104])[0]
    ch = []
    for h in range(4):
        ch += [slice(gq + h * P, gq + (h + 1) * P), slice(gk + h * P, gk + (h + 1) * P)]
        ch += sl(gv + h * 256, 256) + sl(gr + h * 256, 256)
    r["w_gla"] = cols(w, ch)
    for name, at, n in (("w_za", za, 1024), ("w_zb", zb, 1024), ("w_dkv", dkv, 256), ("w_iq", iq, 512),
                        ("w_dq", dq, 1024)):
        r[name] = cols(w, sl(at, n))
    r["w_ba"], r["w_bb"], r["w_out"] = (cols(a[n][0], sl(0, 1024)) for n in ("w_branch_a_2", "w_branch_b_2", "w_out_2"))
    r["w_pq"] = cols(a["peer_w_q_2"][0], sl(0, 2048))
    uk = a["dsa_w_uk_2"][0].transpose(0, 2, 1).reshape(8, 2, P, 128)
    uv = a["dsa_w_uv_2"][0].reshape(8, 2, P, 128)
    r["w_ukuv"] = np.concatenate([uk, uv], axis=-1).transpose(0, 2, 1, 3).reshape(8, P, 512)
    r["gate_up"] = a["gla_w_gate_up_2"][0]
    r["skT"] = np.concatenate([a["peer_sub_keys_1_2"][0].T, a["peer_sub_keys_2_2"][0].T], axis=1)
    r["U"] = a["peer_u_2"][0].reshape(P, 64, 2, 8, P).transpose(1, 4, 2, 3, 0).reshape(64, P, 2048)
    r["V"] = a["peer_v_2"][0].reshape(P, 32, 4, 2, 512).transpose(1, 3, 0, 2, 4).reshape(64, P, 2048)
    return {k: np.ascontiguousarray(v) for k, v in r.items()}


def kernel(**inputs):
    import concourse.bacc as bacc
    from concourse.bass_utils import run_bass_kernel_spmd as run

    nc = bacc.Bacc("TRN2", target_bir_lowering=False, num_devices=1)
    arrays = layouts(inputs)
    args = {k: nc.dram_tensor("in_" + k, v.shape, F32, kind="ExternalInput").ap() for k, v in arrays.items()}
    out = nc.dram_tensor("out_0", (1, T, 1024), F32, kind="ExternalOutput").ap()
    build(nc, args, out)
    r = run(nc, [{"in_" + k: v for k, v in arrays.items()}], core_ids=[0])
    return r.results[0]["out_0"]
```
